# Optimizing a Trainium2 kernel written in Bass

```python
import jax, jax.numpy as jnp
from jax import lax
import numpy as np

D_MODEL = 1024
BATCH = 1
SEQ = 1024
DEPTH = 2
DEC_BATCH = 8
DEC_SEQ = 8
PAST_LEN = 8192
PAGE_SIZE = 128

N_EVEN = (DEPTH + 1) // 2
N_ODD = DEPTH // 2
HG_HEADS = 4
HG_KDIM = 128
HG_VDIM = D_MODEL // 2 // HG_HEADS
HG_QDIM = HG_HEADS * HG_KDIM
HG_WIDTH = HG_HEADS * HG_VDIM
MLA_HEADS = 4
QK_NOPE = 128
QK_ROPE = 64
V_HEAD = 128
Q_LORA = 384
KV_LORA = 256
LAT_DIM = KV_LORA + QK_ROPE
MLA_WIDTH = MLA_HEADS * V_HEAD
MLA_SCALE = (QK_NOPE + QK_ROPE) ** -0.5
ROPE_THETA = 10000.0
Q_BLOCK = 128
NEG_BIG = -1e30
TINY = 1e-30
GLA_HEADS = 4
GLA_KEY = D_MODEL // 2
GLA_VAL = D_MODEL
GLA_HK = GLA_KEY // GLA_HEADS
GLA_HV = GLA_VAL // GLA_HEADS
GATE_RANK = 16
GATE_TAU = 16.0
D_FF = 4 * D_MODEL
CHUNK = 64
EPS = 1e-6

EVEN_SPLIT = [HG_QDIM, HG_QDIM, HG_WIDTH, HG_WIDTH, Q_LORA, KV_LORA, QK_ROPE]
EVEN_COLS = sum(EVEN_SPLIT)
ODD_SPLIT = [GLA_KEY, GLA_KEY, GLA_VAL, GLA_VAL, GATE_RANK]
ODD_COLS = sum(ODD_SPLIT)

kernel_name = 'hybrid_hgrn2_mla_gla_decode_step'

def _split(x, sizes):
    idx = np.cumsum(sizes)[:-1].tolist()
    return jnp.split(x, idx, axis=-1)

def rmsnorm(x, w):
    xf = x.astype(jnp.float32)
    y = xf * lax.rsqrt(jnp.mean(xf * xf, axis=-1, keepdims=True) + EPS)
    return (y * w.astype(jnp.float32)).astype(x.dtype)

def rope(x, pos):
    half = x.shape[-1] // 2
    inv = ROPE_THETA ** (-jnp.arange(half, dtype=jnp.float32) / half)
    ang = pos.astype(jnp.float32)[:, None] * inv[None, :]
    cos = jnp.cos(ang)[:, None, :]
    sin = jnp.sin(ang)[:, None, :]
    x1 = x[..., :half].astype(jnp.float32)
    x2 = x[..., half:].astype(jnp.float32)
    return jnp.concatenate([x1 * cos - x2 * sin, x1 * sin + x2 * cos], axis=-1).astype(x.dtype)

def gated_linear_scan(q, k, v, log_f, s0):
    B, T, H, K = q.shape
    V = v.shape[-1]
    L = min(CHUNK, T)
    n = -(-T // L)
    pad = n * L - T

    def blocks(a):
        a = jnp.pad(a.astype(jnp.float32), ((0, 0), (0, pad), (0, 0), (0, 0)))
        return a.reshape(B, n, L, H, a.shape[-1]).transpose(1, 0, 3, 2, 4)

    qc, kc, vc, gc = blocks(q), blocks(k), blocks(v), blocks(log_f)
    causal = jnp.tril(jnp.ones((L, L), dtype=bool))[:, :, None]

    def step(S, inp):
        qb, kb, vb, gb = inp
        b = jnp.cumsum(gb, axis=2)
        o_inter = jnp.einsum('bhtk,bhkv->bhtv', qb * jnp.exp(b), S)
        diff = b[:, :, :, None, :] - b[:, :, None, :, :]
        decay = jnp.where(causal, jnp.exp(jnp.minimum(diff, 0.0)), 0.0)
        scores = jnp.sum(qb[:, :, :, None, :] * decay * kb[:, :, None, :, :], axis=-1)
        o = o_inter + jnp.einsum('bhts,bhsv->bhtv', scores, vb)
        b_last = b[:, :, -1, :]
        k_dec = kb * jnp.exp(b_last[:, :, None, :] - b)
        S_new = jnp.exp(b_last)[..., None] * S + jnp.einsum('bhsk,bhsv->bhkv', k_dec, vb)
        return S_new, o

    S, o = lax.scan(step, s0.astype(jnp.float32), (qc, kc, vc, gc))
    o = o.transpose(1, 0, 3, 2, 4).reshape(B, n * L, H, V)[:, :T]
    return o.astype(v.dtype), S.astype(s0.dtype)

def hgrn2_mixer(q_raw, f_raw, i_raw, g_raw, lb, norm_w, s0):
    B, T, _ = q_raw.shape
    shp_k = (B, T, HG_HEADS, HG_KDIM)
    z = f_raw.reshape(shp_k).astype(jnp.float32)
    lbh = lb.reshape(HG_HEADS, HG_KDIM).astype(jnp.float32)
    f = lbh + (1.0 - lbh) * jax.nn.sigmoid(z)
    log_f = jnp.log(jnp.maximum(f, TINY))
    k = (1.0 - lbh) * jax.nn.sigmoid(-z)
    q = jax.nn.silu(q_raw.reshape(shp_k)) * (HG_KDIM ** -0.5)
    v = i_raw.reshape(B, T, HG_HEADS, HG_VDIM)
    o, s_new = gated_linear_scan(q, k, v, log_f, s0)
    o = rmsnorm(o, norm_w) * jax.nn.silu(g_raw.reshape(B, T, HG_HEADS, HG_VDIM))
    return o.reshape(B, T, HG_WIDTH), s_new

def mla_attend(q_lat, q_pe, lat, q_pos, k_pos):
    c_kv = lat[..., :KV_LORA]
    k_pe = lat[..., KV_LORA:]
    s = (jnp.einsum('bqhc,bkc->bhqk', q_lat, c_kv, preferred_element_type=jnp.float32)
         + jnp.einsum('bqhr,bkr->bhqk', q_pe, k_pe, preferred_element_type=jnp.float32)) * MLA_SCALE
    s = jnp.where(k_pos[None, :] <= q_pos[:, None], s, NEG_BIG)
    p = jax.nn.softmax(s, axis=-1)
    return jnp.einsum('bhqk,bkc->bqhc', p.astype(lat.dtype), c_kv)

def mla_mixer(c_q, c_kv_raw, k_r, pos, past_lat, q_norm_w, w_uq, kv_norm_w, w_uk, w_uv):
    B, T, _ = c_q.shape
    q = (rmsnorm(c_q, q_norm_w) @ w_uq).reshape(B, T, MLA_HEADS, QK_NOPE + QK_ROPE)
    q_nope = q[..., :QK_NOPE]
    q_pe = rope(q[..., QK_NOPE:], pos)
    c_kv = rmsnorm(c_kv_raw, kv_norm_w)
    k_pe = rope(k_r[:, :, None, :], pos)[:, :, 0, :]
    rows = jnp.concatenate([c_kv, k_pe], axis=-1)
    q_lat = jnp.einsum('bthn,hcn->bthc', q_nope, w_uk)
    if past_lat is None:
        blk = min(Q_BLOCK, T)
        nb = T // blk

        def blockwise(a):
            return a.reshape(B, nb, blk, *a.shape[2:]).swapaxes(0, 1)

        out = lax.map(lambda qs: mla_attend(qs[0], qs[1], rows, qs[2], pos),
                      (blockwise(q_lat), blockwise(q_pe), pos.reshape(nb, blk)))
        out = out.swapaxes(0, 1).reshape(B, T, MLA_HEADS, KV_LORA)
    else:
        lat = jnp.concatenate([past_lat, rows], axis=1)
        k_pos = jnp.arange(lat.shape[1])
        out = mla_attend(q_lat, q_pe, lat, pos, k_pos)
    o = jnp.einsum('bthc,hcv->bthv', out, w_uv)
    return o.reshape(B, T, MLA_WIDTH), rows

def even_mixer(h, pos, past_lat, s0, lb, w_in, hg_norm_w, q_norm_w, w_uq, kv_norm_w, w_uk, w_uv, w_out):
    hq, hf, hi, hg, cq, ckv, kr = _split(h @ w_in, EVEN_SPLIT)
    o_a, s_new = hgrn2_mixer(hq, hf, hi, hg, lb, hg_norm_w, s0)
    o_b, rows = mla_mixer(cq, ckv, kr, pos, past_lat, q_norm_w, w_uq, kv_norm_w, w_uk, w_uv)
    return jnp.concatenate([o_a, o_b], axis=-1) @ w_out, rows, s_new

def gla_mixer(h, s0, w_in, w_a2, b_a, norm_w, w_out):
    B, T, _ = h.shape
    q, k, v, r, a1 = _split(h @ w_in, ODD_SPLIT)
    log_a = jax.nn.log_sigmoid((a1 @ w_a2 + b_a).astype(jnp.float32)) / GATE_TAU
    shp_k = (B, T, GLA_HEADS, GLA_HK)
    o, s_new = gated_linear_scan(q.reshape(shp_k) * (GLA_HK ** -0.5), k.reshape(shp_k),
                                 v.reshape(B, T, GLA_HEADS, GLA_HV), log_a.reshape(shp_k), s0)
    o = rmsnorm(o, norm_w) * jax.nn.silu(r.reshape(B, T, GLA_HEADS, GLA_HV))
    return o.reshape(B, T, GLA_VAL) @ w_out, s_new

def sq_relu_mlp(h, w_up, w_down):
    a = jax.nn.relu(h @ w_up)
    return (a * a) @ w_down

def setup_inputs(seed: int = 0) -> dict:
    key = jax.random.key(seed)
    ks = jax.random.split(key, 25)
    f32 = jnp.float32

    def nrm(k, shape, scale):
        return jax.random.normal(k, shape, f32) * scale

    def gain(k, shape):
        return 1.0 + 0.02 * jax.random.normal(k, shape, f32)

    n_pages = PAST_LEN // PAGE_SIZE
    n_used = DEC_BATCH * n_pages
    n_phys = -(-n_used * 5 // 4)
    page_table = jax.random.permutation(ks[5], n_phys)[:n_used].reshape(DEC_BATCH, n_pages).astype(jnp.int32)
    return {
        'x_prompt': nrm(ks[0], (BATCH, SEQ, D_MODEL), 1.0),
        'x_sample': nrm(ks[1], (DEC_BATCH, DEC_SEQ, D_MODEL), 1.0),
        'cache_mla': nrm(ks[2], (N_EVEN, n_phys, PAGE_SIZE, LAT_DIM), 1.0),
        'state_hgrn': nrm(ks[3], (N_EVEN, DEC_BATCH, HG_HEADS, HG_KDIM, HG_VDIM), 0.5),
        'state_gla': nrm(ks[4], (N_ODD, DEC_BATCH, GLA_HEADS, GLA_HK, GLA_HV), 0.5),
        'page_table': page_table,
        'norm_mix': gain(ks[6], (DEPTH, D_MODEL)),
        'norm_mlp': gain(ks[7], (DEPTH, D_MODEL)),
        'norm_final': gain(ks[8], (D_MODEL,)),
        'w_in_even': nrm(ks[9], (N_EVEN, D_MODEL, EVEN_COLS), D_MODEL ** -0.5),
        'lower_bounds': nrm(ks[10], (N_EVEN, HG_QDIM), 0.5),
        'hgrn_norm': gain(ks[11], (N_EVEN, HG_VDIM)),
        'q_norm': gain(ks[12], (N_EVEN, Q_LORA)),
        'w_uq': nrm(ks[13], (N_EVEN, Q_LORA, MLA_HEADS * (QK_NOPE + QK_ROPE)), Q_LORA ** -0.5),
        'kv_norm': gain(ks[14], (N_EVEN, KV_LORA)),
        'w_uk': nrm(ks[15], (N_EVEN, MLA_HEADS, KV_LORA, QK_NOPE), QK_NOPE ** -0.5),
        'w_uv': nrm(ks[16], (N_EVEN, MLA_HEADS, KV_LORA, V_HEAD), KV_LORA ** -0.5),
        'w_out_even': nrm(ks[17], (N_EVEN, HG_WIDTH + MLA_WIDTH, D_MODEL), (HG_WIDTH + MLA_WIDTH) ** -0.5),
        'w_in_odd': nrm(ks[18], (N_ODD, D_MODEL, ODD_COLS), D_MODEL ** -0.5),
        'w_alpha2': nrm(ks[19], (N_ODD, GATE_RANK, GLA_KEY), GATE_RANK ** -0.5),
        'b_alpha': nrm(ks[20], (N_ODD, GLA_KEY), 0.01),
        'gla_norm': gain(ks[21], (N_ODD, GLA_HV)),
        'w_out_odd': nrm(ks[22], (N_ODD, GLA_VAL, D_MODEL), GLA_VAL ** -0.5),
        'w_up': nrm(ks[23], (DEPTH, D_MODEL, D_FF), D_MODEL ** -0.5),
        'w_down': nrm(ks[24], (DEPTH, D_FF, D_MODEL), D_FF ** -0.5),
    }

def reference(x_prompt, x_sample, cache_mla, state_hgrn, state_gla, page_table, norm_mix, norm_mlp,
              norm_final, w_in_even, lower_bounds, hgrn_norm, q_norm, w_uq, kv_norm, w_uk, w_uv,
              w_out_even, w_in_odd, w_alpha2, b_alpha, gla_norm, w_out_odd, w_up, w_down):
    B, T, _ = x_prompt.shape
    Bd, Td, _ = x_sample.shape
    n_pages = page_table.shape[1]
    past_len = n_pages * PAGE_SIZE
    pos_p = jnp.arange(T)
    pos_s = past_len + jnp.arange(Td)
    p_lb = jax.nn.softmax(lower_bounds.astype(jnp.float32), axis=0)
    lbs = jnp.cumsum(p_lb, axis=0) - p_lb[0]
    zero_hg = jnp.zeros((B, HG_HEADS, HG_KDIM, HG_VDIM), x_prompt.dtype)
    zero_gla = jnp.zeros((B, GLA_HEADS, GLA_HK, GLA_HV), x_prompt.dtype)

    xp, xs = x_prompt, x_sample
    mla_p, mla_s, hg_p, hg_s, gla_p, gla_s = [], [], [], [], [], []
    for layer in range(DEPTH):
        hp = rmsnorm(xp, norm_mix[layer])
        hs = rmsnorm(xs, norm_mix[layer])
        if layer % 2 == 0:
            e = layer // 2
            past = cache_mla[e][page_table].reshape(Bd, past_len, LAT_DIM)
            wts = (lbs[e], w_in_even[e], hgrn_norm[e], q_norm[e], w_uq[e], kv_norm[e],
                   w_uk[e], w_uv[e], w_out_even[e])
            dp, rows_p, sp = even_mixer(hp, pos_p, None, zero_hg, *wts)
            ds, rows_s, ss = even_mixer(hs, pos_s, past, state_hgrn[e], *wts)
            mla_p.append(rows_p)
            mla_s.append(rows_s)
            hg_p.append(sp)
            hg_s.append(ss)
        else:
            o = layer // 2
            wts = (w_in_odd[o], w_alpha2[o], b_alpha[o], gla_norm[o], w_out_odd[o])
            dp, sp = gla_mixer(hp, zero_gla, *wts)
            ds, ss = gla_mixer(hs, state_gla[o], *wts)
            gla_p.append(sp)
            gla_s.append(ss)
        xp = xp + dp
        xs = xs + ds
        xp = xp + sq_relu_mlp(rmsnorm(xp, norm_mlp[layer]), w_up[layer], w_down[layer])
        xs = xs + sq_relu_mlp(rmsnorm(xs, norm_mlp[layer]), w_up[layer], w_down[layer])

    y_prompt = rmsnorm(xp, norm_final)
    y_sample = rmsnorm(xs, norm_final)
    return (y_prompt, y_sample, jnp.stack(mla_p), jnp.stack(mla_s), jnp.stack(hg_p),
            jnp.stack(hg_s), jnp.stack(gla_p), jnp.stack(gla_s))


_drawn_inputs = setup_inputs


def setup_inputs(seed=0):
    import zlib

    import numpy as np

    out = dict(_drawn_inputs(seed))
    spreads = {}
    factors = {'norm_final': 8.93,
     'hgrn_norm': 4.408,
     'q_norm': 8.0,
     'kv_norm': 3.267,
     'b_alpha': 8.0,
     'gla_norm': 27.215,
     'norm_mlp': 2.668}
    for name, (base, spread) in spreads.items():
        noise = np.random.default_rng([zlib.crc32(name.encode()), seed]).standard_normal(out[name].shape)
        drawn = base * np.exp(spread * noise) if base else spread * noise
        out[name] = __import__('jax').numpy.asarray(drawn.astype(out[name].dtype))
    for name, factor in factors.items():
        out[name] = (out[name] * factor).astype(out[name].dtype)
    return out
```

```python
from contextlib import ExitStack

import numpy as np

import concourse.bass as bass
from concourse import mybir

F32 = mybir.dt.float32
F32R = mybir.dt.float32r
I32 = mybir.dt.int32
ACT = mybir.ActivationFunctionType
ALU = mybir.AluOpType
AX = mybir.AxisListType

P = 128
D = 1024
KD = D // P
SEQ = 1024
NB, TS = 8, 8
NS = NB * TS
T = SEQ + NS
HEADS = 4
CHUNKS = [(0, 384), (384, 352), (736, 352)]
NC = len(CHUNKS)
FF = 4096
EVEN_COLS = 2752
ODD_COLS = 3088
Q_LORA, KV_LORA, ROPE = 384, 256, 64
LAT = KV_LORA + ROPE
PAGES = 64
PG = 4
SCALE = (128 + ROPE) ** -0.5
ROPE_THETA = 10000.0
NEG = -1e30
EPS = 1e-6
TINY = 1e-30
GATE_RANK, GATE_TAU = 16, 16.0
LEVELS = [1, 2, 4, 8, 16, 32, 64]

Z_Q, Z_F, Z_I, Z_G, Z_CQ, Z_CKV, Z_KR = 0, 512, 1024, 1536, 2048, 2432, 2688
G_Q, G_K, G_V, G_R, G_A, G_GATE = 0, 512, 1024, 2048, 3072, 3088
Z_ROWS = 3600


class Kit:
    pass


class Stage:

    def __init__(self, nc, name):
        self.nc, self.name, self.stack, self.sems = nc, name, ExitStack(), []

    def __enter__(self):
        return self

    def __exit__(self, *a):
        self.stack.__exit__(*a)
        self.nc.clear_and_free_semaphores(self.sems)
        self.nc.all_engine_barrier()

    def sb(self, name, shape, dt=F32):
        return self.stack.enter_context(self.nc.sbuf_tensor(f"{self.name}_{name}", shape, dt))

    def ps(self, name, shape, dt=F32):
        return self.stack.enter_context(self.nc.psum_tensor(f"{self.name}_{name}", shape, dt))

    def sem(self, name):
        self.sems.append(self.nc.alloc_semaphore(f"{self.name}_{name}"))
        return self.sems[-1]

    def block(self):
        return self.stack.enter_context(self.nc.Block())


def r32(ap):
    return ap.bitcast(F32)


def mm3(pe, out, w_hi, w_lo, x_hi, x_lo, first, last):
    pe.matmul(out, w_hi, x_hi, start=first, stop=False)
    pe.matmul(out, w_hi, x_lo, start=False, stop=False)
    return pe.matmul(out, w_lo, x_hi, start=False, stop=last)


def wait_apart(eng, sem, value, spare):
    eng.wait_ge(sem, value)
    eng.sem_inc(spare, 1)



def load_stage(nc, K):
    with Stage(nc, "load") as s:
        xin = s.sb("xin", [P, 2, D])
        tp = [s.ps(f"tp{i}", [P, 4, P]) for i in range(4)]
        const_in, ident_in, xin_in = s.sem("const_in"), s.sem("ident_in"), [s.sem("xin_in0"), s.sem("xin_in1")]
        xin_used, turned = s.sem("xin_used"), s.sem("turned")
        copied_lo, copied_hi = s.sem("copied_lo"), s.sem("copied_hi")
        block = s.block()
        xp, xs = K.x_prompt, K.x_sample

        @block.sync
        def _(sp):
            sp.dma_start(K.ident[:], K.c_ident).then_inc(ident_in, 16)
            for i in range(2):
                sp.dma_start(xin[:, i, :], xp[i * P:(i + 1) * P, :]).then_inc(xin_in[i], 16)
            with sp.Fori(1, 4) as j:
                for i in range(2):
                    sp.wait_ge(xin_used, 2 * j + (i - 1))
                    sp.dma_start(xin[:, i, :], xp[bass.ds(j * 2 * P + i * P, P), :]).then_inc(xin_in[i], 16)
            sp.wait_ge(xin_used, 7)
            sp.dma_start(xin[0:NS, 0, :], xs).then_inc(xin_in[0], 16)

        @block.gpsimd
        def _(pool):
            pool.memset(K.ones[:], 1.0)
            pool.memset(K.eps[:], EPS)
            with nc.allow_non_contiguous_dma(reason="a column of each norm weight, once"):
                for n, w in enumerate([K.norm_mix[0], K.norm_mlp[0], K.norm_mix[1], K.norm_mlp[1], K.norm_final]):
                    pool.dma_start(K.norms[:, n, :], w.rearrange("(k p) -> p k", p=P)).then_inc(const_in, 16)
            pool.wait_ge(const_in, 5 * 16)

        @block.tensor
        def _(pe):
            def turn(tile, i, rows):
                for half in range(2):
                    pe.wait_ge(copied_lo if half == 0 else copied_hi, tile + 1)
                    for k in range(4):
                        c = (4 * half + k) * P
                        last = pe.transpose(tp[2 * i + half][:, k, 0:rows], xin[0:rows, i, c:c + P],
                                            K.ident[0:rows, 0:rows])
                    last.then_inc(turned, 1)
            pe.wait_ge(ident_in, 16)
            with pe.Fori(0, 4) as j:
                for i in range(2):
                    pe.wait_ge(xin_in[i], j * 16 + 16)
                    turn(j * 2 + i, i, P)
            pe.wait_ge(xin_in[0], 5 * 16)
            turn(8, 0, NS)

        def copy_out(eng, copy, half, copied):
            eng.sem_inc(copied, 2)
            dst = K.xT[:, 4 * half:4 * half + 4, :]
            with eng.Fori(0, 4) as j:
                for i in range(2):
                    eng.wait_ge(turned, j * 4 + (2 * i + half + 1))
                    copy(dst[:, :, bass.ds(j * 2 * P + i * P, P)], tp[2 * i + half][:]).then_inc(copied, 1)
                    if half:
                        eng.sem_inc(xin_used, 1)
            eng.wait_ge(turned, 17 + half)
            copy(dst[:, :, SEQ:T], tp[half][:, :, 0:NS]).then_inc(copied, 1)

        @block.scalar
        def _(act):
            copy_out(act, lambda o, x: act.activation(o, x, ACT.Copy), 0, copied_lo)

        @block.vector
        def _(dve):
            copy_out(dve, lambda o, x: dve.tensor_copy(o, x), 1, copied_hi)


def store_stage(nc, K):
    with Stage(nc, "store") as s:
        sq = s.sb("sq", [P, 2, T])
        acc = s.sb("acc", [P, T])
        rstd = s.sb("rstd", [P, T])
        y = s.sb("y", [P, 2, D])
        psum = [s.ps(f"sum{i}", [P, 512]) for i in range(NC)]
        tp = [s.ps(f"tp{i}", [P, 4, P]) for i in range(4)]
        n = Norm(s, K, 4, sq, acc, rstd, psum)
        normed = s.sem("normed")
        turned, copied_lo, copied_hi = s.sem("turned"), s.sem("copied_lo"), s.sem("copied_hi")
        y_out = [s.sem("y_out0"), s.sem("y_out1")]
        y_free = s.sem("y_free")
        block = s.block()
        yp, ys = K.y_prompt, K.y_sample

        @block.tensor
        def _(pe):
            n.pe(pe)
            pe.wait_ge(normed, KD)

            for tile in range(9):
                rows, i = (P if tile < 8 else NS), tile % 2
                for half in range(2):
                    pe.wait_ge(copied_lo if half == 0 else copied_hi, tile + 1)
                    for k in range(4):
                        last = pe.transpose(tp[2 * i + half][0:rows, k, :],
                                            K.xT[:, 4 * half + k, tile * P:tile * P + rows], K.ident[:])
                    last.then_inc(turned, 1)

        @block.scalar
        def _(act):
            act.sem_inc(copied_lo, 2)
            n.act_squares(act)
            n.act_rstd(act)
            for tile in range(9):
                rows, i = (P if tile < 8 else NS), tile % 2
                act.wait_ge(turned, 2 * tile + 1)
                act.wait_ge(y_free, tile + 1)
                act.activation(y[0:rows, i, 0:512], tp[2 * i][0:rows], ACT.Copy).then_inc(copied_lo, 1)

        @block.vector
        def _(dve):
            dve.sem_inc(copied_hi, 2)
            n.dve_sum(dve)
            dve.wait_ge(n.rstd_ready, NC)
            for k in range(KD):
                dve.scalar_tensor_tensor(out=K.xT[:, k, :], in0=K.xT[:, k, :], scalar=K.norms[:, 4, k:k + 1],
                                         in1=rstd[:], op0=ALU.mult, op1=ALU.mult).then_inc(normed, 1)
            for tile in range(9):
                rows, i = (P if tile < 8 else NS), tile % 2
                dve.wait_ge(turned, 2 * tile + 2)
                dve.wait_ge(y_free, tile + 1)
                dve.tensor_copy(y[0:rows, i, 512:1024], tp[2 * i + 1][0:rows]).then_inc(copied_hi, 1)

        @block.sync
        def _(sp):
            sp.sem_inc(y_free, 2)
            for tile in range(9):
                rows, i = (P if tile < 8 else NS), tile % 2
                sp.wait_ge(copied_lo, tile + 3)
                sp.wait_ge(copied_hi, tile + 3)
                dst = yp[tile * P:(tile + 1) * P, :] if tile < 8 else ys
                sp.dma_start(dst, y[0:rows, i, :]).then_inc(y_out[i], 16)
                if tile:
                    sp.wait_ge(y_out[1 - i], 16 * ((tile + 1) // 2))
                    sp.sem_inc(y_free, 1)
            sp.wait_ge(y_out[0], 5 * 16)


class Norm:

    def __init__(self, s, K, which, sq, acc, rstd, psum):
        self.K, self.which, self.sq, self.acc, self.rstd, self.psum = K, which, sq, acc, rstd, psum
        self.squared, self.sq_used = s.sem("squared"), s.sem("sq_used")
        self.mean_in, self.logged, self.rstd_ready = s.sem("mean_in"), s.sem("logged"), s.sem("rstd_ready")

    def act_squares(self, act):
        act.sem_inc(self.sq_used, 2)
        for k in range(KD):
            act.wait_ge(self.sq_used, k + 1)
            act.activation(self.sq[:, k % 2, :], self.K.xT[:, k, :], ACT.Square).then_inc(self.squared, 1)

    def dve_sum(self, dve):
        for k in range(KD):
            dve.wait_ge(self.squared, k + 1)
            if k == 0:
                dve.tensor_copy(self.acc[:], self.sq[:, 0, :]).then_inc(self.sq_used, 1)
            else:
                dve.wait_ge(self.sq_used, 2 + k)
                dve.tensor_tensor(self.acc[:], self.acc[:], self.sq[:, k % 2, :], ALU.add).then_inc(self.sq_used, 1)

    def pe(self, pe):
        pe.wait_ge(self.sq_used, 2 + KD)
        for c, (t0, tn) in enumerate(CHUNKS):
            pe.matmul(self.psum[c][:, 0:tn], self.K.ones[:], self.acc[:, t0:t0 + tn],
                      start=True, stop=True).then_inc(self.mean_in, 1)

    def act_rstd(self, act):
        for c, (t0, tn) in enumerate(CHUNKS):
            act.wait_ge(self.mean_in, c + 1)
            act.activation(self.rstd[:, t0:t0 + tn], self.psum[c][:, 0:tn], ACT.Ln,
                           scale=1.0 / D, bias=self.K.eps[:, 0:1]).then_inc(self.logged, 1)
        act.wait_ge(self.logged, NC)
        for c, (t0, tn) in enumerate(CHUNKS):
            act.activation(self.rstd[:, t0:t0 + tn], self.rstd[:, t0:t0 + tn], ACT.Exp,
                           scale=-0.5).then_inc(self.rstd_ready, 1)



def project_stage(nc, K, name, w, cols, norm=None, z=None, mix=None):
    pairs = cols // P // 2
    tail = [(col, min(P, cols - col)) for col in range(2 * pairs * P, cols, P)]
    with Stage(nc, name) as s:
        x_hi, x_lo = s.sb("x_hi", [P, KD, T], F32R), s.sb("x_lo", [P, KD, T], F32R)
        raw = s.sb("raw", [P, 2, KD, P])
        w_hi, w_lo = s.sb("w_hi", [P, 2, KD, P], F32R), s.sb("w_lo", [P, 2, KD, P], F32R)
        sq = s.sb("sq", [P, 2, T])
        bank = [[s.ps(f"bank{i}{c}", [P, 512]) for c in range(NC)] for i in range(2)]
        raw_in = [s.sem("raw_in0"), s.sem("raw_in1")]
        hi_done, lo_done = s.sem("hi_done"), s.sem("lo_done")
        summed, evacuated = s.sem("summed"), s.sem("evacuated")
        xhi_done, xlo_done = s.sem("xhi_done"), s.sem("xlo_done")
        z_out = [s.sem("z_out0"), s.sem("z_out1")]
        mix_in = [s.sem("mix_in0"), s.sem("mix_in1")]
        n = None
        if mix is None:
            rstd, zout = s.sb("rstd", [P, T]), s.sb("zout", [P, 2, T])
            n = Norm(s, K, norm, sq, s.sb("acc", [P, T]), rstd,
                     [s.ps("sum0", [P, 512]), s.ps("sum1", [P, 512]), bank[1][2]])
        block = s.block()
        wv = w.rearrange("(k p) n -> p k n", p=P)

        @block.sync
        def _(sp):
            def load(g, i, width=P):
                sp.dma_start(raw[:, i, :, 0:width], wv[:, :, bass.ds(g * P, width)]).then_inc(raw_in[i], 16)

            def store(g, i, width=P):
                sp.wait_ge(evacuated, 3 * g + 9)
                sp.dma_start(z[bass.ds(g * P, width), :], zout[0:width, i, :]).then_inc(z_out[i], 16)

            load(0, 0)
            load(1, 1)
            if mix is not None:
                for k in range(KD):
                    if k >= 2:
                        sp.wait_ge(xlo_done, k - 1)
                    sp.dma_start(sq[:, k % 2, :], mix[k * P:(k + 1) * P, :]).then_inc(mix_in[k % 2], 16)
            with sp.Fori(1, pairs) as j:
                for i in range(2):
                    sp.wait_ge(lo_done, j * 2 + (i - 1))
                    load(j * 2 + i, i)
                    if z is not None:
                        store(j * 2 + (i - 2), i)
            for m, (col, width) in enumerate(tail):
                g = 2 * pairs + m
                sp.wait_ge(lo_done, g - 1)
                load(g, g % 2, width)
            if z is not None:
                for g in range(2 * pairs - 2, 2 * pairs + len(tail)):
                    store(g, g % 2, tail[g - 2 * pairs][1] if g >= 2 * pairs else P)
                total = 2 * pairs + len(tail)
                sp.wait_ge(z_out[0], 16 * ((total + 1) // 2))
                sp.wait_ge(z_out[1], 16 * (total // 2))

        @block.scalar
        def _(act):
            for k in range(KD):
                if mix is None:
                    act.activation(x_hi[:, k, :], K.xT[:, k, :], ACT.Copy,
                                   scale=K.norms[:, norm, k:k + 1]).then_inc(xhi_done, 1)
                else:
                    act.wait_ge(mix_in[k % 2], 16 * (k // 2 + 1))
                    act.activation(x_hi[:, k, :], sq[:, k % 2, :], ACT.Copy).then_inc(xhi_done, 1)

            def split(i, width=P):
                act.activation(w_hi[:, i, :, 0:width], raw[:, i, :, 0:width], ACT.Copy).then_inc(hi_done, 1)

            for i in range(2):
                act.wait_ge(raw_in[i], 16)
                split(i)
            if n is not None:
                n.act_squares(act)
                n.act_rstd(act)
            with act.Fori(1, pairs) as j:
                for i in range(2):
                    act.wait_ge(raw_in[i], j * 16 + 16)
                    act.wait_ge(summed, j * 6 + (3 * i - 3))
                    split(i)
            for m, (col, width) in enumerate(tail):
                g = 2 * pairs + m
                act.wait_ge(raw_in[g % 2], 16 * (g // 2 + 1))
                act.wait_ge(summed, 3 * g - 3)
                split(g % 2, width)

        @block.vector
        def _(dve):
            for k in range(KD):
                dve.wait_ge(xhi_done, k + 1)
                if mix is None:
                    dve.scalar_tensor_tensor(out=x_lo[:, k, :], in0=K.xT[:, k, :], scalar=K.norms[:, norm, k:k + 1],
                                             in1=r32(x_hi[:, k, :]), op0=ALU.mult, op1=ALU.subtract
                                             ).then_inc(xlo_done, 1)
                else:
                    dve.tensor_tensor(x_lo[:, k, :], sq[:, k % 2, :], r32(x_hi[:, k, :]),
                                      ALU.subtract).then_inc(xlo_done, 1)
            if n is not None:
                n.dve_sum(dve)
                dve.wait_ge(n.rstd_ready, NC)

            def evacuate(g, i, width=P):
                for c, (t0, tn) in enumerate(CHUNKS):
                    dve.wait_ge(summed, 3 * g + (c + 1))
                    if mix is None:
                        dve.tensor_tensor(zout[0:width, i, t0:t0 + tn], bank[i][c][0:width, 0:tn],
                                          rstd[0:width, t0:t0 + tn], ALU.mult).then_inc(evacuated, 1)
                    else:
                        x = K.xT[:, bass.ds(g, 1), t0:t0 + tn].rearrange("p k t -> p (k t)")
                        dve.tensor_tensor(x, x, bank[i][c][:, 0:tn], ALU.add).then_inc(evacuated, 1)

            for i in range(2):
                evacuate(i, i)
            with dve.Fori(1, pairs) as j:
                for i in range(2):
                    if z is not None:
                        dve.wait_ge(z_out[i], j * 16)
                    evacuate(j * 2 + i, i)
            for m, (col, width) in enumerate(tail):
                g = 2 * pairs + m
                if z is not None:
                    dve.wait_ge(z_out[g % 2], 16 * (g // 2))
                evacuate(g, g % 2, width)

        @block.gpsimd
        def _(pool):
            def split(g, i, width=P):
                pool.wait_ge(hi_done, g + 1)
                pool.tensor_tensor(w_lo[:, i, :, 0:width], raw[:, i, :, 0:width],
                                   r32(w_hi[:, i, :, 0:width]), ALU.subtract).then_inc(lo_done, 1)

            with pool.Fori(0, pairs) as j:
                for i in range(2):
                    split(j * 2 + i, i)
            for m, (col, width) in enumerate(tail):
                split(2 * pairs + m, (2 * pairs + m) % 2, width)

        @block.tensor
        def _(pe):
            pe.sem_inc(evacuated, 6)
            if n is not None:
                n.pe(pe)
                pe.wait_ge(n.logged, NC)
            pe.wait_ge(xlo_done, KD)

            def group(g, i):
                pe.wait_ge(lo_done, g + 1)
                for c, (t0, tn) in enumerate(CHUNKS):
                    pe.wait_ge(evacuated, 3 * g + (c + 1))
                    for k in range(KD):
                        last = mm3(pe, bank[i][c][:, 0:tn], w_hi[:, i, k, :], w_lo[:, i, k, :],
                                   x_hi[:, k, t0:t0 + tn], x_lo[:, k, t0:t0 + tn], k == 0, k == KD - 1)
                    last.then_inc(summed, 1)

            with pe.Fori(0, pairs) as j:
                for i in range(2):
                    group(j * 2 + i, i)
            for m in range(len(tail)):
                group(2 * pairs + m, (2 * pairs + m) % 2)



def mlp_stage(nc, K, name, norm, w_up, w_down):
    UP, DOWN = 4, KD
    blocks = FF // (UP * P)
    with Stage(nc, name) as s:
        x_hi, x_lo = s.sb("x_hi", [P, KD, T], F32R), s.sb("x_lo", [P, KD, T], F32R)
        a_hi, a_lo = s.sb("a_hi", [P, UP, T], F32R), s.sb("a_lo", [P, UP, T], F32R)
        raw = s.sb("raw", [P, 2, KD * P])
        w_hi, w_lo = s.sb("w_hi", [P, 2, KD * P], F32R), s.sb("w_lo", [P, 2, KD * P], F32R)
        sq = s.sb("sq", [P, 2, T])
        rstd = s.sb("rstd", [P, T])
        bank = [[s.ps(f"bank{i}{c}", [P, 512]) for c in range(NC)] for i in range(2)]
        n = Norm(s, K, norm, sq, s.sb("acc", [P, T]), rstd,
                 [s.ps("sum0", [P, 512]), s.ps("sum1", [P, 512]), bank[1][2]])
        relu, act2 = s.sb("relu", [P, 2, 384]), s.sb("act2", [P, 2, 384])
        raw_in = [s.sem("raw_in0"), s.sem("raw_in1")]
        hi_done, lo_done = s.sem("hi_done"), s.sem("lo_done")
        up_summed, up_out = s.sem("up_summed"), s.sem("up_out")
        down_summed, down_out = s.sem("down_summed"), s.sem("down_out")
        squared, ahi_done, alo_done = s.sem("squared_a"), s.sem("ahi_done"), s.sem("alo_done")
        xhi_done, xlo_done = s.sem("xhi_done"), s.sem("xlo_done")
        block = s.block()
        up_v = w_up.rearrange("(k p) f -> p k f", p=P)
        down_v = w_down.rearrange("(f p) d -> p f d", p=P)
        TILES = UP + DOWN // 2
        UPC, DNC = UP * NC, DOWN * NC

        def used_before(j, t):
            u = t - 2
            if u < 0:
                return down_summed, (j - 1) * DNC + NC * 2 * (TILES + u - UP + 1)
            if u < UP:
                return up_summed, j * UPC + NC * (u + 1)
            return down_summed, j * DNC + NC * 2 * (u - UP + 1)

        @block.sync
        def _(sp):
            def load(j, t):
                i = t % 2
                if t < UP:
                    src = up_v[:, :, bass.ds(j * (UP * P) + t * P, P)]
                    dst = raw[:, i, :].rearrange("p (k n) -> p k n", k=KD)
                else:
                    src = down_v[:, bass.ds(j * UP, UP), (t - UP) * 256:(t - UP + 1) * 256]
                    dst = raw[:, i, :].rearrange("p (f n) -> p f n", f=UP)
                sp.dma_start(dst, src).then_inc(raw_in[i], 16)

            def body(j, first=False):
                for t in range(TILES):
                    if not (first and t < 2):
                        sp.wait_ge(lo_done, j * TILES + (t - 1))
                    load(j, t)

            body(0, True)
            with sp.Fori(1, blocks) as j:
                body(j)

        @block.scalar
        def _(act):
            for k in range(KD):
                act.activation(x_hi[:, k, :], K.xT[:, k, :], ACT.Copy,
                               scale=K.norms[:, norm, k:k + 1]).then_inc(xhi_done, 1)

            def split(j, t, first=False):
                act.wait_ge(raw_in[t % 2], j * (16 * TILES // 2) + 16 * (t // 2 + 1))
                if not (first and t < 2):
                    act.wait_ge(*used_before(j, t))
                act.activation(w_hi[:, t % 2, :], raw[:, t % 2, :], ACT.Copy).then_inc(hi_done, 1)

            def square(j, u):
                for c, (t0, tn) in enumerate(CHUNKS):
                    m = u * NC + c
                    act.wait_ge(up_out, j * UPC + (m + 1))
                    act.wait_ge(alo_done, j * UPC + (m + 1))
                    act.activation(act2[:, m % 2, 0:tn], relu[:, m % 2, 0:tn], ACT.Square).then_inc(squared, 1)
                    act.wait_ge(squared, j * UPC + (m + 1))
                    act.activation(a_hi[:, u, t0:t0 + tn], act2[:, m % 2, 0:tn], ACT.Copy).then_inc(ahi_done, 1)

            def body(j, first=False):
                for t in range(TILES):
                    if 2 <= t < 2 + UP:
                        square(j, t - 2)
                    if not (first and t < 2):
                        split(j, t, first)

            split(0, 0, True)
            split(0, 1, True)
            n.act_squares(act)
            n.act_rstd(act)
            body(0, True)
            with act.Fori(1, blocks) as j:
                body(j)

        @block.gpsimd
        def _(pool):
            with pool.Fori(0, blocks) as j:
                for t in range(TILES):
                    pool.wait_ge(hi_done, j * TILES + (t + 1))
                    pool.tensor_tensor(w_lo[:, t % 2, :], raw[:, t % 2, :], r32(w_hi[:, t % 2, :]),
                                       ALU.subtract).then_inc(lo_done, 1)

        @block.vector
        def _(dve):
            for k in range(KD):
                dve.wait_ge(xhi_done, k + 1)
                dve.scalar_tensor_tensor(out=x_lo[:, k, :], in0=K.xT[:, k, :], scalar=K.norms[:, norm, k:k + 1],
                                         in1=r32(x_hi[:, k, :]), op0=ALU.mult, op1=ALU.subtract
                                         ).then_inc(xlo_done, 1)
            n.dve_sum(dve)
            dve.wait_ge(n.rstd_ready, NC)
            dve.sem_inc(alo_done, 2)

            def low(j, m):
                u, (t0, tn) = m // NC, CHUNKS[m % NC]
                dve.wait_ge(ahi_done, j * UPC + (m + 1))
                dve.tensor_tensor(a_lo[:, u, t0:t0 + tn], act2[:, m % 2, 0:tn], r32(a_hi[:, u, t0:t0 + tn]),
                                  ALU.subtract).then_inc(alo_done, 1)

            with dve.Fori(0, blocks) as j:
                for m in range(UPC):
                    u, (t0, tn) = m // NC, CHUNKS[m % NC]
                    dve.wait_ge(up_summed, j * UPC + (m + 1))
                    dve.scalar_tensor_tensor(out=relu[:, m % 2, 0:tn], in0=bank[u % 2][m % NC][:, 0:tn], scalar=0.0,
                                             in1=rstd[:, t0:t0 + tn], op0=ALU.max, op1=ALU.mult).then_inc(up_out, 1)
                    if m:
                        low(j, m - 1)
                low(j, UPC - 1)
                for d in range(DOWN):
                    for c, (t0, tn) in enumerate(CHUNKS):
                        dve.wait_ge(down_summed, j * DNC + (d * NC + c + 1))
                        dve.tensor_tensor(K.xT[:, d, t0:t0 + tn], K.xT[:, d, t0:t0 + tn], bank[d % 2][c][:, 0:tn],
                                          ALU.add).then_inc(down_out, 1)

        @block.tensor
        def _(pe):
            pe.sem_inc(down_out, 6)
            n.pe(pe)
            pe.wait_ge(n.logged, NC)
            pe.wait_ge(xlo_done, KD)

            def up(j, u):
                i = u % 2
                w = [w[:, i, :].rearrange("p (k n) -> p k n", k=KD) for w in (w_hi, w_lo)]
                pe.wait_ge(lo_done, j * TILES + (u + 1))
                for c, (t0, tn) in enumerate(CHUNKS):
                    if u < 2:
                        pe.wait_ge(down_out, j * DNC + (NC * u + c + 1))
                    else:
                        pe.wait_ge(up_out, j * UPC + (NC * (u - 2) + c + 1))
                    for k in range(KD):
                        last = mm3(pe, bank[i][c][:, 0:tn], w[0][:, k, :], w[1][:, k, :],
                                   x_hi[:, k, t0:t0 + tn], x_lo[:, k, t0:t0 + tn], k == 0, k == KD - 1)
                    last.then_inc(up_summed, 1)

            def down(j, d):
                i, t = d % 2, UP + d // 2
                w = [w[:, t % 2, :].rearrange("p (f n) -> p f n", f=UP)[:, :, (d % 2) * P:(d % 2 + 1) * P]
                     for w in (w_hi, w_lo)]
                pe.wait_ge(lo_done, j * TILES + (t + 1))
                for c in range(NC):
                    if d < 2:
                        pe.wait_ge(up_out, j * UPC + (NC * (UP - 2 + d) + c + 1))
                    else:
                        pe.wait_ge(down_out, j * DNC + (NC * (d - 2) + c + 7))
                    if d == 0:
                        if c == 0:
                            pe.wait_ge(alo_done, j * UPC + NC * (UP - 1) + 2)
                        fs = range(UP - 1)
                    else:
                        fs = range(UP)
                    for f in fs:
                        t0, tn = CHUNKS[c]
                        last = mm3(pe, bank[i][c][:, 0:tn], w[0][:, f, :], w[1][:, f, :],
                                   a_hi[:, f, t0:t0 + tn], a_lo[:, f, t0:t0 + tn], f == 0, f == UP - 1)
                    if d:
                        last.then_inc(down_summed, 1)
                if d == 0:
                    for c, (t0, tn) in enumerate(CHUNKS):
                        f = UP - 1
                        pe.wait_ge(alo_done, j * UPC + (NC * f + c + 3))
                        mm3(pe, bank[i][c][:, 0:tn], w[0][:, f, :], w[1][:, f, :],
                            a_hi[:, f, t0:t0 + tn], a_lo[:, f, t0:t0 + tn], False, True).then_inc(down_summed, 1)

            with pe.Fori(0, blocks) as j:
                for u in range(UP):
                    up(j, u)
                for d in range(DOWN):
                    down(j, d)



def latent_stage(nc, K, M):
    with Stage(nc, "latent") as s:
        cq = s.sb("cq", [P, 3, T])
        cq_hi, cq_lo = s.sb("cq_hi", [P, 3, T], F32R), s.sb("cq_lo", [P, 3, T], F32R)
        w_raw = s.sb("w_raw", [P, 3, HEADS, 192])
        w_hi, w_lo = s.sb("w_hi", [P, 3, 6, P], F32R), s.sb("w_lo", [P, 3, 6, P], F32R)
        cos, sin, rot = s.sb("cos", [P, T]), s.sb("sin", [P, T]), s.sb("rot", [P, P])
        norm_q, norm_kv = s.sb("norm_q", [P, 3]), s.sb("norm_kv", [P, 2])
        square = s.sb("square", [P, 5, T])
        rstd = s.sb("rstd", [P, 2, T])
        turned = s.sb("turned", [P, 2, 512])
        bank = [s.ps(f"bank{i}", [P, 512]) for i in range(8)]
        cq_in, ckv_in, kr_in, w_in, tab_in, norm_in = (s.sem(n) for n in ("cq_in", "ckv_in", "kr_in", "w_in", "tab_in", "norm_in"))
        squared, summed, logged, rstd_ready = (s.sem(n) for n in ("squared", "summed", "logged", "rstd_ready"))
        cq_normed, cqhi_done, cqlo_done = s.sem("cq_normed"), s.sem("cqhi_done"), s.sem("cqlo_done")
        whi_done, wlo_done = s.sem("whi_done"), s.sem("wlo_done")
        projected, q_out = s.sem("projected"), s.sem("q_out")
        rotated, rot_out, by_sin, by_cos = s.sem("rotated"), s.sem("rot_out"), s.sem("by_sin"), s.sem("by_cos")
        block = s.block()

        @block.sync
        def _(sp):
            sp.dma_start(cq[:], K.z[Z_CQ:Z_CKV, :].rearrange("(k p) t -> p k t", p=P)).then_inc(cq_in, 16)
            sp.dma_start(M.ckv[:], K.z[Z_CKV:Z_KR, :].rearrange("(k p) t -> p k t", p=P)).then_inc(ckv_in, 16)
            sp.dma_start(w_raw[:], K.w_uq[0].rearrange("(k p) (h n) -> p k h n", p=P, h=HEADS)).then_inc(w_in, 16)
            for i in range(2):
                sp.dma_start(M.kpe[64 * i:64 * i + 64, :], K.z[Z_KR:Z_KR + ROPE, :]).then_inc(kr_in, 16)
            for dst, src in ((cos, K.c_cos), (sin, K.c_sin), (rot, K.c_rot)):
                sp.dma_start(dst[:], src).then_inc(tab_in, 16)

        @block.gpsimd
        def _(pool):
            with nc.allow_non_contiguous_dma(reason="a column of each norm weight, once"):
                pool.dma_start(norm_q[:], K.q_norm[0].rearrange("(k p) -> p k", p=P)).then_inc(norm_in, 16)
                pool.dma_start(norm_kv[:], K.kv_norm[0].rearrange("(k p) -> p k", p=P)).then_inc(norm_in, 16)
            pool.wait_ge(norm_in, 32)
            pool.wait_ge(whi_done, 2)
            pool.wait_ge(w_in, 16)
            raw = w_raw[:]
            pool.tensor_tensor(w_lo[:, :, 0:4, :], raw[:, :, :, 0:P], r32(w_hi[:, :, 0:4, :]),
                               ALU.subtract).then_inc(wlo_done, 1)
            pool.tensor_tensor(w_lo[:, :, 4:6, :].rearrange("p k g (h n) -> p k (g h) n", h=2), raw[:, :, :, P:192],
                               r32(w_hi[:, :, 4:6, :]).rearrange("p k g (h n) -> p k (g h) n", h=2),
                               ALU.subtract).then_inc(wlo_done, 1)

        @block.scalar
        def _(act):
            act.wait_ge(cq_in, 16)
            for k in range(3):
                act.activation(square[:, k, :], cq[:, k, :], ACT.Square).then_inc(squared, 1)
            act.wait_ge(ckv_in, 16)
            for k in range(2):
                act.activation(square[:, 3 + k, :], M.ckv[:, k, :], ACT.Square).then_inc(squared, 1)
            act.wait_ge(w_in, 16)
            act.activation(w_hi[:, :, 0:4, :], w_raw[:, :, :, 0:P], ACT.Copy).then_inc(whi_done, 1)
            act.activation(w_hi[:, :, 4:6, :].rearrange("p k g (h n) -> p k (g h) n", h=2), w_raw[:, :, :, P:192],
                           ACT.Copy).then_inc(whi_done, 1)
            for m, width in ((0, Q_LORA), (1, KV_LORA)):
                for c, (t0, tn) in enumerate(CHUNKS):
                    act.wait_ge(summed, NC * m + c + 1)
                    act.activation(rstd[:, m, t0:t0 + tn], bank[NC * m + c][:, 0:tn], ACT.Ln,
                                   scale=1.0 / width, bias=K.eps[:, 0:1]).then_inc(logged, 1)
                act.wait_ge(logged, NC * (m + 1))
                act.activation(rstd[:, m, :], rstd[:, m, :], ACT.Exp, scale=-0.5).then_inc(rstd_ready, 1)
            for k in range(3):
                act.wait_ge(cq_normed, k + 1)
                act.activation(cq_hi[:, k, :], cq[:, k, :], ACT.Copy).then_inc(cqhi_done, 1)
            for g in range(6):
                for c, (t0, tn) in enumerate(CHUNKS):
                    act.wait_ge(projected, NC * g + c + 1)
                    dst = M.qn[:, g, t0:t0 + tn] if g < 4 else M.qpe[:, g - 4, t0:t0 + tn]
                    act.activation(dst, bank[NC * (g % 2) + c][:, 0:tn], ACT.Copy).then_inc(q_out, 1)

        @block.tensor
        def _(pe):
            for m, ks in ((0, range(3)), (1, range(3, 5))):
                pe.wait_ge(squared, ks[-1] + 1)
                for c, (t0, tn) in enumerate(CHUNKS):
                    for k in ks:
                        last = pe.matmul(bank[NC * m + c][:, 0:tn], K.ones[:], square[:, k, t0:t0 + tn],
                                         start=(k == ks[0]), stop=(k == ks[-1]))
                    last.then_inc(summed, 1)
            pe.wait_ge(logged, 2 * NC)
            pe.wait_ge(wlo_done, 2)
            pe.wait_ge(cqlo_done, 3)
            for g in range(6):
                for c, (t0, tn) in enumerate(CHUNKS):
                    if g >= 2:
                        pe.wait_ge(q_out, NC * (g - 2) + c + 1)
                    for k in range(3):
                        last = mm3(pe, bank[NC * (g % 2) + c][:, 0:tn], w_hi[:, k, g, :], w_lo[:, k, g, :],
                                   cq_hi[:, k, t0:t0 + tn], cq_lo[:, k, t0:t0 + tn], k == 0, k == 2)
                    last.then_inc(projected, 1)
            pe.wait_ge(q_out, 6 * NC)
            pe.wait_ge(tab_in, 48)
            pe.wait_ge(kr_in, 32)
            for m, x in enumerate((M.qpe[:, 0, :], M.qpe[:, 1, :], M.kpe[:])):
                for c, (t0, tn) in enumerate(CHUNKS):
                    i = NC * m + c
                    if i >= 2:
                        pe.wait_ge(by_sin, i - 1)
                    pe.matmul(bank[6 + i % 2][:, 0:tn], rot[:], x[:, t0:t0 + tn], start=True, stop=True
                              ).then_inc(rotated, 1)

        @block.vector
        def _(dve):
            dve.wait_ge(norm_in, 32)
            dve.wait_ge(rstd_ready, 1)
            for k in range(3):
                dve.scalar_tensor_tensor(out=cq[:, k, :], in0=cq[:, k, :], scalar=norm_q[:, k:k + 1], in1=rstd[:, 0, :],
                                         op0=ALU.mult, op1=ALU.mult).then_inc(cq_normed, 1)
            for k in range(3):
                dve.wait_ge(cqhi_done, k + 1)
                dve.tensor_tensor(cq_lo[:, k, :], cq[:, k, :], r32(cq_hi[:, k, :]), ALU.subtract).then_inc(cqlo_done, 1)
            dve.wait_ge(rstd_ready, 2)
            for k in range(2):
                dve.scalar_tensor_tensor(out=M.ckv[:, k, :], in0=M.ckv[:, k, :], scalar=norm_kv[:, k:k + 1],
                                         in1=rstd[:, 1, :], op0=ALU.mult, op1=ALU.mult)
            for m, x in enumerate((M.qpe[:, 0, :], M.qpe[:, 1, :], M.kpe[:])):
                for c, (t0, tn) in enumerate(CHUNKS):
                    i = NC * m + c
                    dve.wait_ge(rotated, i + 1)
                    dve.tensor_tensor(turned[:, i % 2, 0:tn], bank[6 + i % 2][:, 0:tn], sin[:, t0:t0 + tn],
                                      ALU.mult).then_inc(by_sin, 1)
                    dve.tensor_tensor(x[:, t0:t0 + tn], x[:, t0:t0 + tn], cos[:, t0:t0 + tn], ALU.mult).then_inc(by_cos, 1)
                    dve.wait_ge(by_sin, i + 1)
                    dve.wait_ge(by_cos, i + 1)
                    dve.tensor_tensor(x[:, t0:t0 + tn], x[:, t0:t0 + tn], turned[:, i % 2, 0:tn],
                                      ALU.add).then_inc(rot_out, 1)


def keys_stage(nc, K, M):
    with Stage(nc, "keys") as s:
        wuk = s.sb("wuk", [P, HEADS, 2, P])
        wukT = s.sb("wukT", [P, HEADS, 2, P])
        bank = [s.ps(f"bank{i}", [P, 512]) for i in range(4)]
        wuk_in, wuv_in, rows_out = s.sem("wuk_in"), s.sem("wuv_in"), s.sem("rows_out")
        made, out_act, out_dve = s.sem("made"), s.sem("out_act"), s.sem("out_dve")
        block = s.block()
        KN, V, WT, ROWS, QL = 0, 8, 16, 20, 29
        END = 33

        @block.sync
        def _(sp):
            sp.dma_start(wuk[:], K.w_uk[0].rearrange("h (k p) n -> p (h k) n", p=P)).then_inc(wuk_in, 16)
            for k in range(2):
                sp.dma_start(M.wuv[:, k, :, :], K.w_uv[0][:, k * P:(k + 1) * P, :].rearrange("h p v -> p h v")
                             ).then_inc(wuv_in, 16)
            sp.wait_ge(out_act, (ROWS + 10) // 2)
            sp.wait_ge(out_dve, (ROWS + 8) // 2)
            sp.dma_start(K.rows_prompt.rearrange("(i p) c -> p i c", p=P), M.rows[:, 0:8, :]).then_inc(rows_out, 16)
            sp.dma_start(K.rows_sample, M.rows[0:NS, 8, :]).then_inc(rows_out, 16)
            sp.wait_ge(rows_out, 32)

        @block.tensor
        def _(pe):
            def free(n):
                if n >= 4:
                    pe.wait_ge(out_act if n % 2 == 0 else out_dve, (n - 4) // 2 + 1)
                return bank[n % 4]

            pe.wait_ge(wuk_in, 16)
            pe.wait_ge(wuv_in, 32)
            for n in range(8):
                h, half = n // 2, n % 2
                b = free(KN + n)
                for k in range(2):
                    last = pe.matmul(b[:], wuk[:, h, k, :], M.ckv[:, k, half * 512:half * 512 + 512],
                                     start=(k == 0), stop=(k == 1))
                last.then_inc(made, 1)
            for n in range(8):
                b = free(V + n)
                for k in range(2):
                    last = pe.matmul(b[:], M.ckv[:, k, n * P:(n + 1) * P],
                                     M.wuv[:, k, :, :].rearrange("p h v -> p (h v)"), start=(k == 0), stop=(k == 1))
                last.then_inc(made, 1)
            for h in range(HEADS):
                b = free(WT + h)
                for k in range(2):
                    last = pe.transpose(b[:, k * P:(k + 1) * P], wuk[:, h, k, :], K.ident[:])
                last.then_inc(made, 1)
            for n in range(9):
                b, rows = free(ROWS + n), (P if n < 8 else NS)
                for k in range(2):
                    pe.transpose(b[0:rows, k * P:(k + 1) * P], M.ckv[:, k, n * P:n * P + rows], K.ident[:])
                pe.transpose(b[0:rows, KV_LORA:LAT], M.kpe[0:ROPE, n * P:n * P + rows], K.ident[0:ROPE, 0:ROPE]
                             ).then_inc(made, 1)
            for h in range(HEADS):
                b = free(QL + h)
                if h == 0:
                    pe.wait_ge(out_act, (WT + 4) // 2)
                    pe.wait_ge(out_dve, (WT + 4) // 2)
                for k in range(2):
                    last = pe.matmul(b[:, k * NS:(k + 1) * NS], wukT[:, h, k, :], M.qn[:, h, SEQ:T],
                                     start=True, stop=True)
                last.then_inc(made, 1)

        def copies(eng, copy, parity, out):
            for n in range(parity, END, 2):
                b = bank[n % 4]
                eng.wait_ge(made, n + 1)
                if n < V:
                    h, half = n // 2, n % 2
                    last = copy(M.kn[:, h, half * 512:half * 512 + 512], b[:])
                elif n < WT:
                    last = copy(M.v[:, n - V, :], b[:])
                elif n < ROWS:
                    last = copy(wukT[:, n - WT, :, :].rearrange("p k c -> p (k c)"), b[:, 0:2 * P])
                elif n < QL:
                    rows = P if n - ROWS < 8 else NS
                    last = copy(M.rows[0:rows, n - ROWS, :], b[0:rows, 0:LAT])
                else:
                    last = copy(M.qs[:, 0:2, :, n - QL, :], b[:, 0:2 * NS].rearrange("p (k b t) -> p k b t", k=2, b=NB))
                last.then_inc(out, 1)

        @block.gpsimd
        def _(pool):
            pool.memset(M.qs[ROPE:P, 2, :, :, :], 0.0)

        @block.scalar
        def _(act):
            for h in range(HEADS):
                o = 64 * (h % 2)
                act.activation(M.qs[0:ROPE, 2, :, h, :],
                               M.qpe[o:o + ROPE, h // 2, SEQ:T].rearrange("p (b t) -> p b t", b=NB), ACT.Copy)
            copies(act, lambda o, x: act.activation(o, x, ACT.Copy), 0, out_act)

        @block.vector
        def _(dve):
            copies(dve, lambda o, x: dve.tensor_copy(o, x), 1, out_dve)


def prompt_attention_stage(nc, K, M):
    with Stage(nc, "pattn") as s:
        q = s.sb("q", [P, 2, SEQ])
        qpe = s.sb("qpe", [P, SEQ])
        v = s.sb("v", [P, 2, 8, P])
        p, pT = s.sb("p", [P, 2, SEQ]), s.sb("pT", [P, 2, 8, P])
        o = s.sb("o", [P, 2, SEQ])
        diag = s.sb("diag", [P, P])
        top, ntop, den, rden = (s.sb(n, [P, 2]) for n in ("top", "ntop", "den", "rden"))
        S = [s.ps(f"S{i}", [P, SEQ]) for i in range(2)]
        PT = s.ps("PT", [P, 8, P])
        O = [s.ps(f"O{i}", [P, 512]) for i in range(2)]
        diag_in, q_ready = s.sem("diag_in"), s.sem("q_ready")
        scored, masked, topped, ntopped = s.sem("scored"), s.sem("masked"), s.sem("topped"), s.sem("ntopped")
        expd, inverted, p_ready, turned = s.sem("expd"), s.sem("inverted"), s.sem("p_ready"), s.sem("turned")
        out_lo, out_hi, valued, o_out = s.sem("out_lo"), s.sem("out_hi"), s.sem("valued"), s.sem("o_out")
        stored = [s.sem("stored0"), s.sem("stored1")]
        o_free = s.sem("o_free")
        block = s.block()
        TILES = 16

        @block.sync
        def _(sp):
            sp.dma_start(diag[:], K.c_causal).then_inc(diag_in, 16)
            sp.sem_inc(o_free, 2)
            with sp.Fori(0, 2) as i:
                for hd in range(2):
                    sp.wait_ge(o_out, i * TILES + (8 * hd + 10))
                    sp.dma_start(K.mix[bass.ds(i * 256 + (512 + P * hd), P), 0:SEQ], o[:, hd, :]).then_inc(stored[hd], 16)
                for hd in range(2):
                    sp.wait_ge(stored[hd], i * 16 + 16)
                    sp.sem_inc(o_free, 1)

        @block.vector
        def _(dve):
            def soften(i, n):
                hd, qt, x = n // 8, n % 8, n % 2
                dve.wait_ge(scored, i * TILES + (n + 1))
                d = S[x][:, qt * P:(qt + 1) * P]
                dve.tensor_tensor(d, d, diag[:], ALU.add).then_inc(masked, 1)
                dve.wait_ge(masked, i * TILES + (n + 1))
                dve.tensor_reduce(top[:, x:x + 1], S[x][:, 0:(qt + 1) * P], AX.X, ALU.max).then_inc(topped, 1)
                dve.wait_ge(topped, i * TILES + (n + 1))
                dve.tensor_scalar(ntop[:, x:x + 1], top[:, x:x + 1], -SCALE, None, ALU.mult).then_inc(ntopped, 1)

            def divide(i, n):
                hd, qt, x = n // 8, n % 8, n % 2
                dve.wait_ge(expd, i * TILES + (n + 3))
                dve.reciprocal(rden[:, x:x + 1], den[:, x:x + 1]).then_inc(inverted, 1)
                dve.wait_ge(inverted, i * TILES + (n + 1))
                dve.tensor_scalar(p[:, x, 0:(qt + 1) * P], p[:, x, 0:(qt + 1) * P], rden[:, x:x + 1], None,
                                  ALU.mult).then_inc(p_ready, 1)

            def copy_hi(i, n):
                hd, qt, x = n // 8, n % 8, n % 2
                if qt >= 4:
                    dve.wait_ge(turned, i * TILES + (n + 3))
                    dve.wait_ge(valued, i * TILES + (n + 1))
                    dve.tensor_copy(pT[:, x, 4:qt + 1, :], PT[:, 4:qt + 1, :]).then_inc(out_hi, 1)

            dve.wait_ge(diag_in, 16)
            dve.sem_inc(out_hi, 1)
            with dve.Fori(0, 2) as i:
                dve.wait_ge(valued, i * TILES + 2)
                for hd in range(2):
                    h = i * 2 + hd
                    dve.tensor_copy(q[:, hd, :], M.qn[:, bass.ds(h, 1), 0:SEQ].rearrange("p a t -> p (a t)"))
                    dve.tensor_copy(v[:, hd, :, :], M.v[:, :, bass.ds(h * P, P)])
                dve.tensor_copy(qpe[:], M.qpe[:, bass.ds(i, 1), 0:SEQ].rearrange("p a t -> p (a t)")).then_inc(q_ready, 1)
                soften(i, 0)
                for n in range(TILES):
                    divide(i, n)
                    if n + 1 < TILES:
                        soften(i, n + 1)
                    copy_hi(i, n)

        @block.scalar
        def _(act):
            act.sem_inc(expd, 2)
            act.sem_inc(out_lo, 1)
            act.sem_inc(o_out, 2)

            def softmax(i, n):
                hd, qt, x = n // 8, n % 8, n % 2
                act.wait_ge(ntopped, i * TILES + (n + 1))
                act.wait_ge(turned, i * TILES + (n + 1))
                act.activation(p[:, x, 0:(qt + 1) * P], S[x][:, 0:(qt + 1) * P], ACT.Exp, bias=ntop[:, x:x + 1],
                               scale=SCALE, accum_out=den[:, x:x + 1]).then_inc(expd, 1)

            def copy_lo(i, n):
                hd, qt, x = n // 8, n % 8, n % 2
                m = min(qt + 1, 4)
                act.wait_ge(turned, i * TILES + (n + 3))
                act.wait_ge(valued, i * TILES + (n + 1))
                act.activation(pT[:, x, 0:m, :], PT[:, 0:m, :], ACT.Copy).then_inc(out_lo, 1)

            def copy_o(i, n):
                hd, qt, x = n // 8, n % 8, n % 2
                act.wait_ge(valued, i * TILES + (n + 3))
                if qt == 0:
                    act.wait_ge(o_free, i * 2 + (hd + 1))
                act.activation(o[:, hd, qt * P:(qt + 1) * P], O[x][:, 0:P], ACT.Copy).then_inc(o_out, 1)

            with act.Fori(0, 2) as i:
                softmax(i, 0)
                for n in range(TILES):
                    if n + 1 < TILES:
                        softmax(i, n + 1)
                    copy_lo(i, n)
                    if n:
                        copy_o(i, n - 1)
                copy_o(i, TILES - 1)

        @block.tensor
        def _(pe):
            pe.sem_inc(turned, 2)
            pe.sem_inc(valued, 2)

            def score(i, n):
                hd, qt, x = n // 8, n % 8, n % 2
                pe.wait_ge(expd, i * TILES + (n + 1))
                keys, o64 = (qt + 1) * P, 64 * hd
                for k0 in range(0, keys, 512):
                    kn = min(512, keys - k0)
                    pe.matmul(S[x][:, k0:k0 + kn], q[:, hd, qt * P:(qt + 1) * P],
                              M.kn[:, bass.ds(i * 2 + hd, 1), k0:k0 + kn].rearrange("p a t -> p (a t)"),
                              start=True, stop=False)
                    last = pe.matmul(S[x][:, k0:k0 + kn], qpe[o64:o64 + 64, qt * P:(qt + 1) * P],
                                     M.kpe[o64:o64 + 64, k0:k0 + kn], start=False, stop=True)
                last.then_inc(scored, 1)

            def turn(i, n):
                hd, qt, x = n // 8, n % 8, n % 2
                pe.wait_ge(p_ready, i * TILES + (n + 1))
                pe.wait_ge(out_lo, i * TILES + (n + 1))
                if qt >= 4:
                    pe.wait_ge(out_hi, i * 8 + (4 * hd + qt - 3))
                for k in range(qt + 1):
                    last = pe.transpose(PT[:, k, :], p[:, x, k * P:(k + 1) * P], K.ident[:])
                last.then_inc(turned, 1)

            def value(i, n):
                hd, qt, x = n // 8, n % 8, n % 2
                pe.wait_ge(out_lo, i * TILES + (n + 2))
                if qt >= 4:
                    pe.wait_ge(out_hi, i * 8 + (4 * hd + qt - 2))
                pe.wait_ge(o_out, i * TILES + (n + 1))
                for k in range(qt + 1):
                    last = pe.matmul(O[x][:, 0:P], v[:, hd, k, :], pT[:, x, k, :], start=(k == 0), stop=(k == qt))
                last.then_inc(valued, 1)

            with pe.Fori(0, 2) as i:
                pe.wait_ge(q_ready, i + 1)
                score(i, 0)
                for n in range(TILES):
                    if n + 1 < TILES:
                        score(i, n + 1)
                    turn(i, n)
                    if n:
                        value(i, n - 1)
                value(i, TILES - 1)


def sample_attention_stage(nc, K, M):
    GROUPS = PAGES // PG
    RING = 4
    Q = HEADS * TS
    with Stage(nc, "sattn") as s:
        lat = s.sb("lat", [P, RING, PG, LAT])
        pages = s.sb("pages", [1, NB * PAGES], I32)
        newmask = s.sb("newmask", [Q, NB, NS])
        q = s.sb("q", [P, 3, Q])
        kT = s.sb("kT", [P, 3, 512])
        p, pT = s.sb("p", [Q, 2, 512]), s.sb("pT", [P, PG, Q])
        pn, pnT, sn = s.sb("pn", [Q, NS]), s.sb("pnT", [NS, Q]), s.sb("sn", [Q, NS])
        m, den, acc = s.sb("m", [Q, 2]), s.sb("den", [Q, 1]), s.sb("acc", [Q, KV_LORA])
        gm, nm, alpha, gsum, rden = (s.sb(n, [Q, 1]) for n in ("gm", "nm", "alpha", "gsum", "rden"))
        outT = s.sb("outT", [P, 2, HEADS, NS])
        o = s.sb("o", [P, HEADS, NS])
        KT = s.ps("KT", [P, 3, 512])
        S = [s.ps(f"S{i}", [P, 512]) for i in range(2)]
        PT, O, X = s.ps("PT", [P, 512]), s.ps("O", [P, 512]), s.ps("X", [P, 512])
        SN, PNT, OT = X[0:Q, 0:NS], X[0:NS, 128:128 + Q], X[:, 256:256 + 2 * Q]
        tab_in, lat_in = s.sem("tab_in"), [s.sem(f"lat_in{i}") for i in range(RING)]
        q_ready, passed = s.sem("q_ready"), s.sem("passed")
        sn_made, sn_masked, pn_made, pn_turned, pn_out = (s.sem(n) for n in ("sn_made", "sn_masked", "pn_made", "pn_turned", "pn_out"))
        on_made, on_out = s.sem("on_made"), s.sem("on_out")
        kt_made, kt_act, kt_dve = s.sem("kt_made"), s.sem("kt_act"), s.sem("kt_dve")
        scored, topped, chain, expd = (s.sem(n) for n in ("scored", "topped", "chain", "expd"))
        turned, pt_out, valued, acc_done = (s.sem(n) for n in ("turned", "pt_out", "valued", "acc_done"))
        acc_final, ot_made, ot_out = s.sem("acc_final"), s.sem("ot_made"), s.sem("ot_out")
        o_made, o_out, stored = s.sem("o_made"), s.sem("o_out"), s.sem("stored")
        block = s.block()
        n_phys = K.cache.shape[0]

        @block.sync
        def _(sp):
            sp.dma_start(pages[:], K.page_table).then_inc(tab_in, 16)
            sp.dma_start(newmask[:], K.c_newmask).then_inc(tab_in, 16)
            sp.wait_ge(tab_in, 32)

            def load(g, i):
                for n in range(PG):
                    page = sp.value_load(pages[0:1, bass.ds(g * PG + n, 1)], min_val=0, max_val=n_phys - 1)
                    sp.dma_start(lat[:, i, n, :], K.cache[bass.ds(page, 1), :, :].rearrange("a p c -> (a p) c")
                                 ).then_inc(lat_in[i], 16)

            for i in range(RING):
                load(i, i)
            with sp.Fori(1, NB * GROUPS // RING) as j:
                for i in range(RING):
                    sp.wait_ge(valued, j * RING + (i - RING + 1))
                    load(j * RING + i, i)
            sp.wait_ge(o_out, 1)
            sp.dma_start(K.mix[512:1024, SEQ:T].rearrange("(h p) t -> p h t", p=P), o[:]).then_inc(stored, 16)
            sp.wait_ge(stored, 16)

        @block.tensor
        def _(pe):
            def turn_keys(b, g, i):
                pe.wait_ge(lat_in[i % RING], b * (16 * PAGES // RING) + g * (16 * PG // RING) + (i // RING + 1) * 16 * PG)
                for c, w in ((0, P), (1, P), (2, ROPE)):
                    for n in range(PG):
                        last = pe.transpose(KT[0:w, c, n * P:(n + 1) * P], lat[:, i % RING, n, c * P:c * P + w], K.ident[:])
                last.then_inc(kt_made, 1)

            def score(b, g, i):
                pe.wait_ge(kt_act, b * GROUPS + g + (i + 1))
                pe.wait_ge(kt_dve, b * GROUPS + g + (i + 1))
                pe.wait_ge(expd, b * GROUPS + g + (i + 1))
                for c, w in ((0, P), (1, P), (2, ROPE)):
                    last = pe.matmul(S[i % 2][0:Q, :], q[0:w, c, :], kT[0:w, c, :], start=(c == 0), stop=(c == 2))
                last.then_inc(scored, 1)

            def value(b, g, i):
                wait_apart(pe, expd, b * GROUPS + g + (i + 3), passed)
                wait_apart(pe, pt_out, b * GROUPS + g + (i + 1), passed)
                for n in range(PG):
                    last = pe.transpose(PT[:, n * Q:(n + 1) * Q], p[:, i % 2, n * P:(n + 1) * P], K.ident[0:Q, 0:Q])
                last.then_inc(turned, 1)
                pe.wait_ge(pt_out, b * GROUPS + g + (i + 2))
                pe.wait_ge(acc_done, b * GROUPS + g + (i + 1))
                for n in range(PG):
                    last = pe.matmul(O[0:Q, 0:KV_LORA], pT[:, n, :], lat[:, i % RING, n, 0:KV_LORA],
                                     start=(n == 0), stop=(n == PG - 1))
                last.then_inc(valued, 1)

            pe.sem_inc(turned, 2)
            with pe.Fori(0, NB) as b:
                pe.wait_ge(q_ready, b + 1)
                for c, w in ((0, P), (1, P), (2, ROPE)):
                    k = M.ckv[:, c, SEQ:T] if c < 2 else M.kpe[0:ROPE, SEQ:T]
                    last = pe.matmul(SN, q[0:w, c, :], k, start=(c == 0), stop=(c == 2))
                last.then_inc(sn_made, 1)
                turn_keys(b, 0, 0)
                wait_apart(pe, pn_made, b + 1, passed)
                pe.transpose(PNT, pn[:], K.ident[0:Q, 0:Q]).then_inc(pn_turned, 1)
                wait_apart(pe, pn_out, b + 1, passed)
                wait_apart(pe, acc_done, b * GROUPS + 1, passed)
                pe.matmul(O[0:Q, 0:KV_LORA], pnT[:], M.rows[0:NS, 8, 0:KV_LORA], start=True, stop=True).then_inc(on_made, 1)
                score(b, 0, 0)
                wait_apart(pe, on_out, b + 1, passed)
                with pe.Fori(0, GROUPS - RING, RING) as g:
                    for i in range(RING):
                        turn_keys(b, g, i + 1)
                        value(b, g, i)
                        score(b, g, i + 1)
                for i in range(RING):
                    if i + 1 < RING:
                        turn_keys(b, GROUPS - RING, i + 1)
                    value(b, GROUPS - RING, i)
                    if i + 1 < RING:
                        score(b, GROUPS - RING, i + 1)
                wait_apart(pe, acc_final, b + 1, passed)
                for c in range(2):
                    last = pe.transpose(OT[:, c * Q:(c + 1) * Q], acc[:, c * P:(c + 1) * P], K.ident[0:Q, 0:Q])
                last.then_inc(ot_made, 1)
                pe.wait_ge(ot_out, b + 2)
            for h in range(HEADS):
                for c in range(2):
                    last = pe.matmul(X[:, h * NS:(h + 1) * NS], M.wuv[:, c, h, :], outT[:, c, h, :],
                                     start=(c == 0), stop=(c == 1))
            last.then_inc(o_made, 1)

        @block.scalar
        def _(act):
            act.sem_inc(expd, 2)

            def copy_keys(b, g, i):
                act.wait_ge(kt_made, b * GROUPS + g + (i + 1))
                act.activation(kT[:, 0, :], KT[:, 0, :], ACT.Copy)
                act.activation(kT[0:ROPE, 2, :], KT[0:ROPE, 2, :], ACT.Copy).then_inc(kt_act, 1)

            def softmax(b, g, i):
                act.wait_ge(topped, b * GROUPS + g + (i + 1))
                act.activation(alpha[:], m[:, (i + 1) % 2:(i + 1) % 2 + 1], ACT.Exp, bias=nm[:, 0:1], scale=SCALE)
                act.wait_ge(turned, b * GROUPS + g + (i + 1))
                act.activation(p[:, i % 2, :], S[i % 2][0:Q, :], ACT.Exp, bias=nm[:, 0:1], scale=SCALE,
                               accum_out=gsum[:, 0:1]).then_inc(expd, 1)

            with act.Fori(0, NB) as b:
                act.wait_ge(sn_masked, b + 1)
                act.activation(pn[:], sn[:], ACT.Exp, bias=nm[:, 0:1], scale=SCALE, accum_out=den[:, 0:1]).then_inc(pn_made, 1)
                copy_keys(b, 0, 0)
                act.wait_ge(pn_turned, b + 1)
                act.activation(pnT[:], PNT, ACT.Copy).then_inc(pn_out, 1)
                with act.Fori(0, GROUPS - RING, RING) as g:
                    for i in range(RING):
                        softmax(b, g, i)
                        copy_keys(b, g, i + 1)
                for i in range(RING):
                    softmax(b, GROUPS - RING, i)
                    if i + 1 < RING:
                        copy_keys(b, GROUPS - RING, i + 1)
                act.wait_ge(ot_made, b + 1)
                act.activation(outT[:, :, :, bass.ds(b * TS, TS)],
                               OT.rearrange("p (c h t) -> p c h t", c=2, h=HEADS), ACT.Copy).then_inc(ot_out, 1)
            act.wait_ge(o_made, 1)
            act.activation(o[:], X[:, 0:HEADS * NS].rearrange("p (h t) -> p h t", h=HEADS), ACT.Copy).then_inc(o_out, 1)

        @block.vector
        def _(dve):
            CH = 2 + 2 * GROUPS + 1

            def copy_keys(b, g, i):
                dve.wait_ge(kt_made, b * GROUPS + g + (i + 1))
                dve.tensor_copy(kT[:, 1, :], KT[:, 1, :]).then_inc(kt_dve, 1)

            def top(b, g, i):
                x, link = i % 2, b * CH + g * 2 + (2 + 2 * i)
                dve.wait_ge(scored, b * GROUPS + g + (i + 1))
                dve.tensor_reduce(gm[:], S[x][0:Q, :], AX.X, ALU.max).then_inc(chain, 1)
                dve.wait_ge(chain, link + 1)
                dve.tensor_tensor(m[:, x:x + 1], m[:, 1 - x:2 - x], gm[:], ALU.max).then_inc(chain, 1)
                dve.wait_ge(chain, link + 2)
                dve.tensor_scalar(nm[:], m[:, x:x + 1], -SCALE, None, ALU.mult).then_inc(topped, 1)

            def gather(b, g, i):
                dve.wait_ge(turned, b * GROUPS + g + (i + 3))
                dve.tensor_copy(pT[:], PT[:, 0:PG * Q]).then_inc(pt_out, 1)
                dve.wait_ge(expd, b * GROUPS + g + (i + 3))
                dve.scalar_tensor_tensor(out=den[:], in0=den[:], scalar=alpha[:, 0:1], in1=gsum[:],
                                         op0=ALU.mult, op1=ALU.add)
                dve.wait_ge(valued, b * GROUPS + g + (i + 1))
                dve.scalar_tensor_tensor(out=acc[:], in0=acc[:], scalar=alpha[:, 0:1], in1=O[0:Q, 0:KV_LORA],
                                         op0=ALU.mult, op1=ALU.add).then_inc(acc_done, 1)

            dve.sem_inc(pt_out, 1)
            dve.sem_inc(acc_done, 1)
            dve.sem_inc(ot_out, 1)
            dve.wait_ge(tab_in, 32)
            with dve.Fori(0, NB) as b:
                dve.wait_ge(ot_out, b + 1)
                dve.tensor_copy(q[:], M.qs[:, :, bass.ds(b, 1), :, :].rearrange("p c a h t -> p c (a h t)")).then_inc(q_ready, 1)
                dve.wait_ge(sn_made, b + 1)
                dve.tensor_tensor(sn[:], SN, newmask[:, bass.ds(b, 1), :].rearrange("p a t -> p (a t)"), ALU.add).then_inc(chain, 1)
                dve.wait_ge(chain, b * CH + 1)
                dve.tensor_reduce(m[:, 1:2], sn[:], AX.X, ALU.max).then_inc(chain, 1)
                dve.wait_ge(chain, b * CH + 2)
                dve.tensor_scalar(nm[:], m[:, 1:2], -SCALE, None, ALU.mult).then_inc(sn_masked, 1)
                copy_keys(b, 0, 0)
                dve.wait_ge(pn_made, b + 1)
                dve.wait_ge(on_made, b + 1)
                dve.tensor_copy(acc[:], O[0:Q, 0:KV_LORA]).then_inc(on_out, 1)
                wait_apart(dve, on_out, b + 1, passed)
                with dve.Fori(0, GROUPS - RING, RING) as g:
                    for i in range(RING):
                        top(b, g, i)
                        copy_keys(b, g, i + 1)
                        gather(b, g, i)
                for i in range(RING):
                    top(b, GROUPS - RING, i)
                    if i + 1 < RING:
                        copy_keys(b, GROUPS - RING, i + 1)
                    gather(b, GROUPS - RING, i)
                dve.wait_ge(acc_done, b * GROUPS + (GROUPS + 1))
                dve.reciprocal(rden[:], den[:]).then_inc(chain, 1)
                dve.wait_ge(chain, b * CH + CH)
                dve.tensor_scalar(acc[:], acc[:], rden[:, 0:1], None, ALU.mult).then_inc(acc_final, 1)



def alpha_stage(nc, K):
    with Stage(nc, "alpha") as s:
        a1, w2, bias = s.sb("a1", [GATE_RANK, T]), s.sb("w2", [GATE_RANK, HEADS * P]), s.sb("bias", [P, HEADS])
        out = s.sb("out", [P, HEADS, T])
        bank = [[s.ps(f"bank{i}{c}", [P, 512]) for c in range(NC)] for i in range(2)]
        loaded, projected, biased, stored = (s.sem(n) for n in ("loaded", "projected", "biased", "stored"))
        block = s.block()

        @block.sync
        def _(sp):
            sp.dma_start(a1[:], K.z[G_A:G_A + GATE_RANK, :]).then_inc(loaded, 16)
            sp.dma_start(w2[:], K.w_alpha2[0]).then_inc(loaded, 16)
            with nc.allow_non_contiguous_dma(reason="a column of b_alpha for each head, once"):
                sp.dma_start(bias[:], K.b_alpha[0].rearrange("(h p) -> p h", p=P)).then_inc(loaded, 16)
            for h in range(HEADS):
                sp.wait_ge(biased, NC * (h + 1))
                sp.dma_start(K.z[G_GATE + h * P:G_GATE + (h + 1) * P, :], out[:, h, :]).then_inc(stored, 16)
            sp.wait_ge(stored, 16 * HEADS)

        @block.tensor
        def _(pe):
            pe.wait_ge(loaded, 48)
            for h in range(HEADS):
                for c, (t0, tn) in enumerate(CHUNKS):
                    if h >= 2:
                        pe.wait_ge(biased, NC * (h - 2) + c + 1)
                    pe.matmul(bank[h % 2][c][:, 0:tn], w2[:, h * P:(h + 1) * P], a1[:, t0:t0 + tn],
                              start=True, stop=True).then_inc(projected, 1)

        @block.scalar
        def _(act):
            act.wait_ge(loaded, 48)
            for h in range(HEADS):
                for c, (t0, tn) in enumerate(CHUNKS):
                    act.wait_ge(projected, NC * h + c + 1)
                    act.activation(out[:, h, t0:t0 + tn], bank[h % 2][c][:, 0:tn], ACT.Identity,
                                   bias=bias[:, h:h + 1]).then_inc(biased, 1)


def scan_stage(nc, K, name, hgrn, rows, norm_w, state_in, state_prompt, state_sample, mix):
    VC = 1 if hgrn else 2
    V = VC * P
    C = SEQ // P
    L = len(LEVELS) + 1
    LS = 4
    JS = NB * V // 512
    r_q, r_k, r_v, r_g, r_f = rows
    with Stage(nc, name) as s:
        f_raw = s.sb("f_raw", [P, T])
        q, k = s.sb("q", [P, 2, T]), s.sb("k", [P, 2, T])
        v, gate = s.sb("v", [P, VC, T]), s.sb("gate", [P, VC, T])
        soft, logf, b = s.sb("soft", [P, T]), s.sb("logf", [P, T]), s.sb("b", [P, T])
        expb = s.sb("expb", [P, T])
        q_dec = s.sb("q_dec", [P, 2, T])
        last_dec = s.sb("last_dec", [P, 2, C + NB])
        k_tok, v_tok = s.sb("k_tok", [P, 2, C + 1, P]), s.sb("v_tok", [P, 2, C + 1, V])
        dec, x = s.sb("dec", [P, 2, T]), s.sb("x", [P, 2, T])
        a = s.sb("a", [P, C + 1, P])
        state, s0 = s.sb("state", [P, C, V]), s.sb("s0", [P, NB, V])
        v_own = s.sb("v_own", [NS, NB, V])
        o, sq, rstd = s.sb("o", [P, VC, T]), s.sb("sq", [P, VC, T]), s.sb("rstd", [P, T])
        levels, starts, own = s.sb("levels", [P, L, P], I32), s.sb("starts", [P, T]), s.sb("own", [NS, NB])
        w_norm = s.sb("w_norm", [P, VC])
        lb = s.sb("lb", [P, 5, HEADS]) if hgrn else None
        lbh = s.sb("lbh", [P, 2, 2]) if hgrn else None
        S = [s.ps(f"S{i}", [P, 4, P]) for i in range(4)]
        TB = [s.ps(f"TB{i}", [P, 4, P]) for i in range(2)]
        SS, U = s.ps("SS", [P, 512]), s.ps("U", [P, 512])
        mean = [TB[0][:].rearrange("p c t -> p (c t)"), U, SS]
        const_in, norm_in, f_in, v_in, gate_in, s0_in = (s.sem(n) for n in (
            "const_in", "norm_in", "f_in", "v_in", "gate_in", "s0_in"))
        qk_in = [s.sem("qk_in0"), s.sem("qk_in1")]
        passed = s.sem("passed")
        stores_done = s.sem("stores_done")
        stored, lb_made, cleared = s.sem("stored"), s.sem("lb_made"), s.sem("cleared")
        QK = 16 if hgrn else 32
        GROUPS = 3
        TURNS = GROUPS * (1 + VC)
        per = dict(abs_out=1, e_out=1, soft_out=1, log_sig=1, neg_made=1, k_exp=1, f_exp=1, f_mixed=1, f_clamped=1,
                   log_out=1, clamped=1, b_made=1, q_silu=1, q_ready=1, k_ready=1, expb_out=1, q_dec_made=1,
                   k_diff=1, k_decay=1, k_dec_made=1, turned=TURNS, tok_out=TURNS,
                   diffed=7, decayed=7, x_made=7, scored=L, a_out=L,
                   u_made=C, s_made=C, valued=3, o_out=3, own_made=1, us_made=JS, us_out=JS,
                   mean_in=NC, mean_out=NC, rstd_out=1, gate_silu=1, normed=VC, final=VC)
        sem = {n: s.sem(n) for n in per}
        block = s.block()

        def wait(eng, n, h, count):
            eng.wait_ge(sem[n], h[0] * (2 * per[n]) + (h[1] * per[n] + per[n] + count))

        def wait_before(eng, n, h, count=None):
            count = per[n] if count is None else count
            eng.wait_ge(sem[n], h[0] * (2 * per[n]) + (h[1] * per[n] + count))

        def credit(eng, names):
            for n in names.split():
                eng.sem_inc(sem[n], per[n])

        def loads(eng, sm, h, of_head):
            eng.wait_ge(sm, h[0] * (2 * of_head) + (h[1] + 1) * of_head)

        def qk_loaded(eng, h):
            eng.wait_ge(qk_in[h[1]], h[0] * QK + QK)

        def row(base, h, width=P):
            return bass.ds(h[0] * (2 * width) + (base + h[1] * width), width)

        def half(ap, m, second):
            n = ap.shape[-1]
            return ap.rearrange("p (n m) -> p n m", m=2 * m)[:, :, m:2 * m] if second else \
                ap.rearrange("p (n m) -> p n m", m=2 * m)[:, :, 0:m]

        def width(li):
            return T if li < LS else SEQ

        @block.sync
        def _(sp):
            sp.dma_start(levels[:], K.c_levels).then_inc(const_in, 16)
            sp.dma_start(starts[:], K.c_starts).then_inc(const_in, 16)
            sp.dma_start(own[:], K.c_own).then_inc(const_in, 16)
            sp.sem_inc(stores_done, 1)

            def load_head(h, first=False):
                if not first:
                    wait_before(sp, "neg_made" if hgrn else "log_sig", h)
                sp.dma_start(f_raw[:], K.z[row(r_f, h), :]).then_inc(f_in, 16)
                if not first:
                    wait_before(sp, "turned", h)
                    sp.wait_ge(sem["a_out"], h[0] * (2 * L) + h[1] * L)
                    sp.wait_ge(sem["k_dec_made"], h[0] * 2 + h[1])
                sp.dma_start(q[:, h[1], :], K.z[row(r_q, h), :]).then_inc(qk_in[h[1]], 16)
                if not hgrn:
                    sp.dma_start(k[:, h[1], :], K.z[row(r_k, h), :]).then_inc(qk_in[h[1]], 16)
                sp.dma_start(v[:], K.z[row(r_v, h, V), :].rearrange("(c p) t -> p c t", p=P)).then_inc(v_in, 16)

            def load_tail(h, first=False):
                if not first:
                    wait_before(sp, "final", h)
                    sp.wait_ge(stored, h[0] * 96 + h[1] * 48)
                    sp.sem_inc(stores_done, 1)
                sp.dma_start(gate[:], K.z[row(r_g, h, V), :].rearrange("(c p) t -> p c t", p=P)).then_inc(gate_in, 16)
                sp.dma_start(s0[:], state_in[:, row(0, h, 1), :, :].rearrange("b a k v -> k (b a) v")).then_inc(s0_in, 16)

            def store(h):
                wait(sp, "s_made", h, C)
                sp.dma_start(state_prompt[row(0, h, 1), :, :].rearrange("a k v -> (a k) v"),
                             state[:, C - 1, :]).then_inc(stored, 16)
                wait(sp, "us_out", h, JS)
                sp.dma_start(state_sample[:, row(0, h, 1), :, :].rearrange("b a k v -> k (b a) v"), s0[:]
                             ).then_inc(stored, 16)
                wait(sp, "final", h, VC)
                sp.dma_start(mix[row(0, h, V), :].rearrange("(c p) t -> p c t", p=P), o[:]).then_inc(stored, 16)

            load_head((0, 0), True)
            load_tail((0, 0), True)
            load_head((0, 1))
            store((0, 0))
            load_tail((0, 1))
            with sp.Fori(1, HEADS // 2) as i:
                load_head((i, 0))
                store((i - 1, 1))
                load_tail((i, 0))
                load_head((i, 1))
                store((i, 0))
                load_tail((i, 1))
            store((HEADS // 2 - 1, 1))
            sp.wait_ge(stored, 48 * HEADS)

        @block.gpsimd
        def _(pool):
            credit(pool, "q_ready diffed own_made")
            with nc.allow_non_contiguous_dma(reason="norm weights and lower bounds, once"):
                pool.dma_start(w_norm[:], norm_w.rearrange("(c p) -> p c", p=P)).then_inc(norm_in, 16)
                if hgrn:
                    pool.dma_start(lb[:, 0, :], K.lower_bounds[0].rearrange("(h p) -> p h", p=P)).then_inc(norm_in, 16)
            pool.memset(a[:], 0.0).then_inc(cleared, 1)
            pool.wait_ge(const_in, 48)

            def prepare(h):
                y = h[1]
                if hgrn:
                    wait(pool, "q_silu", h, 1)
                else:
                    qk_loaded(pool, h)
                pool.sem_inc(passed, 1)
                pool.tensor_scalar(q[:, y, :], q[:, y, :], P ** -0.5, None, ALU.mult).then_inc(sem["q_ready"], 1)

            def differences(h):
                wait(pool, "b_made", h, 1)
                for n, m in enumerate(LEVELS):
                    w = width(n + 1)
                    blocks = b[:, 0:w].rearrange("p (n m) -> p n m", m=2 * m)
                    wait(pool, "x_made", h, max(n - 1, 0))
                    pool.tensor_tensor(dec[:, n % 2, 0:w].rearrange("p (n m) -> p n m", m=2 * m), blocks,
                                       blocks[:, :, m - 1:m].broadcast_to([P, w // (2 * m), 2 * m]),
                                       ALU.subtract).then_inc(sem["diffed"], 1)

            def tail(h):
                wait(pool, "tok_out", h, TURNS)
                wait_before(pool, "us_made", h)
                pool.tensor_tensor(v_own[:], v_tok[0:NS, h[1], C:C + 1, :].broadcast_to([NS, NB, V]),
                                   own[:].unsqueeze(2).broadcast_to([NS, NB, V]), ALU.mult).then_inc(sem["own_made"], 1)

            with pool.Fori(0, HEADS // 2) as i:
                prepare((i, 0))
                differences((i, 0))
                prepare((i, 1))
                tail((i, 0))
                differences((i, 1))
                tail((i, 1))

        @block.scalar
        def _(act):
            credit(act, "abs_out e_out soft_out k_exp f_exp log_out q_silu expb_out k_decay tok_out decayed o_out "
                        "mean_out rstd_out gate_silu")

            if hgrn:
                act.wait_ge(lb_made, 1)
                act.activation(lb[:, 2, :], lb[:, 1, :], ACT.Exp).then_inc(lb_made, 1)

            def prepare(h):
                y = h[1]
                loads(act, f_in, h, 16)
                wait_before(act, "turned", h)
                act.activation(soft[:], f_raw[:], ACT.Abs).then_inc(sem["abs_out"], 1)
                wait(act, "abs_out", h, 1)
                act.activation(soft[:], soft[:], ACT.Exp, scale=-1.0).then_inc(sem["e_out"], 1)
                wait(act, "e_out", h, 1)
                act.activation(soft[:], soft[:], ACT.Ln, bias=1.0).then_inc(sem["soft_out"], 1)
                if hgrn:
                    wait(act, "log_sig", h, 1)
                    act.activation(logf[:], logf[:], ACT.Exp).then_inc(sem["f_exp"], 1)
                    wait(act, "neg_made", h, 1)
                    act.activation(k[:, y, :], k[:, y, :], ACT.Exp, scale=-1.0).then_inc(sem["k_exp"], 1)
                    wait(act, "f_clamped", h, 1)
                    act.activation(logf[:], logf[:], ACT.Ln).then_inc(sem["log_out"], 1)
                    qk_loaded(act, h)
                    act.activation(q[:, y, :], q[:, y, :], ACT.Silu).then_inc(sem["q_silu"], 1)
                wait(act, "b_made", h, 1)
                wait_before(act, "k_dec_made", h)
                act.activation(expb[:], b[:], ACT.Exp).then_inc(sem["expb_out"], 1)
                wait(act, "k_diff", h, 1)
                act.activation(soft[:], soft[:], ACT.Exp).then_inc(sem["k_decay"], 1)
                n = 0
                for tok, cs in ((k_tok, 1), (v_tok, VC)):
                    for c in range(cs):
                        for g in range(GROUPS):
                            wait(act, "turned", h, n + 1)
                            if g < GROUPS - 1:
                                act.activation(tok[:, y, 4 * g:4 * g + 4, c * P:(c + 1) * P], TB[n % 2][:],
                                               ACT.Copy).then_inc(sem["tok_out"], 1)
                            else:
                                act.activation(tok[0:NS, y, C, c * P:(c + 1) * P], TB[n % 2][0:NS, 0, :],
                                               ACT.Copy).then_inc(sem["tok_out"], 1)
                            n += 1

            def decays(h):
                for n, m in enumerate(LEVELS):
                    d = dec[:, n % 2, 0:width(n + 1)]
                    wait(act, "diffed", h, n + 1)
                    act.activation(half(d, m, False), half(d, m, False), ACT.Exp, scale=-1.0)
                    act.activation(half(d, m, True), half(d, m, True), ACT.Exp).then_inc(sem["decayed"], 1)

            def tail(h):
                loads(act, gate_in, h, 16)
                act.activation(gate[:], gate[:], ACT.Silu).then_inc(sem["gate_silu"], 1)
                act.wait_ge(stores_done, h[0] * 2 + (h[1] + 1))
                for g in range(3):
                    wait(act, "valued", h, g + 1)
                    for c in range(VC):
                        src = S[2 * c + g][:].rearrange("p c t -> p (c t)") if g < 2 else SS[:, c * NS:(c + 1) * NS]
                        t0, tn = g * 512, (512 if g < 2 else NS)
                        act.activation(o[:, c, t0:t0 + tn], src, ACT.Copy)
                        last = act.activation(sq[:, c, t0:t0 + tn], src, ACT.Square)
                    last.then_inc(sem["o_out"], 1)
                wait_before(act, "normed", h)
                for c, (t0, tn) in enumerate(CHUNKS):
                    wait(act, "mean_in", h, c + 1)
                    act.activation(rstd[:, t0:t0 + tn], mean[c][:, 0:tn], ACT.Ln, scale=1.0 / V,
                                   bias=K.eps[:, 0:1]).then_inc(sem["mean_out"], 1)
                wait(act, "mean_out", h, NC)
                act.activation(rstd[:], rstd[:], ACT.Exp, scale=-0.5).then_inc(sem["rstd_out"], 1)

            with act.Fori(0, HEADS // 2) as i:
                prepare((i, 0))
                decays((i, 0))
                prepare((i, 1))
                tail((i, 0))
                decays((i, 1))
                tail((i, 1))

        @block.vector
        def _(dve):
            credit(dve, "log_sig neg_made f_mixed f_clamped clamped b_made k_ready q_dec_made k_diff k_dec_made "
                        "x_made a_out s_made us_out normed final")
            dve.wait_ge(const_in, 48)
            dve.wait_ge(norm_in, 32 if hgrn else 16)
            dve.wait_ge(cleared, 1)
            if hgrn:
                top, e, pr = lb[:, 1, :], lb[:, 2, :], lb[:, 2, :]
                dve.tensor_tensor(top, lb[:, 0, :], lb[:, 0, :], ALU.subtract).then_inc(lb_made, 1)
                dve.wait_ge(lb_made, 2)
                dve.reciprocal(lb[:, 0, :], e).then_inc(lb_made, 1)
                dve.wait_ge(lb_made, 3)
                dve.tensor_tensor(lb[:, 1, :], e, lb[:, 0, :], ALU.mult).then_inc(lb_made, 1)
                dve.wait_ge(lb_made, 4)
                dve.tensor_tensor(lb[:, 3, :], lb[:, 1, :], lb[:, 1, :], ALU.subtract).then_inc(lb_made, 1)
                dve.wait_ge(lb_made, 5)
                dve.tensor_scalar(lb[:, 4, :], lb[:, 3, :], -1.0, 1.0, ALU.mult, ALU.add).then_inc(lb_made, 1)
                dve.wait_ge(lb_made, 6)

            def prepare(h):
                y = h[1]
                wait(dve, "soft_out", h, 1)
                dve.scalar_tensor_tensor(out=logf[:], in0=f_raw[:], scalar=0.0, in1=soft[:], op0=ALU.min,
                                         op1=ALU.subtract).then_inc(sem["log_sig"], 1)
                if hgrn:
                    dve.scalar_tensor_tensor(out=k[:, y, :], in0=f_raw[:], scalar=0.0, in1=soft[:], op0=ALU.max,
                                             op1=ALU.add).then_inc(sem["neg_made"], 1)
                    dve.tensor_copy(lbh[:, y, :], lb[:, 3:5, row(0, h, 1)].rearrange("p c a -> p (c a)")
                                    ).then_inc(lb_made, 1)
                    dve.wait_ge(lb_made, h[0] * 2 + (h[1] + 7))
                    wait(dve, "f_exp", h, 1)
                    dve.tensor_scalar(logf[:], logf[:], lbh[:, y, 1:2], lbh[:, y, 0:1], ALU.mult, ALU.add
                                      ).then_inc(sem["f_mixed"], 1)
                    wait(dve, "f_mixed", h, 1)
                    dve.tensor_scalar(logf[:], logf[:], TINY, None, ALU.max).then_inc(sem["f_clamped"], 1)
                    wait(dve, "k_exp", h, 1)
                    dve.tensor_scalar(k[:, y, :], k[:, y, :], lbh[:, y, 1:2], None, ALU.mult).then_inc(sem["k_ready"], 1)
                    wait(dve, "log_out", h, 1)
                    dve.tensor_scalar(logf[:], logf[:], 0.0, None, ALU.min).then_inc(sem["clamped"], 1)
                else:
                    wait(dve, "log_sig", h, 1)
                    dve.tensor_scalar(logf[:], logf[:], 1.0 / GATE_TAU, 0.0, ALU.mult, ALU.min
                                      ).then_inc(sem["clamped"], 1)
                wait(dve, "clamped", h, 1)
                dve.tensor_tensor_scan(b[:], starts[:], logf[:], 0.0, ALU.mult, ALU.add).then_inc(sem["b_made"], 1)
                wait(dve, "b_made", h, 1)
                for t0, t1, m in ((0, SEQ, P), (SEQ, T, TS)):
                    bl = b[:, t0:t1].rearrange("p (n m) -> p n m", m=m)
                    last = dve.tensor_tensor(soft[:, t0:t1].rearrange("p (n m) -> p n m", m=m),
                                             bl[:, :, m - 1:m].broadcast_to([P, (t1 - t0) // m, m]), bl, ALU.subtract)
                last.then_inc(sem["k_diff"], 1)
                wait(dve, "expb_out", h, 1)
                wait(dve, "q_ready", h, 1)
                dve.tensor_tensor(q_dec[:, y, :], q[:, y, :], expb[:], ALU.mult).then_inc(sem["q_dec_made"], 1)
                dve.tensor_copy(last_dec[:, y, 0:C], expb[:, P - 1:SEQ:P])
                dve.tensor_copy(last_dec[:, y, C:C + NB], expb[:, SEQ + TS - 1:T:TS])
                wait(dve, "k_decay", h, 1)
                if hgrn:
                    wait(dve, "k_ready", h, 1)
                else:
                    qk_loaded(dve, h)
                dve.tensor_tensor(soft[:], k[:, y, :], soft[:], ALU.mult).then_inc(sem["k_dec_made"], 1)

            def scores(h):
                y = h[1]

                def scale(n):
                    m, w, z = LEVELS[n], width(n + 1), n % 2
                    wait(dve, "decayed", h, n + 1)
                    if n >= 2:
                        wait(dve, "scored", h, n)
                    dve.tensor_tensor(half(x[:, z, 0:w], m, False), half(dec[:, z, 0:w], m, False),
                                      half(k[:, y, 0:w], m, False), ALU.mult)
                    dve.tensor_tensor(half(x[:, z, 0:w], m, True), half(dec[:, z, 0:w], m, True),
                                      half(q[:, y, 0:w], m, True), ALU.mult).then_inc(sem["x_made"], 1)

                def keep(li):
                    wait(dve, "scored", h, li + 1)
                    if li:
                        wait(dve, "a_out", h, li)
                    dve.sem_inc(passed, 1)
                    for g in range(2):
                        last = dve.copy_predicated(a[:, 4 * g:4 * g + 4, :],
                                                   levels[:, li:li + 1, :].broadcast_to([P, 4, P]), S[2 * (li % 2) + g][:])
                    if li < LS:
                        last = dve.copy_predicated(a[0:NS, C, 0:NS], levels[0:NS, li, 0:NS],
                                                   (SS, U)[li % 2][0:NS, 0:NS])
                    last.then_inc(sem["a_out"], 1)

                wait_before(dve, "valued", h)
                for n in range(7):
                    scale(n)
                    keep(n)
                keep(7)

            def tail(h):
                y = h[1]
                for c in range(C):
                    wait(dve, "u_made", h, c + 1)
                    u = U[:, 0:V]
                    if c == 0:
                        dve.wait_ge(stores_done, h[0] * 2 + (h[1] + 1))
                        dve.tensor_copy(state[:, 0, :], u).then_inc(sem["s_made"], 1)
                    else:
                        wait(dve, "s_made", h, c)
                        dve.scalar_tensor_tensor(out=state[:, c, :], in0=state[:, c - 1, :], scalar=last_dec[:, y, c:c + 1],
                                                 in1=u, op0=ALU.mult, op1=ALU.add).then_inc(sem["s_made"], 1)
                wait(dve, "valued", h, 3)
                for j in range(JS):
                    wait(dve, "us_made", h, j + 1)
                    for n in range(512 // V):
                        bi = j * (512 // V) + n
                        last = dve.scalar_tensor_tensor(out=s0[:, bi, :], in0=s0[:, bi, :],
                                                        scalar=last_dec[:, y, C + bi:C + bi + 1],
                                                        in1=U[:, n * V:(n + 1) * V], op0=ALU.mult, op1=ALU.add)
                    last.then_inc(sem["us_out"], 1)
                wait(dve, "rstd_out", h, 1)
                wait(dve, "o_out", h, 3)
                for c in range(VC):
                    dve.scalar_tensor_tensor(out=o[:, c, :], in0=o[:, c, :], scalar=w_norm[:, c:c + 1], in1=rstd[:],
                                             op0=ALU.mult, op1=ALU.mult).then_inc(sem["normed"], 1)
                wait(dve, "gate_silu", h, 1)
                for c in range(VC):
                    wait(dve, "normed", h, c + 1)
                    dve.tensor_tensor(o[:, c, :], o[:, c, :], gate[:, c, :], ALU.mult).then_inc(sem["final"], 1)

            with dve.Fori(0, HEADS // 2) as i:
                prepare((i, 0))
                scores((i, 0))
                prepare((i, 1))
                tail((i, 0))
                scores((i, 1))
                tail((i, 1))

        @block.tensor
        def _(pe):
            credit(pe, "turned scored u_made valued us_made mean_in")

            def prepare(h):
                y, n = h[1], 0
                wait_before(pe, "mean_out", (h[0], 0))
                for src, cs in ((None, 1), (v, VC)):
                    for c in range(cs):
                        x_f = soft[:] if src is None else v[:, c, :]
                        for g in range(GROUPS):
                            if n == 0:
                                wait(pe, "k_dec_made", h, 1)
                            if n == GROUPS:
                                loads(pe, v_in, h, 16)
                            if n < 2:
                                wait_before(pe, "tok_out", h)
                            else:
                                wait(pe, "tok_out", h, n - 1)
                            pe.sem_inc(passed, 1)
                            for i in range(4 if g < GROUPS - 1 else 1):
                                t0 = (4 * g + i) * P
                                tn = min(P, T - t0)
                                last = pe.transpose(TB[n % 2][0:tn, i, :], x_f[:, t0:t0 + tn], K.ident[:])
                            last.then_inc(sem["turned"], 1)
                            n += 1

            def scores(h):
                y = h[1]
                for li in range(L):
                    if li == 0:
                        if hgrn:
                            wait(pe, "k_ready", h, 1)
                        else:
                            qk_loaded(pe, h)
                        wait(pe, "q_ready", h, 1)
                        first, second = k[:, y, :], q[:, y, :]
                        wait_before(pe, "o_out", h)
                        wait_before(pe, "mean_out", h)
                    else:
                        wait(pe, "x_made", h, li)
                        first = second = x[:, (li - 1) % 2, :]
                        if li >= 2:
                            wait(pe, "a_out", h, li - 1)
                    for c in range(C):
                        t = slice(c * P, (c + 1) * P)
                        last = pe.matmul(S[2 * (li % 2) + c // 4][:, c % 4, :], first[:, t], second[:, t],
                                         start=True, stop=True)
                    if li < LS:
                        last = pe.matmul((SS, U)[li % 2][0:NS, 0:NS], first[:, SEQ:T], second[:, SEQ:T],
                                         start=True, stop=True)
                    last.then_inc(sem["scored"], 1)

            def tail(h):
                y = h[1]
                wait(pe, "tok_out", h, TURNS)
                wait(pe, "a_out", h, L)
                wait(pe, "q_dec_made", h, 1)
                wait_before(pe, "us_out", h)
                wait_before(pe, "mean_out", h)
                loads(pe, s0_in, h, 16)
                for c in range(C):
                    for vc in range(VC):
                        last = pe.matmul(S[2 * vc + c // 4][:, c % 4, :], v_tok[:, y, c, vc * P:(vc + 1) * P], a[:, c, :],
                                         start=True, stop=(c == 0))
                    if c:
                        wait(pe, "s_made", h, c)
                    pe.matmul(U[:, 0:V], k_tok[:, y, c, :], v_tok[:, y, c, :], start=True, stop=True
                              ).then_inc(sem["u_made"], 1)
                    for vc in range(VC if c else 0):
                        last = pe.matmul(S[2 * vc + c // 4][:, c % 4, :], state[:, c - 1, vc * P:(vc + 1) * P],
                                         q_dec[:, y, c * P:(c + 1) * P], start=False, stop=True)
                    if c % 4 == 3:
                        last.then_inc(sem["valued"], 1)
                for vc in range(VC):
                    out = SS[:, vc * NS:(vc + 1) * NS]
                    pe.matmul(out, v_tok[0:NS, y, C, vc * P:(vc + 1) * P], a[0:NS, C, 0:NS], start=True, stop=False)
                    for bi in range(NB):
                        t = slice(bi * TS, (bi + 1) * TS)
                        last = pe.matmul(out[:, t], s0[:, bi, vc * P:(vc + 1) * P],
                                         q_dec[:, y, SEQ + bi * TS:SEQ + (bi + 1) * TS], start=False,
                                         stop=(bi == NB - 1))
                last.then_inc(sem["valued"], 1)
                wait(pe, "own_made", h, 1)
                for j in range(JS):
                    if j == 0:
                        wait(pe, "s_made", h, C)
                    else:
                        wait(pe, "us_out", h, j)
                    n = 512 // V
                    pe.matmul(U[:], k_tok[0:NS, y, C, :], v_own[:, j * n:(j + 1) * n, :].rearrange("p b v -> p (b v)"),
                              start=True, stop=True).then_inc(sem["us_made"], 1)
                wait(pe, "o_out", h, 3)
                for c, (t0, tn) in enumerate(CHUNKS):
                    if c == 1:
                        wait(pe, "us_out", h, JS)
                    if c == 0 and y == 0:
                        wait(pe, "tok_out", (h[0], 1), TURNS)
                    for vc in range(VC):
                        last = pe.matmul(mean[c][:, 0:tn], K.ones[:], sq[:, vc, t0:t0 + tn], start=(vc == 0),
                                         stop=(vc == VC - 1))
                    last.then_inc(sem["mean_in"], 1)

            with pe.Fori(0, HEADS // 2) as i:
                prepare((i, 0))
                scores((i, 0))
                prepare((i, 1))
                tail((i, 0))
                scores((i, 1))
                tail((i, 1))


def latent_attention(nc, K):
    with ExitStack() as stack:
        M = Kit()

        def keep(name, shape, dt=F32):
            return stack.enter_context(nc.sbuf_tensor(name, shape, dt))

        M.qn, M.qpe = keep("mla_qn", [P, HEADS, T]), keep("mla_qpe", [P, 2, T])
        M.ckv, M.kpe = keep("mla_ckv", [P, 2, T]), keep("mla_kpe", [P, T])
        latent_stage(nc, K, M)
        M.kn, M.v = keep("mla_kn", [P, HEADS, SEQ]), keep("mla_v", [P, 8, HEADS * P])
        M.wuv, M.rows = keep("mla_wuv", [P, 2, HEADS, P]), keep("mla_rows", [P, 9, LAT])
        M.qs = keep("mla_qs", [P, 3, NB, HEADS, TS])
        keys_stage(nc, K, M)
        prompt_attention_stage(nc, K, M)
        sample_attention_stage(nc, K, M)



def program(nc, K):
    with ExitStack() as stack:
        def keep(name, shape, dt=F32):
            return stack.enter_context(nc.sbuf_tensor(name, shape, dt))

        K.xT = keep("xT", [P, KD, T])
        K.ident, K.ones = keep("ident", [P, P]), keep("ones", [P, P])
        K.norms, K.eps = keep("norms", [P, 5, KD]), keep("eps", [P, 1])
        load_stage(nc, K)
        project_stage(nc, K, "even", K.w_in_even[0], EVEN_COLS, norm=0, z=K.z)
        latent_attention(nc, K)
        scan_stage(nc, K, "hgrn", True, (Z_Q, None, Z_I, Z_G, Z_F), K.hgrn_norm[0], K.state_hgrn[0],
                   K.hgrn_prompt, K.hgrn_sample, K.mix)
        project_stage(nc, K, "evenout", K.w_out_even[0], D, mix=K.mix)
        mlp_stage(nc, K, "mlp0", 1, K.w_up[0], K.w_down[0])
        project_stage(nc, K, "odd", K.w_in_odd[0], ODD_COLS, norm=2, z=K.z)
        alpha_stage(nc, K)
        scan_stage(nc, K, "gla", False, (G_Q, G_K, G_V, G_R, G_GATE), K.gla_norm[0], K.state_gla[0],
                   K.gla_prompt, K.gla_sample, K.mix)
        project_stage(nc, K, "oddout", K.w_out_odd[0], D, mix=K.mix)
        mlp_stage(nc, K, "mlp1", 3, K.w_up[1], K.w_down[1])
        store_stage(nc, K)



def constants():
    f = np.float32
    pos = np.concatenate([np.arange(SEQ)] + [PAGES * P + np.arange(TS)] * NB)
    inv = (ROPE_THETA ** (-np.arange(ROPE // 2) / (ROPE // 2))).astype(f)
    ang = (pos.astype(f)[None, :] * inv[:, None]).astype(np.float64)
    cos = np.tile(np.cos(ang), (4, 1)).astype(f)
    sin = np.tile(np.concatenate([-np.sin(ang), np.sin(ang)]), (2, 1)).astype(f)
    rot = np.zeros((P, P), f)
    rot[np.arange(P) ^ (ROPE // 2), np.arange(P)] = 1
    i = np.arange(P)
    s, t = i[:, None], i[None, :]
    causal = np.where(t <= s, 0, NEG).astype(f)
    tok, row = np.arange(NS), np.arange(HEADS * TS)
    seen = ((tok[None, None, :] // TS == np.arange(NB)[None, :, None])
            & (tok[None, None, :] % TS <= (row % TS)[:, None, None]))
    pairs = [s == t] + [(s // (2 * m) == t // (2 * m)) & (s % (2 * m) < m) & (t % (2 * m) >= m) for m in LEVELS]
    starts = np.ones((P, T), f)
    starts[:, 0:SEQ:P] = 0
    starts[:, SEQ::TS] = 0
    return dict(c_ident=np.eye(P, dtype=f), c_cos=cos, c_sin=sin, c_rot=rot, c_causal=causal,
                c_newmask=np.where(seen, 0, NEG).astype(f), c_levels=np.stack(pairs, 1).astype(np.int32),
                c_starts=starts, c_own=(tok[:, None] // TS == np.arange(NB)[None, :]).astype(f))


OUTPUTS = dict(y_prompt=(1, SEQ, D), y_sample=(NB, TS, D), mla_rows_prompt=(1, 1, SEQ, LAT),
               mla_rows_sample=(1, NB, TS, LAT), hgrn_state_prompt=(1, 1, HEADS, P, P),
               hgrn_state_sample=(1, NB, HEADS, P, P), gla_state_prompt=(1, 1, HEADS, P, 2 * P),
               gla_state_sample=(1, NB, HEADS, P, 2 * P))


def bind(nc, a, o):
    K = Kit()
    K.x_prompt, K.x_sample = a["x_prompt"][0], a["x_sample"].rearrange("b t d -> (b t) d")
    K.cache, K.page_table = a["cache_mla"][0], a["page_table"].rearrange("(a b) p -> a (b p)", a=1)
    K.state_hgrn, K.state_gla = a["state_hgrn"], a["state_gla"]
    K.norm_mix, K.norm_mlp, K.norm_final = a["norm_mix"], a["norm_mlp"], a["norm_final"]
    K.w_in_even, K.w_out_even, K.w_in_odd, K.w_out_odd = a["w_in_even"], a["w_out_even"], a["w_in_odd"], a["w_out_odd"]
    K.w_up, K.w_down, K.w_uq, K.w_uk, K.w_uv = a["w_up"], a["w_down"], a["w_uq"], a["w_uk"], a["w_uv"]
    K.q_norm, K.kv_norm, K.hgrn_norm, K.gla_norm = a["q_norm"], a["kv_norm"], a["hgrn_norm"], a["gla_norm"]
    K.lower_bounds, K.w_alpha2, K.b_alpha = a["lower_bounds"], a["w_alpha2"], a["b_alpha"]
    K.c_ident, K.c_cos, K.c_sin, K.c_rot, K.c_causal = a["c_ident"], a["c_cos"], a["c_sin"], a["c_rot"], a["c_causal"]
    K.c_newmask, K.c_levels, K.c_starts, K.c_own = a["c_newmask"], a["c_levels"], a["c_starts"], a["c_own"]
    K.z = nc.dram_tensor("projections", [Z_ROWS, T], F32, kind="Internal").ap()
    K.mix = nc.dram_tensor("mixed", [D, T], F32, kind="Internal").ap()
    K.y_prompt, K.y_sample = o["y_prompt"][0], o["y_sample"].rearrange("b t d -> (b t) d")
    K.rows_prompt = o["mla_rows_prompt"][0, 0]
    K.rows_sample = o["mla_rows_sample"][0].rearrange("b t c -> (b t) c")
    K.hgrn_prompt, K.hgrn_sample = o["hgrn_state_prompt"][0, 0], o["hgrn_state_sample"][0]
    K.gla_prompt, K.gla_sample = o["gla_state_prompt"][0, 0], o["gla_state_sample"][0]
    return K


def kernel(**inputs):
    import concourse.bacc as bacc
    from concourse.bass_utils import run_bass_kernel_spmd

    nc = bacc.Bacc("TRN2", target_bir_lowering=False, num_devices=1)
    arrays = {f"in_{n}": np.ascontiguousarray(x) for n, x in {**inputs, **constants()}.items()}
    a = {n[3:]: nc.dram_tensor(n, x.shape, mybir.dt.from_np(x.dtype), kind="ExternalInput").ap()
         for n, x in arrays.items()}
    o = {n: nc.dram_tensor(f"out_{n}", shape, F32, kind="ExternalOutput").ap() for n, shape in OUTPUTS.items()}
    program(nc, bind(nc, a, o))
    result = run_bass_kernel_spmd(nc, [arrays], core_ids=[0]).results[0]
    return tuple(result[f"out_{n}"] for n in OUTPUTS)
```

```python
from collections import namedtuple
from contextlib import ExitStack

import numpy as np

import concourse.bass as bass
from concourse import mybir

F32 = mybir.dt.float32
F32R = mybir.dt.float32r
I32 = mybir.dt.int32
ACT = mybir.ActivationFunctionType
ALU = mybir.AluOpType
AX = mybir.AxisListType

P = 128
D = 1024
KD = D // P
SEQ = 1024
NB, TS = 8, 8
NS = NB * TS
T = SEQ + NS
HEADS = 4
CHUNKS = [(0, 384), (384, 352), (736, 352)]
NC = len(CHUNKS)
FF = 4096
EVEN_COLS = 2752
ODD_COLS = 3088
Q_LORA, KV_LORA, ROPE = 384, 256, 64
LAT = KV_LORA + ROPE
PAGES = 64
PG = 4
SCALE = (128 + ROPE) ** -0.5
ROPE_THETA = 10000.0
NEG = -1e30
EPS = 1e-6
TINY = 1e-30
GATE_RANK, GATE_TAU = 16, 16.0
LEVELS = [1, 2, 4, 8, 16, 32, 64]

Z_Q, Z_F, Z_I, Z_G, Z_CQ, Z_CKV, Z_KR = 0, 512, 1024, 1536, 2048, 2432, 2688
G_Q, G_K, G_V, G_R, G_A, G_GATE = 0, 512, 1024, 2048, 3072, 3088
Z_ROWS = 3600


class Kit:
    pass


class Stage:

    def __init__(self, nc, name):
        self.nc, self.name, self.stack, self.sems = nc, name, ExitStack(), []

    def __enter__(self):
        return self

    def __exit__(self, *a):
        self.stack.__exit__(*a)
        self.nc.clear_and_free_semaphores(self.sems)
        self.nc.all_engine_barrier()

    def sb(self, name, shape, dt=F32):
        return self.stack.enter_context(self.nc.sbuf_tensor(f"{self.name}_{name}", shape, dt))

    def ps(self, name, shape, dt=F32):
        return self.stack.enter_context(self.nc.psum_tensor(f"{self.name}_{name}", shape, dt))

    def sem(self, name):
        self.sems.append(self.nc.alloc_semaphore(f"{self.name}_{name}"))
        return self.sems[-1]

    def block(self):
        return self.stack.enter_context(self.nc.Block())


def r32(ap):
    return ap.bitcast(F32)


def mm3(pe, out, w_hi, w_lo, x_hi, x_lo, first, last):
    pe.matmul(out, w_hi, x_hi, start=first, stop=False)
    pe.matmul(out, w_hi, x_lo, start=False, stop=False)
    return pe.matmul(out, w_lo, x_hi, start=False, stop=last)


def wait_apart(eng, sem, value, spare):
    eng.wait_ge(sem, value)
    eng.sem_inc(spare, 1)



def load_stage(nc, K):
    with Stage(nc, "load") as s:
        xin = s.sb("xin", [P, 2, D])
        tp = [s.ps(f"tp{i}", [P, 4, P]) for i in range(4)]
        const_in, ident_in, xin_in = s.sem("const_in"), s.sem("ident_in"), [s.sem("xin_in0"), s.sem("xin_in1")]
        xin_used, turned = s.sem("xin_used"), s.sem("turned")
        copied_lo, copied_hi = s.sem("copied_lo"), s.sem("copied_hi")
        block = s.block()
        xp, xs = K.x_prompt, K.x_sample

        @block.sync
        def _(sp):
            sp.dma_start(K.ident[:], K.c_ident).then_inc(ident_in, 16)
            for i in range(2):
                sp.dma_start(xin[:, i, :], xp[i * P:(i + 1) * P, :]).then_inc(xin_in[i], 16)
            with sp.Fori(1, 4) as j:
                for i in range(2):
                    sp.wait_ge(xin_used, 2 * j + (i - 1))
                    sp.dma_start(xin[:, i, :], xp[bass.ds(j * 2 * P + i * P, P), :]).then_inc(xin_in[i], 16)
            sp.wait_ge(xin_used, 7)
            sp.dma_start(xin[0:NS, 0, :], xs).then_inc(xin_in[0], 16)

        @block.gpsimd
        def _(pool):
            pool.memset(K.ones[:], 1.0)
            pool.memset(K.eps[:], EPS)
            with nc.allow_non_contiguous_dma(reason="a column of each norm weight, once"):
                for n, w in enumerate([K.norm_mix[0], K.norm_mlp[0], K.norm_mix[1], K.norm_mlp[1], K.norm_final]):
                    pool.dma_start(K.norms[:, n, :], w.rearrange("(k p) -> p k", p=P)).then_inc(const_in, 16)
            pool.wait_ge(const_in, 5 * 16)

        @block.tensor
        def _(pe):
            def turn(tile, i, rows):
                for half in range(2):
                    pe.wait_ge(copied_lo if half == 0 else copied_hi, tile + 1)
                    for k in range(4):
                        c = (4 * half + k) * P
                        last = pe.transpose(tp[2 * i + half][:, k, 0:rows], xin[0:rows, i, c:c + P],
                                            K.ident[0:rows, 0:rows])
                    last.then_inc(turned, 1)
            pe.wait_ge(ident_in, 16)
            with pe.Fori(0, 4) as j:
                for i in range(2):
                    pe.wait_ge(xin_in[i], j * 16 + 16)
                    turn(j * 2 + i, i, P)
            pe.wait_ge(xin_in[0], 5 * 16)
            turn(8, 0, NS)

        def copy_out(eng, copy, half, copied):
            eng.sem_inc(copied, 2)
            dst = K.xT[:, 4 * half:4 * half + 4, :]
            with eng.Fori(0, 4) as j:
                for i in range(2):
                    eng.wait_ge(turned, j * 4 + (2 * i + half + 1))
                    copy(dst[:, :, bass.ds(j * 2 * P + i * P, P)], tp[2 * i + half][:]).then_inc(copied, 1)
                    if half:
                        eng.sem_inc(xin_used, 1)
            eng.wait_ge(turned, 17 + half)
            copy(dst[:, :, SEQ:T], tp[half][:, :, 0:NS]).then_inc(copied, 1)

        @block.scalar
        def _(act):
            copy_out(act, lambda o, x: act.activation(o, x, ACT.Copy), 0, copied_lo)

        @block.vector
        def _(dve):
            copy_out(dve, lambda o, x: dve.tensor_copy(o, x), 1, copied_hi)


def store_stage(nc, K):
    with Stage(nc, "store") as s:
        sq = s.sb("sq", [P, 2, T])
        acc = s.sb("acc", [P, T])
        rstd = s.sb("rstd", [P, T])
        y = s.sb("y", [P, 2, D])
        psum = [s.ps(f"sum{i}", [P, 512]) for i in range(NC)]
        tp = [s.ps(f"tp{i}", [P, 4, P]) for i in range(4)]
        n = Norm(s, K, 4, sq, acc, rstd, psum)
        normed = s.sem("normed")
        turned, copied_lo, copied_hi = s.sem("turned"), s.sem("copied_lo"), s.sem("copied_hi")
        y_out = [s.sem("y_out0"), s.sem("y_out1")]
        y_free = s.sem("y_free")
        block = s.block()
        yp, ys = K.y_prompt, K.y_sample

        @block.tensor
        def _(pe):
            n.pe(pe)
            pe.wait_ge(normed, KD)

            for tile in range(9):
                rows, i = (P if tile < 8 else NS), tile % 2
                for half in range(2):
                    pe.wait_ge(copied_lo if half == 0 else copied_hi, tile + 1)
                    for k in range(4):
                        last = pe.transpose(tp[2 * i + half][0:rows, k, :],
                                            K.xT[:, 4 * half + k, tile * P:tile * P + rows], K.ident[:])
                    last.then_inc(turned, 1)

        @block.scalar
        def _(act):
            act.sem_inc(copied_lo, 2)
            n.act_squares(act)
            n.act_rstd(act)
            for tile in range(9):
                rows, i = (P if tile < 8 else NS), tile % 2
                act.wait_ge(turned, 2 * tile + 1)
                act.wait_ge(y_free, tile + 1)
                act.activation(y[0:rows, i, 0:512], tp[2 * i][0:rows], ACT.Copy).then_inc(copied_lo, 1)

        @block.vector
        def _(dve):
            dve.sem_inc(copied_hi, 2)
            n.dve_sum(dve)
            dve.wait_ge(n.rstd_ready, NC)
            for k in range(KD):
                dve.scalar_tensor_tensor(out=K.xT[:, k, :], in0=K.xT[:, k, :], scalar=K.norms[:, 4, k:k + 1],
                                         in1=rstd[:], op0=ALU.mult, op1=ALU.mult).then_inc(normed, 1)
            for tile in range(9):
                rows, i = (P if tile < 8 else NS), tile % 2
                dve.wait_ge(turned, 2 * tile + 2)
                dve.wait_ge(y_free, tile + 1)
                dve.tensor_copy(y[0:rows, i, 512:1024], tp[2 * i + 1][0:rows]).then_inc(copied_hi, 1)

        @block.sync
        def _(sp):
            sp.sem_inc(y_free, 2)
            for tile in range(9):
                rows, i = (P if tile < 8 else NS), tile % 2
                sp.wait_ge(copied_lo, tile + 3)
                sp.wait_ge(copied_hi, tile + 3)
                dst = yp[tile * P:(tile + 1) * P, :] if tile < 8 else ys
                sp.dma_start(dst, y[0:rows, i, :]).then_inc(y_out[i], 16)
                if tile:
                    sp.wait_ge(y_out[1 - i], 16 * ((tile + 1) // 2))
                    sp.sem_inc(y_free, 1)
            sp.wait_ge(y_out[0], 5 * 16)


class Norm:

    def __init__(self, s, K, which, sq, acc, rstd, psum):
        self.K, self.which, self.sq, self.acc, self.rstd, self.psum = K, which, sq, acc, rstd, psum
        self.squared, self.sq_used = s.sem("squared"), s.sem("sq_used")
        self.mean_in, self.logged, self.rstd_ready = s.sem("mean_in"), s.sem("logged"), s.sem("rstd_ready")

    def act_squares(self, act):
        act.sem_inc(self.sq_used, 2)
        for k in range(KD):
            act.wait_ge(self.sq_used, k + 1)
            act.activation(self.sq[:, k % 2, :], self.K.xT[:, k, :], ACT.Square).then_inc(self.squared, 1)

    def dve_sum(self, dve):
        for k in range(KD):
            dve.wait_ge(self.squared, k + 1)
            if k == 0:
                dve.tensor_copy(self.acc[:], self.sq[:, 0, :]).then_inc(self.sq_used, 1)
            else:
                dve.wait_ge(self.sq_used, 2 + k)
                dve.tensor_tensor(self.acc[:], self.acc[:], self.sq[:, k % 2, :], ALU.add).then_inc(self.sq_used, 1)

    def pe(self, pe):
        pe.wait_ge(self.sq_used, 2 + KD)
        for c, (t0, tn) in enumerate(CHUNKS):
            pe.matmul(self.psum[c][:, 0:tn], self.K.ones[:], self.acc[:, t0:t0 + tn],
                      start=True, stop=True).then_inc(self.mean_in, 1)

    def act_rstd(self, act):
        for c, (t0, tn) in enumerate(CHUNKS):
            act.wait_ge(self.mean_in, c + 1)
            act.activation(self.rstd[:, t0:t0 + tn], self.psum[c][:, 0:tn], ACT.Ln,
                           scale=1.0 / D, bias=self.K.eps[:, 0:1]).then_inc(self.logged, 1)
        act.wait_ge(self.logged, NC)
        for c, (t0, tn) in enumerate(CHUNKS):
            act.activation(self.rstd[:, t0:t0 + tn], self.rstd[:, t0:t0 + tn], ACT.Exp,
                           scale=-0.5).then_inc(self.rstd_ready, 1)



def project_stage(nc, K, name, w, cols, norm=None, z=None, mix=None):
    pairs = cols // P // 2
    tail = [(col, min(P, cols - col)) for col in range(2 * pairs * P, cols, P)]
    with Stage(nc, name) as s:
        x_hi, x_lo = s.sb("x_hi", [P, KD, T], F32R), s.sb("x_lo", [P, KD, T], F32R)
        raw = s.sb("raw", [P, 2, KD, P])
        w_hi, w_lo = s.sb("w_hi", [P, 2, KD, P], F32R), s.sb("w_lo", [P, 2, KD, P], F32R)
        sq = s.sb("sq", [P, 2, T])
        bank = [[s.ps(f"bank{i}{c}", [P, 512]) for c in range(NC)] for i in range(2)]
        raw_in = [s.sem("raw_in0"), s.sem("raw_in1")]
        hi_done, lo_done = s.sem("hi_done"), s.sem("lo_done")
        summed, evacuated = s.sem("summed"), s.sem("evacuated")
        xhi_done, xlo_done = s.sem("xhi_done"), s.sem("xlo_done")
        z_out = [s.sem("z_out0"), s.sem("z_out1")]
        mix_in = [s.sem("mix_in0"), s.sem("mix_in1")]
        n = None
        if mix is None:
            rstd, zout = s.sb("rstd", [P, T]), s.sb("zout", [P, 2, T])
            n = Norm(s, K, norm, sq, s.sb("acc", [P, T]), rstd,
                     [s.ps("sum0", [P, 512]), s.ps("sum1", [P, 512]), bank[1][2]])
        block = s.block()
        wv = w.rearrange("(k p) n -> p k n", p=P)

        @block.sync
        def _(sp):
            def load(g, i, width=P):
                sp.dma_start(raw[:, i, :, 0:width], wv[:, :, bass.ds(g * P, width)]).then_inc(raw_in[i], 16)

            def store(g, i, width=P):
                sp.wait_ge(evacuated, 3 * g + 9)
                sp.dma_start(z[bass.ds(g * P, width), :], zout[0:width, i, :]).then_inc(z_out[i], 16)

            load(0, 0)
            load(1, 1)
            if mix is not None:
                for k in range(KD):
                    if k >= 2:
                        sp.wait_ge(xlo_done, k - 1)
                    sp.dma_start(sq[:, k % 2, :], mix[k * P:(k + 1) * P, :]).then_inc(mix_in[k % 2], 16)
            with sp.Fori(1, pairs) as j:
                for i in range(2):
                    sp.wait_ge(lo_done, j * 2 + (i - 1))
                    load(j * 2 + i, i)
                    if z is not None:
                        store(j * 2 + (i - 2), i)
            for m, (col, width) in enumerate(tail):
                g = 2 * pairs + m
                sp.wait_ge(lo_done, g - 1)
                load(g, g % 2, width)
            if z is not None:
                for g in range(2 * pairs - 2, 2 * pairs + len(tail)):
                    store(g, g % 2, tail[g - 2 * pairs][1] if g >= 2 * pairs else P)
                total = 2 * pairs + len(tail)
                sp.wait_ge(z_out[0], 16 * ((total + 1) // 2))
                sp.wait_ge(z_out[1], 16 * (total // 2))

        @block.scalar
        def _(act):
            for k in range(KD):
                if mix is None:
                    act.activation(x_hi[:, k, :], K.xT[:, k, :], ACT.Copy,
                                   scale=K.norms[:, norm, k:k + 1]).then_inc(xhi_done, 1)
                else:
                    act.wait_ge(mix_in[k % 2], 16 * (k // 2 + 1))
                    act.activation(x_hi[:, k, :], sq[:, k % 2, :], ACT.Copy).then_inc(xhi_done, 1)

            def split(i, width=P):
                act.activation(w_hi[:, i, :, 0:width], raw[:, i, :, 0:width], ACT.Copy).then_inc(hi_done, 1)

            for i in range(2):
                act.wait_ge(raw_in[i], 16)
                split(i)
            if n is not None:
                n.act_squares(act)
                n.act_rstd(act)
            with act.Fori(1, pairs) as j:
                for i in range(2):
                    act.wait_ge(raw_in[i], j * 16 + 16)
                    act.wait_ge(summed, j * 6 + (3 * i - 3))
                    split(i)
            for m, (col, width) in enumerate(tail):
                g = 2 * pairs + m
                act.wait_ge(raw_in[g % 2], 16 * (g // 2 + 1))
                act.wait_ge(summed, 3 * g - 3)
                split(g % 2, width)

        @block.vector
        def _(dve):
            for k in range(KD):
                dve.wait_ge(xhi_done, k + 1)
                if mix is None:
                    dve.scalar_tensor_tensor(out=x_lo[:, k, :], in0=K.xT[:, k, :], scalar=K.norms[:, norm, k:k + 1],
                                             in1=r32(x_hi[:, k, :]), op0=ALU.mult, op1=ALU.subtract
                                             ).then_inc(xlo_done, 1)
                else:
                    dve.tensor_tensor(x_lo[:, k, :], sq[:, k % 2, :], r32(x_hi[:, k, :]),
                                      ALU.subtract).then_inc(xlo_done, 1)
            if n is not None:
                n.dve_sum(dve)
                dve.wait_ge(n.rstd_ready, NC)

            def evacuate(g, i, width=P):
                for c, (t0, tn) in enumerate(CHUNKS):
                    dve.wait_ge(summed, 3 * g + (c + 1))
                    if mix is None:
                        dve.tensor_tensor(zout[0:width, i, t0:t0 + tn], bank[i][c][0:width, 0:tn],
                                          rstd[0:width, t0:t0 + tn], ALU.mult).then_inc(evacuated, 1)
                    else:
                        x = K.xT[:, bass.ds(g, 1), t0:t0 + tn].rearrange("p k t -> p (k t)")
                        dve.tensor_tensor(x, x, bank[i][c][:, 0:tn], ALU.add).then_inc(evacuated, 1)

            for i in range(2):
                evacuate(i, i)
            with dve.Fori(1, pairs) as j:
                for i in range(2):
                    if z is not None:
                        dve.wait_ge(z_out[i], j * 16)
                    evacuate(j * 2 + i, i)
            for m, (col, width) in enumerate(tail):
                g = 2 * pairs + m
                if z is not None:
                    dve.wait_ge(z_out[g % 2], 16 * (g // 2))
                evacuate(g, g % 2, width)

        @block.gpsimd
        def _(pool):
            def split(g, i, width=P):
                pool.wait_ge(hi_done, g + 1)
                pool.tensor_tensor(w_lo[:, i, :, 0:width], raw[:, i, :, 0:width],
                                   r32(w_hi[:, i, :, 0:width]), ALU.subtract).then_inc(lo_done, 1)

            with pool.Fori(0, pairs) as j:
                for i in range(2):
                    split(j * 2 + i, i)
            for m, (col, width) in enumerate(tail):
                split(2 * pairs + m, (2 * pairs + m) % 2, width)

        @block.tensor
        def _(pe):
            pe.sem_inc(evacuated, 6)
            if n is not None:
                n.pe(pe)
                pe.wait_ge(n.logged, NC)
            pe.wait_ge(xlo_done, KD)

            def group(g, i):
                pe.wait_ge(lo_done, g + 1)
                for c, (t0, tn) in enumerate(CHUNKS):
                    pe.wait_ge(evacuated, 3 * g + (c + 1))
                    for k in range(KD):
                        last = mm3(pe, bank[i][c][:, 0:tn], w_hi[:, i, k, :], w_lo[:, i, k, :],
                                   x_hi[:, k, t0:t0 + tn], x_lo[:, k, t0:t0 + tn], k == 0, k == KD - 1)
                    last.then_inc(summed, 1)

            with pe.Fori(0, pairs) as j:
                for i in range(2):
                    group(j * 2 + i, i)
            for m in range(len(tail)):
                group(2 * pairs + m, (2 * pairs + m) % 2)



def mlp_stage(nc, K, name, norm, w_up, w_down):
    UP, DOWN = 4, KD
    blocks = FF // (UP * P)
    with Stage(nc, name) as s:
        x_hi, x_lo = s.sb("x_hi", [P, KD, T], F32R), s.sb("x_lo", [P, KD, T], F32R)
        a_hi, a_lo = s.sb("a_hi", [P, UP, T], F32R), s.sb("a_lo", [P, UP, T], F32R)
        raw = s.sb("raw", [P, 2, KD * P])
        w_hi, w_lo = s.sb("w_hi", [P, 2, KD * P], F32R), s.sb("w_lo", [P, 2, KD * P], F32R)
        sq = s.sb("sq", [P, 2, T])
        rstd = s.sb("rstd", [P, T])
        bank = [[s.ps(f"bank{i}{c}", [P, 512]) for c in range(NC)] for i in range(2)]
        n = Norm(s, K, norm, sq, s.sb("acc", [P, T]), rstd,
                 [s.ps("sum0", [P, 512]), s.ps("sum1", [P, 512]), bank[1][2]])
        relu, act2 = s.sb("relu", [P, 2, 384]), s.sb("act2", [P, 2, 384])
        raw_in = [s.sem("raw_in0"), s.sem("raw_in1")]
        hi_done, lo_done = s.sem("hi_done"), s.sem("lo_done")
        up_summed, up_out = s.sem("up_summed"), s.sem("up_out")
        down_summed, down_out = s.sem("down_summed"), s.sem("down_out")
        squared, ahi_done, alo_done = s.sem("squared_a"), s.sem("ahi_done"), s.sem("alo_done")
        xhi_done, xlo_done = s.sem("xhi_done"), s.sem("xlo_done")
        block = s.block()
        up_v = w_up.rearrange("(k p) f -> p k f", p=P)
        down_v = w_down.rearrange("(f p) d -> p f d", p=P)
        TILES = UP + DOWN // 2
        UPC, DNC = UP * NC, DOWN * NC

        def used_before(j, t):
            u = t - 2
            if u < 0:
                return down_summed, (j - 1) * DNC + NC * 2 * (TILES + u - UP + 1)
            if u < UP:
                return up_summed, j * UPC + NC * (u + 1)
            return down_summed, j * DNC + NC * 2 * (u - UP + 1)

        @block.sync
        def _(sp):
            def load(j, t):
                i = t % 2
                if t < UP:
                    src = up_v[:, :, bass.ds(j * (UP * P) + t * P, P)]
                    dst = raw[:, i, :].rearrange("p (k n) -> p k n", k=KD)
                else:
                    src = down_v[:, bass.ds(j * UP, UP), (t - UP) * 256:(t - UP + 1) * 256]
                    dst = raw[:, i, :].rearrange("p (f n) -> p f n", f=UP)
                sp.dma_start(dst, src).then_inc(raw_in[i], 16)

            def body(j, first=False):
                for t in range(TILES):
                    if not (first and t < 2):
                        sp.wait_ge(lo_done, j * TILES + (t - 1))
                    load(j, t)

            body(0, True)
            with sp.Fori(1, blocks) as j:
                body(j)

        @block.scalar
        def _(act):
            for k in range(KD):
                act.activation(x_hi[:, k, :], K.xT[:, k, :], ACT.Copy,
                               scale=K.norms[:, norm, k:k + 1]).then_inc(xhi_done, 1)

            def split(j, t, first=False):
                act.wait_ge(raw_in[t % 2], j * (16 * TILES // 2) + 16 * (t // 2 + 1))
                if not (first and t < 2):
                    act.wait_ge(*used_before(j, t))
                act.activation(w_hi[:, t % 2, :], raw[:, t % 2, :], ACT.Copy).then_inc(hi_done, 1)

            def square(j, u):
                for c, (t0, tn) in enumerate(CHUNKS):
                    m = u * NC + c
                    act.wait_ge(up_out, j * UPC + (m + 1))
                    act.wait_ge(alo_done, j * UPC + (m + 1))
                    act.activation(act2[:, m % 2, 0:tn], relu[:, m % 2, 0:tn], ACT.Square).then_inc(squared, 1)
                    act.wait_ge(squared, j * UPC + (m + 1))
                    act.activation(a_hi[:, u, t0:t0 + tn], act2[:, m % 2, 0:tn], ACT.Copy).then_inc(ahi_done, 1)

            def body(j, first=False):
                for t in range(TILES):
                    if 2 <= t < 2 + UP:
                        square(j, t - 2)
                    if not (first and t < 2):
                        split(j, t, first)

            split(0, 0, True)
            split(0, 1, True)
            n.act_squares(act)
            n.act_rstd(act)
            body(0, True)
            with act.Fori(1, blocks) as j:
                body(j)

        @block.gpsimd
        def _(pool):
            with pool.Fori(0, blocks) as j:
                for t in range(TILES):
                    pool.wait_ge(hi_done, j * TILES + (t + 1))
                    pool.tensor_tensor(w_lo[:, t % 2, :], raw[:, t % 2, :], r32(w_hi[:, t % 2, :]),
                                       ALU.subtract).then_inc(lo_done, 1)

        @block.vector
        def _(dve):
            for k in range(KD):
                dve.wait_ge(xhi_done, k + 1)
                dve.scalar_tensor_tensor(out=x_lo[:, k, :], in0=K.xT[:, k, :], scalar=K.norms[:, norm, k:k + 1],
                                         in1=r32(x_hi[:, k, :]), op0=ALU.mult, op1=ALU.subtract
                                         ).then_inc(xlo_done, 1)
            n.dve_sum(dve)
            dve.wait_ge(n.rstd_ready, NC)
            dve.sem_inc(alo_done, 2)

            def low(j, m):
                u, (t0, tn) = m // NC, CHUNKS[m % NC]
                dve.wait_ge(ahi_done, j * UPC + (m + 1))
                dve.tensor_tensor(a_lo[:, u, t0:t0 + tn], act2[:, m % 2, 0:tn], r32(a_hi[:, u, t0:t0 + tn]),
                                  ALU.subtract).then_inc(alo_done, 1)

            with dve.Fori(0, blocks) as j:
                for m in range(UPC):
                    u, (t0, tn) = m // NC, CHUNKS[m % NC]
                    dve.wait_ge(up_summed, j * UPC + (m + 1))
                    dve.scalar_tensor_tensor(out=relu[:, m % 2, 0:tn], in0=bank[u % 2][m % NC][:, 0:tn], scalar=0.0,
                                             in1=rstd[:, t0:t0 + tn], op0=ALU.max, op1=ALU.mult).then_inc(up_out, 1)
                    if m:
                        low(j, m - 1)
                low(j, UPC - 1)
                for d in range(DOWN):
                    for c, (t0, tn) in enumerate(CHUNKS):
                        dve.wait_ge(down_summed, j * DNC + (d * NC + c + 1))
                        dve.tensor_tensor(K.xT[:, d, t0:t0 + tn], K.xT[:, d, t0:t0 + tn], bank[d % 2][c][:, 0:tn],
                                          ALU.add).then_inc(down_out, 1)

        @block.tensor
        def _(pe):
            pe.sem_inc(down_out, 6)
            n.pe(pe)
            pe.wait_ge(n.logged, NC)
            pe.wait_ge(xlo_done, KD)

            def up(j, u):
                i = u % 2
                w = [w[:, i, :].rearrange("p (k n) -> p k n", k=KD) for w in (w_hi, w_lo)]
                pe.wait_ge(lo_done, j * TILES + (u + 1))
                for c, (t0, tn) in enumerate(CHUNKS):
                    if u < 2:
                        pe.wait_ge(down_out, j * DNC + (NC * u + c + 1))
                    else:
                        pe.wait_ge(up_out, j * UPC + (NC * (u - 2) + c + 1))
                    for k in range(KD):
                        last = mm3(pe, bank[i][c][:, 0:tn], w[0][:, k, :], w[1][:, k, :],
                                   x_hi[:, k, t0:t0 + tn], x_lo[:, k, t0:t0 + tn], k == 0, k == KD - 1)
                    last.then_inc(up_summed, 1)

            def down(j, d):
                i, t = d % 2, UP + d // 2
                w = [w[:, t % 2, :].rearrange("p (f n) -> p f n", f=UP)[:, :, (d % 2) * P:(d % 2 + 1) * P]
                     for w in (w_hi, w_lo)]
                pe.wait_ge(lo_done, j * TILES + (t + 1))
                for c in range(NC):
                    if d < 2:
                        pe.wait_ge(up_out, j * UPC + (NC * (UP - 2 + d) + c + 1))
                    else:
                        pe.wait_ge(down_out, j * DNC + (NC * (d - 2) + c + 7))
                    if d == 0:
                        if c == 0:
                            pe.wait_ge(alo_done, j * UPC + NC * (UP - 1) + 2)
                        fs = range(UP - 1)
                    else:
                        fs = range(UP)
                    for f in fs:
                        t0, tn = CHUNKS[c]
                        last = mm3(pe, bank[i][c][:, 0:tn], w[0][:, f, :], w[1][:, f, :],
                                   a_hi[:, f, t0:t0 + tn], a_lo[:, f, t0:t0 + tn], f == 0, f == UP - 1)
                    if d:
                        last.then_inc(down_summed, 1)
                if d == 0:
                    for c, (t0, tn) in enumerate(CHUNKS):
                        f = UP - 1
                        pe.wait_ge(alo_done, j * UPC + (NC * f + c + 3))
                        mm3(pe, bank[i][c][:, 0:tn], w[0][:, f, :], w[1][:, f, :],
                            a_hi[:, f, t0:t0 + tn], a_lo[:, f, t0:t0 + tn], False, True).then_inc(down_summed, 1)

            with pe.Fori(0, blocks) as j:
                for u in range(UP):
                    up(j, u)
                for d in range(DOWN):
                    down(j, d)



def latent_stage(nc, K, M):
    with Stage(nc, "latent") as s:
        cq = s.sb("cq", [P, 3, T])
        cq_hi, cq_lo = s.sb("cq_hi", [P, 3, T], F32R), s.sb("cq_lo", [P, 3, T], F32R)
        w_raw = s.sb("w_raw", [P, 3, HEADS, 192])
        w_hi, w_lo = s.sb("w_hi", [P, 3, 6, P], F32R), s.sb("w_lo", [P, 3, 6, P], F32R)
        cos, sin, rot = s.sb("cos", [P, T]), s.sb("sin", [P, T]), s.sb("rot", [P, P])
        norm_q, norm_kv = s.sb("norm_q", [P, 3]), s.sb("norm_kv", [P, 2])
        square = s.sb("square", [P, 5, T])
        rstd = s.sb("rstd", [P, 2, T])
        turned = s.sb("turned", [P, 2, 512])
        bank = [s.ps(f"bank{i}", [P, 512]) for i in range(8)]
        cq_in, ckv_in, kr_in, w_in, tab_in, norm_in = (s.sem(n) for n in ("cq_in", "ckv_in", "kr_in", "w_in", "tab_in", "norm_in"))
        squared, summed, logged, rstd_ready = (s.sem(n) for n in ("squared", "summed", "logged", "rstd_ready"))
        cq_normed, cqhi_done, cqlo_done = s.sem("cq_normed"), s.sem("cqhi_done"), s.sem("cqlo_done")
        whi_done, wlo_done = s.sem("whi_done"), s.sem("wlo_done")
        projected, q_out = s.sem("projected"), s.sem("q_out")
        rotated, rot_out, by_sin, by_cos = s.sem("rotated"), s.sem("rot_out"), s.sem("by_sin"), s.sem("by_cos")
        block = s.block()

        @block.sync
        def _(sp):
            sp.dma_start(cq[:], K.z[Z_CQ:Z_CKV, :].rearrange("(k p) t -> p k t", p=P)).then_inc(cq_in, 16)
            sp.dma_start(M.ckv[:], K.z[Z_CKV:Z_KR, :].rearrange("(k p) t -> p k t", p=P)).then_inc(ckv_in, 16)
            sp.dma_start(w_raw[:], K.w_uq[0].rearrange("(k p) (h n) -> p k h n", p=P, h=HEADS)).then_inc(w_in, 16)
            for i in range(2):
                sp.dma_start(M.kpe[64 * i:64 * i + 64, :], K.z[Z_KR:Z_KR + ROPE, :]).then_inc(kr_in, 16)
            for dst, src in ((cos, K.c_cos), (sin, K.c_sin), (rot, K.c_rot)):
                sp.dma_start(dst[:], src).then_inc(tab_in, 16)

        @block.gpsimd
        def _(pool):
            with nc.allow_non_contiguous_dma(reason="a column of each norm weight, once"):
                pool.dma_start(norm_q[:], K.q_norm[0].rearrange("(k p) -> p k", p=P)).then_inc(norm_in, 16)
                pool.dma_start(norm_kv[:], K.kv_norm[0].rearrange("(k p) -> p k", p=P)).then_inc(norm_in, 16)
            pool.wait_ge(norm_in, 32)
            pool.wait_ge(whi_done, 2)
            pool.wait_ge(w_in, 16)
            raw = w_raw[:]
            pool.tensor_tensor(w_lo[:, :, 0:4, :], raw[:, :, :, 0:P], r32(w_hi[:, :, 0:4, :]),
                               ALU.subtract).then_inc(wlo_done, 1)
            pool.tensor_tensor(w_lo[:, :, 4:6, :].rearrange("p k g (h n) -> p k (g h) n", h=2), raw[:, :, :, P:192],
                               r32(w_hi[:, :, 4:6, :]).rearrange("p k g (h n) -> p k (g h) n", h=2),
                               ALU.subtract).then_inc(wlo_done, 1)

        @block.scalar
        def _(act):
            act.wait_ge(cq_in, 16)
            for k in range(3):
                act.activation(square[:, k, :], cq[:, k, :], ACT.Square).then_inc(squared, 1)
            act.wait_ge(ckv_in, 16)
            for k in range(2):
                act.activation(square[:, 3 + k, :], M.ckv[:, k, :], ACT.Square).then_inc(squared, 1)
            act.wait_ge(w_in, 16)
            act.activation(w_hi[:, :, 0:4, :], w_raw[:, :, :, 0:P], ACT.Copy).then_inc(whi_done, 1)
            act.activation(w_hi[:, :, 4:6, :].rearrange("p k g (h n) -> p k (g h) n", h=2), w_raw[:, :, :, P:192],
                           ACT.Copy).then_inc(whi_done, 1)
            for m, width in ((0, Q_LORA), (1, KV_LORA)):
                for c, (t0, tn) in enumerate(CHUNKS):
                    act.wait_ge(summed, NC * m + c + 1)
                    act.activation(rstd[:, m, t0:t0 + tn], bank[NC * m + c][:, 0:tn], ACT.Ln,
                                   scale=1.0 / width, bias=K.eps[:, 0:1]).then_inc(logged, 1)
                act.wait_ge(logged, NC * (m + 1))
                act.activation(rstd[:, m, :], rstd[:, m, :], ACT.Exp, scale=-0.5).then_inc(rstd_ready, 1)
            for k in range(3):
                act.wait_ge(cq_normed, k + 1)
                act.activation(cq_hi[:, k, :], cq[:, k, :], ACT.Copy).then_inc(cqhi_done, 1)
            for g in range(6):
                for c, (t0, tn) in enumerate(CHUNKS):
                    act.wait_ge(projected, NC * g + c + 1)
                    dst = M.qn[:, g, t0:t0 + tn] if g < 4 else M.qpe[:, g - 4, t0:t0 + tn]
                    act.activation(dst, bank[NC * (g % 2) + c][:, 0:tn], ACT.Copy).then_inc(q_out, 1)

        @block.tensor
        def _(pe):
            for m, ks in ((0, range(3)), (1, range(3, 5))):
                pe.wait_ge(squared, ks[-1] + 1)
                for c, (t0, tn) in enumerate(CHUNKS):
                    for k in ks:
                        last = pe.matmul(bank[NC * m + c][:, 0:tn], K.ones[:], square[:, k, t0:t0 + tn],
                                         start=(k == ks[0]), stop=(k == ks[-1]))
                    last.then_inc(summed, 1)
            pe.wait_ge(logged, 2 * NC)
            pe.wait_ge(wlo_done, 2)
            pe.wait_ge(cqlo_done, 3)
            for g in range(6):
                for c, (t0, tn) in enumerate(CHUNKS):
                    if g >= 2:
                        pe.wait_ge(q_out, NC * (g - 2) + c + 1)
                    for k in range(3):
                        last = mm3(pe, bank[NC * (g % 2) + c][:, 0:tn], w_hi[:, k, g, :], w_lo[:, k, g, :],
                                   cq_hi[:, k, t0:t0 + tn], cq_lo[:, k, t0:t0 + tn], k == 0, k == 2)
                    last.then_inc(projected, 1)
            pe.wait_ge(q_out, 6 * NC)
            pe.wait_ge(tab_in, 48)
            pe.wait_ge(kr_in, 32)
            for m, x in enumerate((M.qpe[:, 0, :], M.qpe[:, 1, :], M.kpe[:])):
                for c, (t0, tn) in enumerate(CHUNKS):
                    i = NC * m + c
                    if i >= 2:
                        pe.wait_ge(by_sin, i - 1)
                    pe.matmul(bank[6 + i % 2][:, 0:tn], rot[:], x[:, t0:t0 + tn], start=True, stop=True
                              ).then_inc(rotated, 1)

        @block.vector
        def _(dve):
            dve.wait_ge(norm_in, 32)
            dve.wait_ge(rstd_ready, 1)
            for k in range(3):
                dve.scalar_tensor_tensor(out=cq[:, k, :], in0=cq[:, k, :], scalar=norm_q[:, k:k + 1], in1=rstd[:, 0, :],
                                         op0=ALU.mult, op1=ALU.mult).then_inc(cq_normed, 1)
            for k in range(3):
                dve.wait_ge(cqhi_done, k + 1)
                dve.tensor_tensor(cq_lo[:, k, :], cq[:, k, :], r32(cq_hi[:, k, :]), ALU.subtract).then_inc(cqlo_done, 1)
            dve.wait_ge(rstd_ready, 2)
            for k in range(2):
                dve.scalar_tensor_tensor(out=M.ckv[:, k, :], in0=M.ckv[:, k, :], scalar=norm_kv[:, k:k + 1],
                                         in1=rstd[:, 1, :], op0=ALU.mult, op1=ALU.mult)
            for m, x in enumerate((M.qpe[:, 0, :], M.qpe[:, 1, :], M.kpe[:])):
                for c, (t0, tn) in enumerate(CHUNKS):
                    i = NC * m + c
                    dve.wait_ge(rotated, i + 1)
                    dve.tensor_tensor(turned[:, i % 2, 0:tn], bank[6 + i % 2][:, 0:tn], sin[:, t0:t0 + tn],
                                      ALU.mult).then_inc(by_sin, 1)
                    dve.tensor_tensor(x[:, t0:t0 + tn], x[:, t0:t0 + tn], cos[:, t0:t0 + tn], ALU.mult).then_inc(by_cos, 1)
                    dve.wait_ge(by_sin, i + 1)
                    dve.wait_ge(by_cos, i + 1)
                    dve.tensor_tensor(x[:, t0:t0 + tn], x[:, t0:t0 + tn], turned[:, i % 2, 0:tn],
                                      ALU.add).then_inc(rot_out, 1)


def keys_stage(nc, K, M):
    with Stage(nc, "keys") as s:
        wuk = s.sb("wuk", [P, HEADS, 2, P])
        wukT = s.sb("wukT", [P, HEADS, 2, P])
        bank = [s.ps(f"bank{i}", [P, 512]) for i in range(4)]
        wuk_in, wuv_in, rows_out = s.sem("wuk_in"), s.sem("wuv_in"), s.sem("rows_out")
        made, out_act, out_dve = s.sem("made"), s.sem("out_act"), s.sem("out_dve")
        block = s.block()
        KN, V, WT, ROWS, QL = 0, 8, 16, 20, 29
        END = 33

        @block.sync
        def _(sp):
            sp.dma_start(wuk[:], K.w_uk[0].rearrange("h (k p) n -> p (h k) n", p=P)).then_inc(wuk_in, 16)
            for k in range(2):
                sp.dma_start(M.wuv[:, k, :, :], K.w_uv[0][:, k * P:(k + 1) * P, :].rearrange("h p v -> p h v")
                             ).then_inc(wuv_in, 16)
            sp.wait_ge(out_act, (ROWS + 10) // 2)
            sp.wait_ge(out_dve, (ROWS + 8) // 2)
            sp.dma_start(K.rows_prompt.rearrange("(i p) c -> p i c", p=P), M.rows[:, 0:8, :]).then_inc(rows_out, 16)
            sp.dma_start(K.rows_sample, M.rows[0:NS, 8, :]).then_inc(rows_out, 16)
            sp.wait_ge(rows_out, 32)

        @block.tensor
        def _(pe):
            def free(n):
                if n >= 4:
                    pe.wait_ge(out_act if n % 2 == 0 else out_dve, (n - 4) // 2 + 1)
                return bank[n % 4]

            pe.wait_ge(wuk_in, 16)
            pe.wait_ge(wuv_in, 32)
            for n in range(8):
                h, half = n // 2, n % 2
                b = free(KN + n)
                for k in range(2):
                    last = pe.matmul(b[:], wuk[:, h, k, :], M.ckv[:, k, half * 512:half * 512 + 512],
                                     start=(k == 0), stop=(k == 1))
                last.then_inc(made, 1)
            for n in range(8):
                b = free(V + n)
                for k in range(2):
                    last = pe.matmul(b[:], M.ckv[:, k, n * P:(n + 1) * P],
                                     M.wuv[:, k, :, :].rearrange("p h v -> p (h v)"), start=(k == 0), stop=(k == 1))
                last.then_inc(made, 1)
            for h in range(HEADS):
                b = free(WT + h)
                for k in range(2):
                    last = pe.transpose(b[:, k * P:(k + 1) * P], wuk[:, h, k, :], K.ident[:])
                last.then_inc(made, 1)
            for n in range(9):
                b, rows = free(ROWS + n), (P if n < 8 else NS)
                for k in range(2):
                    pe.transpose(b[0:rows, k * P:(k + 1) * P], M.ckv[:, k, n * P:n * P + rows], K.ident[:])
                pe.transpose(b[0:rows, KV_LORA:LAT], M.kpe[0:ROPE, n * P:n * P + rows], K.ident[0:ROPE, 0:ROPE]
                             ).then_inc(made, 1)
            for h in range(HEADS):
                b = free(QL + h)
                if h == 0:
                    pe.wait_ge(out_act, (WT + 4) // 2)
                    pe.wait_ge(out_dve, (WT + 4) // 2)
                for k in range(2):
                    last = pe.matmul(b[:, k * NS:(k + 1) * NS], wukT[:, h, k, :], M.qn[:, h, SEQ:T],
                                     start=True, stop=True)
                last.then_inc(made, 1)

        def copies(eng, copy, parity, out):
            for n in range(parity, END, 2):
                b = bank[n % 4]
                eng.wait_ge(made, n + 1)
                if n < V:
                    h, half = n // 2, n % 2
                    last = copy(M.kn[:, h, half * 512:half * 512 + 512], b[:])
                elif n < WT:
                    last = copy(M.v[:, n - V, :], b[:])
                elif n < ROWS:
                    last = copy(wukT[:, n - WT, :, :].rearrange("p k c -> p (k c)"), b[:, 0:2 * P])
                elif n < QL:
                    rows = P if n - ROWS < 8 else NS
                    last = copy(M.rows[0:rows, n - ROWS, :], b[0:rows, 0:LAT])
                else:
                    last = copy(M.qs[:, 0:2, :, n - QL, :], b[:, 0:2 * NS].rearrange("p (k b t) -> p k b t", k=2, b=NB))
                last.then_inc(out, 1)

        @block.scalar
        def _(act):
            for h in range(HEADS):
                o = 64 * (h % 2)
                for to in (0, ROPE):
                    act.activation(M.qs[to:to + ROPE, 2, :, h, :],
                                   M.qpe[o:o + ROPE, h // 2, SEQ:T].rearrange("p (b t) -> p b t", b=NB), ACT.Copy)
            copies(act, lambda o, x: act.activation(o, x, ACT.Copy), 0, out_act)

        @block.vector
        def _(dve):
            copies(dve, lambda o, x: dve.tensor_copy(o, x), 1, out_dve)


def prompt_attention_stage(nc, K, M):
    with Stage(nc, "pattn") as s:
        q = s.sb("q", [P, 2, SEQ])
        qpe = s.sb("qpe", [P, SEQ])
        v = s.sb("v", [P, 2, 8, P])
        p, pT = s.sb("p", [P, 2, SEQ]), s.sb("pT", [P, 2, 8, P])
        o = s.sb("o", [P, 2, SEQ])
        diag = s.sb("diag", [P, P])
        top, ntop, den, rden = (s.sb(n, [P, 2]) for n in ("top", "ntop", "den", "rden"))
        S = [s.ps(f"S{i}", [P, SEQ]) for i in range(2)]
        PT = s.ps("PT", [P, 8, P])
        O = [s.ps(f"O{i}", [P, 512]) for i in range(2)]
        diag_in, q_ready = s.sem("diag_in"), s.sem("q_ready")
        scored, masked, topped, ntopped = s.sem("scored"), s.sem("masked"), s.sem("topped"), s.sem("ntopped")
        expd, inverted, p_ready, turned = s.sem("expd"), s.sem("inverted"), s.sem("p_ready"), s.sem("turned")
        out_lo, out_hi, valued, o_out = s.sem("out_lo"), s.sem("out_hi"), s.sem("valued"), s.sem("o_out")
        stored = [s.sem("stored0"), s.sem("stored1")]
        o_free = s.sem("o_free")
        block = s.block()
        TILES = 16

        @block.sync
        def _(sp):
            sp.dma_start(diag[:], K.c_causal).then_inc(diag_in, 16)
            sp.sem_inc(o_free, 2)
            with sp.Fori(0, 2) as i:
                for hd in range(2):
                    sp.wait_ge(o_out, i * TILES + (8 * hd + 10))
                    sp.dma_start(K.mix[bass.ds(i * 256 + (512 + P * hd), P), 0:SEQ], o[:, hd, :]).then_inc(stored[hd], 16)
                for hd in range(2):
                    sp.wait_ge(stored[hd], i * 16 + 16)
                    sp.sem_inc(o_free, 1)

        @block.vector
        def _(dve):
            def soften(i, n):
                hd, qt, x = n // 8, n % 8, n % 2
                dve.wait_ge(scored, i * TILES + (n + 1))
                d = S[x][:, qt * P:(qt + 1) * P]
                dve.tensor_tensor(d, d, diag[:], ALU.add).then_inc(masked, 1)
                dve.wait_ge(masked, i * TILES + (n + 1))
                dve.tensor_reduce(top[:, x:x + 1], S[x][:, 0:(qt + 1) * P], AX.X, ALU.max).then_inc(topped, 1)
                dve.wait_ge(topped, i * TILES + (n + 1))
                dve.tensor_scalar(ntop[:, x:x + 1], top[:, x:x + 1], -SCALE, None, ALU.mult).then_inc(ntopped, 1)

            def divide(i, n):
                hd, qt, x = n // 8, n % 8, n % 2
                dve.wait_ge(expd, i * TILES + (n + 3))
                dve.reciprocal(rden[:, x:x + 1], den[:, x:x + 1]).then_inc(inverted, 1)
                dve.wait_ge(inverted, i * TILES + (n + 1))
                dve.tensor_scalar(p[:, x, 0:(qt + 1) * P], p[:, x, 0:(qt + 1) * P], rden[:, x:x + 1], None,
                                  ALU.mult).then_inc(p_ready, 1)

            def copy_hi(i, n):
                hd, qt, x = n // 8, n % 8, n % 2
                if qt >= 4:
                    dve.wait_ge(turned, i * TILES + (n + 3))
                    dve.wait_ge(valued, i * TILES + (n + 1))
                    dve.tensor_copy(pT[:, x, 4:qt + 1, :], PT[:, 4:qt + 1, :]).then_inc(out_hi, 1)

            dve.wait_ge(diag_in, 16)
            dve.sem_inc(out_hi, 1)
            with dve.Fori(0, 2) as i:
                dve.wait_ge(valued, i * TILES + 2)
                for hd in range(2):
                    h = i * 2 + hd
                    dve.tensor_copy(q[:, hd, :], M.qn[:, bass.ds(h, 1), 0:SEQ].rearrange("p a t -> p (a t)"))
                    dve.tensor_copy(v[:, hd, :, :], M.v[:, :, bass.ds(h * P, P)])
                dve.tensor_copy(qpe[:], M.qpe[:, bass.ds(i, 1), 0:SEQ].rearrange("p a t -> p (a t)")).then_inc(q_ready, 1)
                soften(i, 0)
                for n in range(TILES):
                    divide(i, n)
                    if n + 1 < TILES:
                        soften(i, n + 1)
                    copy_hi(i, n)

        @block.scalar
        def _(act):
            act.sem_inc(expd, 2)
            act.sem_inc(out_lo, 1)
            act.sem_inc(o_out, 2)

            def softmax(i, n):
                hd, qt, x = n // 8, n % 8, n % 2
                act.wait_ge(ntopped, i * TILES + (n + 1))
                act.wait_ge(turned, i * TILES + (n + 1))
                act.activation(p[:, x, 0:(qt + 1) * P], S[x][:, 0:(qt + 1) * P], ACT.Exp, bias=ntop[:, x:x + 1],
                               scale=SCALE, accum_out=den[:, x:x + 1]).then_inc(expd, 1)

            def copy_lo(i, n):
                hd, qt, x = n // 8, n % 8, n % 2
                m = min(qt + 1, 4)
                act.wait_ge(turned, i * TILES + (n + 3))
                act.wait_ge(valued, i * TILES + (n + 1))
                act.activation(pT[:, x, 0:m, :], PT[:, 0:m, :], ACT.Copy).then_inc(out_lo, 1)

            def copy_o(i, n):
                hd, qt, x = n // 8, n % 8, n % 2
                act.wait_ge(valued, i * TILES + (n + 3))
                if qt == 0:
                    act.wait_ge(o_free, i * 2 + (hd + 1))
                act.activation(o[:, hd, qt * P:(qt + 1) * P], O[x][:, 0:P], ACT.Copy).then_inc(o_out, 1)

            with act.Fori(0, 2) as i:
                softmax(i, 0)
                for n in range(TILES):
                    if n + 1 < TILES:
                        softmax(i, n + 1)
                    copy_lo(i, n)
                    if n:
                        copy_o(i, n - 1)
                copy_o(i, TILES - 1)

        @block.tensor
        def _(pe):
            pe.sem_inc(turned, 2)
            pe.sem_inc(valued, 2)

            def score(i, n):
                hd, qt, x = n // 8, n % 8, n % 2
                pe.wait_ge(expd, i * TILES + (n + 1))
                keys, o64 = (qt + 1) * P, 64 * hd
                for k0 in range(0, keys, 512):
                    kn = min(512, keys - k0)
                    pe.matmul(S[x][:, k0:k0 + kn], q[:, hd, qt * P:(qt + 1) * P],
                              M.kn[:, bass.ds(i * 2 + hd, 1), k0:k0 + kn].rearrange("p a t -> p (a t)"),
                              start=True, stop=False)
                    last = pe.matmul(S[x][:, k0:k0 + kn], qpe[o64:o64 + 64, qt * P:(qt + 1) * P],
                                     M.kpe[o64:o64 + 64, k0:k0 + kn], start=False, stop=True)
                last.then_inc(scored, 1)

            def turn(i, n):
                hd, qt, x = n // 8, n % 8, n % 2
                pe.wait_ge(p_ready, i * TILES + (n + 1))
                pe.wait_ge(out_lo, i * TILES + (n + 1))
                if qt >= 4:
                    pe.wait_ge(out_hi, i * 8 + (4 * hd + qt - 3))
                for k in range(qt + 1):
                    last = pe.transpose(PT[:, k, :], p[:, x, k * P:(k + 1) * P], K.ident[:])
                last.then_inc(turned, 1)

            def value(i, n):
                hd, qt, x = n // 8, n % 8, n % 2
                pe.wait_ge(out_lo, i * TILES + (n + 2))
                if qt >= 4:
                    pe.wait_ge(out_hi, i * 8 + (4 * hd + qt - 2))
                pe.wait_ge(o_out, i * TILES + (n + 1))
                for k in range(qt + 1):
                    last = pe.matmul(O[x][:, 0:P], v[:, hd, k, :], pT[:, x, k, :], start=(k == 0), stop=(k == qt))
                last.then_inc(valued, 1)

            with pe.Fori(0, 2) as i:
                pe.wait_ge(q_ready, i + 1)
                score(i, 0)
                for n in range(TILES):
                    if n + 1 < TILES:
                        score(i, n + 1)
                    turn(i, n)
                    if n:
                        value(i, n - 1)
                value(i, TILES - 1)


def sample_attention_stage(nc, K, M):
    Place = namedtuple("Place", "first second start last")
    GROUPS = PAGES // PG
    RING = 4
    Q = HEADS * TS
    Q2 = 2 * Q
    with Stage(nc, "sattn") as s:
        lat = s.sb("lat", [P, RING, PG, LAT])
        lat_hi, lat_lo = (s.sb(n, [P, 2, PG, KV_LORA], F32R) for n in ("lat_hi", "lat_lo"))
        k_hi, k_lo = (s.sb(n, [P, 2, 2, 512], F32R) for n in ("k_hi", "k_lo"))
        k_rot = s.sb("k_rot", [P, 2, 512], F32R)
        pages = s.sb("pages", [1, NB * PAGES], I32)
        newmask = s.sb("newmask", [Q2, NB, NS])
        q = s.sb("q", [P, 3, NB, Q2])
        q_hi, q_lo = (s.sb(n, [P, 3, Q2], F32R) for n in ("q_hi", "q_lo"))
        p, pT = s.sb("p", [Q2, 2, 512]), s.sb("pT", [P, PG, Q2], F32R)
        sn, pn, pnT = s.sb("sn", [Q2, NB, NS]), s.sb("pn", [Q2, NB, NS]), s.sb("pnT", [NS, NB, Q2])
        m_new, nm_new, den_new = (s.sb(n, [Q2, NB]) for n in ("m_new", "nm_new", "den_new"))
        acc_new, acc, acc_div = s.sb("acc_new", [Q2, NB, KV_LORA]), s.sb("acc", [Q2, KV_LORA]), s.sb("acc_div", [Q2, KV_LORA])
        m, alpha, gsum = (s.sb(n, [Q2, 2]) for n in ("m", "alpha", "gsum"))
        den, gm, nm, rden = (s.sb(n, [Q2, 1]) for n in ("den", "gm", "nm", "rden"))
        halves = s.sb("halves", [Q2, Q])
        outT = s.sb("outT", [P, 2, HEADS, NS])
        o = s.sb("o", [P, HEADS, NS])
        KT = s.ps("KT", [P, 3, 512])
        S = [s.ps(f"S{i}", [P, 512]) for i in range(2)]
        PT, O, X = s.ps("PT", [P, 512]), s.ps("O", [P, 512]), s.ps("X", [P, 512])
        OT = X[:, 0:2 * Q]
        passed = s.sem("passed")
        tab_in, lat_in = s.sem("tab_in"), [s.sem(f"lat_in{i}") for i in range(RING)]
        halves_made, q_made, zeroed = s.sem("halves_made"), s.sem("q_made"), s.sem("zeroed")
        sn_made, sn_masked, sn_topped, nm_made = (s.sem(n) for n in ("sn_made", "sn_masked", "sn_topped", "nm_made"))
        pn_made, pn_turned, pn_out, on_made, on_out = (s.sem(n) for n in (
            "pn_made", "pn_turned", "pn_out", "on_made", "on_out"))
        kt_made, khi_done, klo_done = s.sem("kt_made"), s.sem("khi_done"), s.sem("klo_done")
        lathi_done, latlo_done = s.sem("lathi_done"), s.sem("latlo_done")
        qhi_done, qlo_done = s.sem("qhi_done"), s.sem("qlo_done")
        scored, chain, topped, expd = (s.sem(n) for n in ("scored", "chain", "topped", "expd"))
        turned, pthi_done, pt_out, valued, acc_done = (s.sem(n) for n in (
            "turned", "pthi_done", "pt_out", "valued", "acc_done"))
        inverted, divided, ot_made, ot_out = (s.sem(n) for n in ("inverted", "divided", "ot_made", "ot_out"))
        o_made, o_out, stored = s.sem("o_made"), s.sem("o_out"), s.sem("stored")
        block = s.block()
        n_phys = K.cache.shape[0]

        def over_groups(eng, step):
            def quad(b, g, first, start=False, last=False):
                for i in range(RING):
                    step(b, g, i, Place(first and i == 0, first and i == 1, start and i == 0, last and i == RING - 1))

            quad(0, 0, True, start=True)
            with eng.Fori(RING, GROUPS, RING) as g:
                quad(0, g, False)
            with eng.Fori(1, NB - 1) as b:
                quad(b, 0, True)
                with eng.Fori(RING, GROUPS, RING) as g:
                    quad(b, g, False)
            quad(NB - 1, 0, True)
            with eng.Fori(RING, GROUPS - RING, RING) as g:
                quad(NB - 1, g, False)
            quad(NB - 1, GROUPS - RING, False, last=True)

        @block.sync
        def _(sp):
            sp.dma_start(pages[:], K.page_table).then_inc(tab_in, 16)
            for i in range(2):
                sp.dma_start(newmask[i * Q:(i + 1) * Q], K.c_newmask).then_inc(tab_in, 16)
            sp.wait_ge(tab_in, 48)

            def load(g, i):
                for n in range(PG):
                    page = sp.value_load(pages[0:1, bass.ds(g * PG + n, 1)], min_val=0, max_val=n_phys - 1)
                    sp.dma_start(lat[:, i, n, :], K.cache[bass.ds(page, 1), :, :].rearrange("a p c -> (a p) c")
                                 ).then_inc(lat_in[i], 16)

            for i in range(RING):
                load(i, i)
            with sp.Fori(1, NB * GROUPS // RING) as j:
                for i in range(RING):
                    sp.wait_ge(kt_made, j * RING + (i - RING + 1))
                    sp.wait_ge(latlo_done, j * RING + (i - RING + 1))
                    load(j * RING + i, i)
            sp.wait_ge(o_out, 1)
            sp.dma_start(K.mix[512:1024, SEQ:T].rearrange("(h p) t -> p h t", p=P), o[:]).then_inc(stored, 16)
            sp.wait_ge(stored, 16)

        def pages_in(eng, b, g, i):
            eng.wait_ge(lat_in[i % RING],
                        b * (16 * PAGES // RING) + g * (16 * PG // RING) + (i // RING + 1) * 16 * PG)

        @block.tensor
        def _(pe):
            pe.sem_inc(turned, 2)
            pe.sem_inc(valued, 2)
            pe.sem_inc(ot_made, 1)
            pe.wait_ge(q_made, 2)
            pe.wait_ge(halves_made, 1)
            for b in range(NB):
                for c, w in ((0, P), (1, P), (2, ROPE)):
                    k = M.ckv[:, c, SEQ:T] if c < 2 else M.kpe[0:ROPE, SEQ:T]
                    last = pe.matmul(S[0][0:Q2, b * NS:(b + 1) * NS], q[0:w, c, b, :], k, start=(c == 0), stop=(c == 2))
            last.then_inc(sn_made, 1)
            pe.wait_ge(pn_made, NB)
            for b in range(NB):
                last = pe.transpose(X[0:NS, b * Q2:(b + 1) * Q2], pn[:, b, :], K.ident[0:Q2, 0:Q2])
            last.then_inc(pn_turned, 1)
            pe.wait_ge(zeroed, 1)
            pe.wait_ge(pn_out, 1)
            for b in range(NB):
                bank = KT[0:Q2, b // 2, :] if b < 6 else S[1][0:Q2, :]
                last = pe.matmul(bank[:, (b % 2) * KV_LORA:(b % 2 + 1) * KV_LORA], pnT[:, b, :], M.rows[0:NS, 8, 0:KV_LORA],
                                 start=True, stop=True)
            last.then_inc(on_made, 1)

            def turn_keys(b, g, i, first=False):
                pages_in(pe, b, g, i)
                for c, w in ((0, P), (1, P), (2, ROPE)):
                    if not first and c == 0:
                        pe.wait_ge(klo_done, b * (2 * GROUPS) + 2 * g + (2 * i - 1))
                    if not first and c == 2:
                        wait_apart(pe, klo_done, b * (2 * GROUPS) + 2 * g + 2 * i, passed)
                    for n in range(PG):
                        last = pe.transpose(KT[0:w, c, n * P:(n + 1) * P], lat[:, i % RING, n, c * P:c * P + w], K.ident[:])
                last.then_inc(kt_made, 1)

            def turn(b, g, i):
                pe.wait_ge(expd, b * GROUPS + g + (i + 3))
                pe.wait_ge(pt_out, b * GROUPS + g + (i + 1))
                pe.sem_inc(passed, 1)
                for n in range(PG):
                    last = pe.transpose(PT[:, n * Q2:(n + 1) * Q2], p[:, i % 2, n * P:(n + 1) * P], K.ident[0:Q2, 0:Q2])
                last.then_inc(turned, 1)

            def value(b, g, i):
                pe.wait_ge(pt_out, b * GROUPS + g + (i + 2))
                pe.wait_ge(latlo_done, b * GROUPS + g + (i + 1))
                pe.wait_ge(acc_done, b * GROUPS + g + (i + 1))
                pe.sem_inc(passed, 1)
                for n in range(PG):
                    pe.matmul(O[0:Q2, 0:KV_LORA], pT[:, n, :], lat_hi[:, i % 2, n, :], start=(n == 0), stop=False)
                    last = pe.matmul(O[0:Q2, 0:KV_LORA], pT[:, n, :], lat_lo[:, i % 2, n, :], start=False,
                                     stop=(n == PG - 1))
                last.then_inc(valued, 1)

            def merge(b):
                pe.wait_ge(divided, b)
                pe.wait_ge(ot_out, b)
                pe.sem_inc(passed, 1)
                for c in range(2):
                    last = pe.matmul(OT[:, c * Q:(c + 1) * Q], acc_div[:, c * P:(c + 1) * P], halves[:],
                                     start=True, stop=True)
                last.then_inc(ot_made, 1)

            def step(b, g, i, at):
                if not at.last:
                    turn_keys(b, g, i + 1)
                if not at.start:
                    turn(b, g, i - 1)
                pe.wait_ge(klo_done, b * (2 * GROUPS) + 2 * g + (2 * i + 2))
                pe.wait_ge(expd, b * GROUPS + g + (i + 1))
                if at.first:
                    pe.wait_ge(qlo_done, b + 1)
                pe.sem_inc(passed, 1)
                out, y = S[i % 2][0:Q2, :], i % 2
                for c in range(2):
                    mm3(pe, out, q_hi[:, c, :], q_lo[:, c, :], k_hi[:, y, c, :], k_lo[:, y, c, :], c == 0, False)
                pe.matmul(out, q_hi[:, 2, :], k_rot[:, y, :], start=False, stop=False)
                pe.matmul(out, q_lo[0:ROPE, 2, :], k_rot[0:ROPE, y, :], start=False, stop=True).then_inc(scored, 1)
                if not at.start:
                    value(b, g, i - 1)
                if at.first and not at.start:
                    merge(b)

            pe.wait_ge(on_out, 2)
            turn_keys(0, 0, 0, first=True)
            over_groups(pe, step)
            turn(NB - 1, GROUPS - RING, RING - 1)
            value(NB - 1, GROUPS - RING, RING - 1)
            merge(NB)
            pe.wait_ge(ot_out, NB + 1)
            for h in range(HEADS):
                for c in range(2):
                    last = pe.matmul(X[:, h * NS:(h + 1) * NS], M.wuv[:, c, h, :], outT[:, c, h, :],
                                     start=(c == 0), stop=(c == 1))
            last.then_inc(o_made, 1)

        @block.scalar
        def _(act):
            act.sem_inc(expd, 2)
            act.sem_inc(ot_out, 1)
            act.activation(q[:, :, :, 0:Q], M.qs[:].rearrange("p c b h t -> p c b (h t)"), ACT.Copy).then_inc(q_made, 1)
            for b in range(NB):
                act.wait_ge(nm_made, 1)
                act.activation(pn[:, b, :], sn[:, b, :], ACT.Exp, bias=nm_new[:, b:b + 1], scale=SCALE,
                               accum_out=den_new[:, b:b + 1]).then_inc(pn_made, 1)
            act.wait_ge(pn_turned, 1)
            act.activation(pnT[:, :, 0:Q], X[0:NS, :].rearrange("p (b q) -> p b q", b=NB)[:, :, 0:Q], ACT.Copy
                           ).then_inc(pn_out, 1)

            def split_keys(b, g, i):
                act.wait_ge(kt_made, b * GROUPS + g + (i + 1))
                act.activation(k_hi[:, i % 2, :, :], KT[:, 0:2, :], ACT.Copy).then_inc(khi_done, 1)
                act.activation(k_rot[0:ROPE, i % 2, :], KT[0:ROPE, 2, :], ACT.Copy).then_inc(khi_done, 1)

            def step(b, g, i, at):
                y = i % 2
                if at.first:
                    if not at.start:
                        act.wait_ge(scored, b * GROUPS)
                    for r in range(2):
                        src = M.qs[:, :, bass.ds(b, 1), :, :].rearrange("p c a h t -> p c (a h t)")
                        h = act.activation(q_hi[:, :, r * Q:(r + 1) * Q], src, ACT.Copy)
                    h.then_inc(qhi_done, 1)
                if not at.last:
                    if not at.start:
                        act.wait_ge(scored, b * GROUPS + g + i)
                    split_keys(b, g, i + 1)
                pages_in(act, b, g, i)
                act.wait_ge(valued, b * GROUPS + g + (i + 1))
                act.activation(lat_hi[:, y, :, :], lat[:, i % RING, :, 0:KV_LORA], ACT.Copy).then_inc(lathi_done, 1)
                act.wait_ge(topped, b * GROUPS + g + (i + 1))
                act.wait_ge(acc_done, b * GROUPS + g + i)
                act.activation(alpha[:, y:y + 1], m[:, 1 - y:2 - y], ACT.Exp, bias=nm[:, 0:1], scale=SCALE)
                act.wait_ge(turned, b * GROUPS + g + (i + 1))
                act.activation(p[:, y, :], S[y][0:Q2, :], ACT.Exp, bias=nm[:, 0:1], scale=SCALE,
                               accum_out=gsum[:, y:y + 1]).then_inc(expd, 1)
                if at.first and not at.start:
                    copy_merged(b)

            def copy_merged(b):
                act.wait_ge(ot_made, b + 1)
                act.activation(outT[:, :, :, bass.ds(b * TS - TS, TS)],
                               OT.rearrange("p (c h t) -> p c h t", c=2, h=HEADS), ACT.Copy).then_inc(ot_out, 1)

            split_keys(0, 0, 0)
            over_groups(act, step)
            copy_merged(NB)
            act.wait_ge(o_made, 1)
            act.activation(o[:], X[:, 0:HEADS * NS].rearrange("p (h t) -> p h t", h=HEADS), ACT.Copy).then_inc(o_out, 1)

        @block.gpsimd
        def _(pool):
            pool.memset(pnT[:, :, Q:Q2], 0.0).then_inc(zeroed, 1)

            def step(b, g, i, at):
                if at.first:
                    pool.wait_ge(qhi_done, b + 1)
                    for r in range(2):
                        src = M.qs[:, :, bass.ds(b, 1), :, :].rearrange("p c a h t -> p c (a h t)")
                        h = pool.tensor_tensor(q_lo[:, :, r * Q:(r + 1) * Q], src, r32(q_hi[:, :, r * Q:(r + 1) * Q]),
                                               ALU.subtract)
                    h.then_inc(qlo_done, 1)
                pool.wait_ge(lathi_done, b * GROUPS + g + (i + 1))
                pool.tensor_tensor(lat_lo[:, i % 2, :, :], lat[:, i % RING, :, 0:KV_LORA], r32(lat_hi[:, i % 2, :, :]),
                                   ALU.subtract).then_inc(latlo_done, 1)

            over_groups(pool, step)

        @block.vector
        def _(dve):
            dve.sem_inc(pt_out, 1)
            dve.sem_inc(acc_done, 1)
            dve.tensor_copy(q[:, :, :, Q:Q2], M.qs[:].rearrange("p c b h t -> p c b (h t)")).then_inc(q_made, 1)
            dve.tensor_tensor(halves[:], K.ident[0:Q2, 0:Q], K.ident[0:Q2, Q:Q2], ALU.add).then_inc(halves_made, 1)
            dve.wait_ge(tab_in, 48)
            dve.wait_ge(sn_made, 1)
            dve.tensor_tensor(sn[:], S[0][0:Q2, :].rearrange("p (b t) -> p b t", b=NB), newmask[:], ALU.add
                              ).then_inc(sn_masked, 1)
            dve.wait_ge(sn_masked, 1)
            dve.tensor_reduce(m_new[:], sn[:], AX.X, ALU.max).then_inc(sn_topped, 1)
            dve.wait_ge(sn_topped, 1)
            dve.tensor_scalar(nm_new[:], m_new[:], -SCALE, None, ALU.mult).then_inc(nm_made, 1)
            dve.wait_ge(on_made, 1)
            dve.tensor_copy(acc_new[:, 0:6, :].rearrange("p b v -> p (b v)"), KT[0:Q2, :, :].rearrange("p c v -> p (c v)")
                            ).then_inc(on_out, 1)
            dve.tensor_copy(acc_new[:, 6:8, :].rearrange("p b v -> p (b v)"), S[1][0:Q2, :]).then_inc(on_out, 1)

            def split_latent_keys(b, g, i):
                y = i % 2
                dve.wait_ge(khi_done, b * (2 * GROUPS) + 2 * g + (2 * i + 1))
                dve.tensor_tensor(k_lo[:, y, :, :], KT[:, 0:2, :], r32(k_hi[:, y, :, :]), ALU.subtract).then_inc(klo_done, 1)

            def split_rotated_keys(b, g, i):
                y = i % 2
                dve.wait_ge(khi_done, b * (2 * GROUPS) + 2 * g + (2 * i + 2))
                dve.tensor_tensor(k_rot[ROPE:P, y, :], KT[0:ROPE, 2, :], r32(k_rot[0:ROPE, y, :]), ALU.subtract
                                  ).then_inc(klo_done, 1)

            def split_p(b, g, i):
                dve.wait_ge(turned, b * GROUPS + g + (i + 3))
                dve.wait_ge(valued, b * GROUPS + g + (i + 2))
                src = PT[:, 0:PG * Q2].rearrange("p (n q) -> p n q", n=PG)
                dve.tensor_copy(pT[:, :, 0:Q], src[:, :, 0:Q]).then_inc(pthi_done, 1)
                dve.wait_ge(pthi_done, b * GROUPS + g + (i + 1))
                dve.tensor_tensor(pT[:, :, Q:Q2], src[:, :, Q:Q2], r32(pT[:, :, 0:Q]), ALU.subtract).then_inc(pt_out, 1)

            CH = 3

            def top(b, g, i, first):
                x, link = i % 2, b * (GROUPS * CH) + g * CH + i * CH
                if first:
                    dve.tensor_copy(m[:, 1:2], m_new[:, bass.ds(b, 1)])
                dve.wait_ge(scored, b * GROUPS + g + (i + 1))
                dve.tensor_reduce(gm[:], S[x][0:Q2, :], AX.X, ALU.max).then_inc(chain, 1)
                dve.wait_ge(chain, link + 1)
                dve.tensor_tensor(m[:, x:x + 1], m[:, 1 - x:2 - x], gm[:], ALU.max).then_inc(chain, 1)
                dve.wait_ge(chain, link + 2)
                dve.tensor_scalar(nm[:], m[:, x:x + 1], -SCALE, None, ALU.mult).then_inc(topped, 1)
                dve.sem_inc(chain, 1)

            def gather(b, g, i, from_new):
                y = i % 2
                dve.wait_ge(valued, b * GROUPS + g + (i + 3))
                den_in = den_new[:, bass.ds(b, 1)] if from_new else den[:]
                acc_in = acc_new[:, bass.ds(b, 1), :].rearrange("p a v -> p (a v)") if from_new else acc[:]
                dve.scalar_tensor_tensor(out=den[:], in0=den_in, scalar=alpha[:, y:y + 1], in1=gsum[:, y:y + 1],
                                         op0=ALU.mult, op1=ALU.add)
                dve.scalar_tensor_tensor(out=acc[:], in0=acc_in, scalar=alpha[:, y:y + 1], in1=O[0:Q2, 0:KV_LORA],
                                         op0=ALU.mult, op1=ALU.add).then_inc(acc_done, 1)

            def divide(b):
                dve.wait_ge(acc_done, b * GROUPS + 1)
                dve.reciprocal(rden[:], den[:]).then_inc(inverted, 1)
                dve.wait_ge(inverted, b)
                dve.wait_ge(ot_made, b)
                dve.tensor_scalar(acc_div[:], acc[:], rden[:, 0:1], None, ALU.mult).then_inc(divided, 1)

            def step(b, g, i, at):
                if not at.start:
                    split_p(b, g, i - 1)
                if not at.last:
                    split_latent_keys(b, g, i + 1)
                top(b, g, i, at.first)
                if not at.last:
                    split_rotated_keys(b, g, i + 1)
                if not at.start:
                    gather(b, g, i - 1, at.second)
                if at.first and not at.start:
                    divide(b)

            split_latent_keys(0, 0, 0)
            split_rotated_keys(0, 0, 0)
            over_groups(dve, step)
            split_p(NB - 1, GROUPS - RING, RING - 1)
            gather(NB - 1, GROUPS - RING, RING - 1, False)
            divide(NB)



def alpha_stage(nc, K):
    with Stage(nc, "alpha") as s:
        a1, w2, bias = s.sb("a1", [GATE_RANK, T]), s.sb("w2", [GATE_RANK, HEADS * P]), s.sb("bias", [P, HEADS])
        out = s.sb("out", [P, HEADS, T])
        bank = [[s.ps(f"bank{i}{c}", [P, 512]) for c in range(NC)] for i in range(2)]
        loaded, projected, biased, stored = (s.sem(n) for n in ("loaded", "projected", "biased", "stored"))
        block = s.block()

        @block.sync
        def _(sp):
            sp.dma_start(a1[:], K.z[G_A:G_A + GATE_RANK, :]).then_inc(loaded, 16)
            sp.dma_start(w2[:], K.w_alpha2[0]).then_inc(loaded, 16)
            with nc.allow_non_contiguous_dma(reason="a column of b_alpha for each head, once"):
                sp.dma_start(bias[:], K.b_alpha[0].rearrange("(h p) -> p h", p=P)).then_inc(loaded, 16)
            for h in range(HEADS):
                sp.wait_ge(biased, NC * (h + 1))
                sp.dma_start(K.z[G_GATE + h * P:G_GATE + (h + 1) * P, :], out[:, h, :]).then_inc(stored, 16)
            sp.wait_ge(stored, 16 * HEADS)

        @block.tensor
        def _(pe):
            pe.wait_ge(loaded, 48)
            for h in range(HEADS):
                for c, (t0, tn) in enumerate(CHUNKS):
                    if h >= 2:
                        pe.wait_ge(biased, NC * (h - 2) + c + 1)
                    pe.matmul(bank[h % 2][c][:, 0:tn], w2[:, h * P:(h + 1) * P], a1[:, t0:t0 + tn],
                              start=True, stop=True).then_inc(projected, 1)

        @block.scalar
        def _(act):
            act.wait_ge(loaded, 48)
            for h in range(HEADS):
                for c, (t0, tn) in enumerate(CHUNKS):
                    act.wait_ge(projected, NC * h + c + 1)
                    act.activation(out[:, h, t0:t0 + tn], bank[h % 2][c][:, 0:tn], ACT.Identity,
                                   bias=bias[:, h:h + 1]).then_inc(biased, 1)


def scan_stage(nc, K, name, hgrn, rows, norm_w, state_in, state_prompt, state_sample, mix):
    VC = 1 if hgrn else 2
    V = VC * P
    C = SEQ // P
    L = len(LEVELS) + 1
    LS = 4
    JS = NB * V // 512
    r_q, r_k, r_v, r_g, r_f = rows
    with Stage(nc, name) as s:
        f_raw = s.sb("f_raw", [P, T])
        q, k = s.sb("q", [P, 2, T]), s.sb("k", [P, 2, T])
        v, gate = s.sb("v", [P, VC, T]), s.sb("gate", [P, VC, T])
        soft, logf, b = s.sb("soft", [P, T]), s.sb("logf", [P, T]), s.sb("b", [P, T])
        expb = s.sb("expb", [P, T])
        q_dec = s.sb("q_dec", [P, 2, T])
        last_dec = s.sb("last_dec", [P, 2, C + NB])
        k_tok, v_tok = s.sb("k_tok", [P, 2, C + 1, P]), s.sb("v_tok", [P, 2, C + 1, V])
        dec, x = s.sb("dec", [P, 2, T]), s.sb("x", [P, 2, T])
        a = s.sb("a", [P, C + 1, P])
        state, s0 = s.sb("state", [P, C, V]), s.sb("s0", [P, NB, V])
        v_own = s.sb("v_own", [NS, NB, V])
        o, sq, rstd = s.sb("o", [P, VC, T]), s.sb("sq", [P, VC, T]), s.sb("rstd", [P, T])
        levels, starts, own = s.sb("levels", [P, L, P], I32), s.sb("starts", [P, T]), s.sb("own", [NS, NB])
        w_norm = s.sb("w_norm", [P, VC])
        lb = s.sb("lb", [P, 5, HEADS]) if hgrn else None
        lbh = s.sb("lbh", [P, 2, 2]) if hgrn else None
        S = [s.ps(f"S{i}", [P, 4, P]) for i in range(4)]
        TB = [s.ps(f"TB{i}", [P, 4, P]) for i in range(2)]
        SS, U = s.ps("SS", [P, 512]), s.ps("U", [P, 512])
        mean = [TB[0][:].rearrange("p c t -> p (c t)"), U, SS]
        const_in, norm_in, f_in, v_in, gate_in, s0_in = (s.sem(n) for n in (
            "const_in", "norm_in", "f_in", "v_in", "gate_in", "s0_in"))
        qk_in = [s.sem("qk_in0"), s.sem("qk_in1")]
        passed = s.sem("passed")
        stores_done = s.sem("stores_done")
        stored, lb_made, cleared = s.sem("stored"), s.sem("lb_made"), s.sem("cleared")
        QK = 16 if hgrn else 32
        GROUPS = 3
        TURNS = GROUPS * (1 + VC)
        per = dict(abs_out=1, e_out=1, soft_out=1, log_sig=1, neg_made=1, k_exp=1, f_exp=1, f_mixed=1, f_clamped=1,
                   log_out=1, clamped=1, b_made=1, q_silu=1, q_ready=1, k_ready=1, expb_out=1, q_dec_made=1,
                   k_diff=1, k_decay=1, k_dec_made=1, turned=TURNS, tok_out=TURNS,
                   diffed=7, decayed=7, x_made=7, scored=L, a_out=L,
                   u_made=C, s_made=C, valued=3, o_out=3, own_made=1, us_made=JS, us_out=JS,
                   mean_in=NC, mean_out=NC, rstd_out=1, gate_silu=1, normed=VC, final=VC)
        sem = {n: s.sem(n) for n in per}
        block = s.block()

        def wait(eng, n, h, count):
            eng.wait_ge(sem[n], h[0] * (2 * per[n]) + (h[1] * per[n] + per[n] + count))

        def wait_before(eng, n, h, count=None):
            count = per[n] if count is None else count
            eng.wait_ge(sem[n], h[0] * (2 * per[n]) + (h[1] * per[n] + count))

        def credit(eng, names):
            for n in names.split():
                eng.sem_inc(sem[n], per[n])

        def loads(eng, sm, h, of_head):
            eng.wait_ge(sm, h[0] * (2 * of_head) + (h[1] + 1) * of_head)

        def qk_loaded(eng, h):
            eng.wait_ge(qk_in[h[1]], h[0] * QK + QK)

        def row(base, h, width=P):
            return bass.ds(h[0] * (2 * width) + (base + h[1] * width), width)

        def half(ap, m, second):
            n = ap.shape[-1]
            return ap.rearrange("p (n m) -> p n m", m=2 * m)[:, :, m:2 * m] if second else \
                ap.rearrange("p (n m) -> p n m", m=2 * m)[:, :, 0:m]

        def width(li):
            return T if li < LS else SEQ

        @block.sync
        def _(sp):
            sp.dma_start(levels[:], K.c_levels).then_inc(const_in, 16)
            sp.dma_start(starts[:], K.c_starts).then_inc(const_in, 16)
            sp.dma_start(own[:], K.c_own).then_inc(const_in, 16)
            sp.sem_inc(stores_done, 1)

            def load_head(h, first=False):
                if not first:
                    wait_before(sp, "neg_made" if hgrn else "log_sig", h)
                sp.dma_start(f_raw[:], K.z[row(r_f, h), :]).then_inc(f_in, 16)
                if not first:
                    wait_before(sp, "turned", h)
                    sp.wait_ge(sem["a_out"], h[0] * (2 * L) + h[1] * L)
                    sp.wait_ge(sem["k_dec_made"], h[0] * 2 + h[1])
                sp.dma_start(q[:, h[1], :], K.z[row(r_q, h), :]).then_inc(qk_in[h[1]], 16)
                if not hgrn:
                    sp.dma_start(k[:, h[1], :], K.z[row(r_k, h), :]).then_inc(qk_in[h[1]], 16)
                sp.dma_start(v[:], K.z[row(r_v, h, V), :].rearrange("(c p) t -> p c t", p=P)).then_inc(v_in, 16)

            def load_tail(h, first=False):
                if not first:
                    wait_before(sp, "final", h)
                    sp.wait_ge(stored, h[0] * 96 + h[1] * 48)
                    sp.sem_inc(stores_done, 1)
                sp.dma_start(gate[:], K.z[row(r_g, h, V), :].rearrange("(c p) t -> p c t", p=P)).then_inc(gate_in, 16)
                sp.dma_start(s0[:], state_in[:, row(0, h, 1), :, :].rearrange("b a k v -> k (b a) v")).then_inc(s0_in, 16)

            def store(h):
                wait(sp, "s_made", h, C)
                sp.dma_start(state_prompt[row(0, h, 1), :, :].rearrange("a k v -> (a k) v"),
                             state[:, C - 1, :]).then_inc(stored, 16)
                wait(sp, "us_out", h, JS)
                sp.dma_start(state_sample[:, row(0, h, 1), :, :].rearrange("b a k v -> k (b a) v"), s0[:]
                             ).then_inc(stored, 16)
                wait(sp, "final", h, VC)
                sp.dma_start(mix[row(0, h, V), :].rearrange("(c p) t -> p c t", p=P), o[:]).then_inc(stored, 16)

            load_head((0, 0), True)
            load_tail((0, 0), True)
            load_head((0, 1))
            store((0, 0))
            load_tail((0, 1))
            with sp.Fori(1, HEADS // 2) as i:
                load_head((i, 0))
                store((i - 1, 1))
                load_tail((i, 0))
                load_head((i, 1))
                store((i, 0))
                load_tail((i, 1))
            store((HEADS // 2 - 1, 1))
            sp.wait_ge(stored, 48 * HEADS)

        @block.gpsimd
        def _(pool):
            credit(pool, "q_ready diffed own_made")
            with nc.allow_non_contiguous_dma(reason="norm weights and lower bounds, once"):
                pool.dma_start(w_norm[:], norm_w.rearrange("(c p) -> p c", p=P)).then_inc(norm_in, 16)
                if hgrn:
                    pool.dma_start(lb[:, 0, :], K.lower_bounds[0].rearrange("(h p) -> p h", p=P)).then_inc(norm_in, 16)
            pool.memset(a[:], 0.0).then_inc(cleared, 1)
            pool.wait_ge(const_in, 48)

            def prepare(h):
                y = h[1]
                if hgrn:
                    wait(pool, "q_silu", h, 1)
                else:
                    qk_loaded(pool, h)
                pool.sem_inc(passed, 1)
                pool.tensor_scalar(q[:, y, :], q[:, y, :], P ** -0.5, None, ALU.mult).then_inc(sem["q_ready"], 1)

            def differences(h):
                wait(pool, "b_made", h, 1)
                for n, m in enumerate(LEVELS):
                    w = width(n + 1)
                    blocks = b[:, 0:w].rearrange("p (n m) -> p n m", m=2 * m)
                    wait(pool, "x_made", h, max(n - 1, 0))
                    pool.tensor_tensor(dec[:, n % 2, 0:w].rearrange("p (n m) -> p n m", m=2 * m), blocks,
                                       blocks[:, :, m - 1:m].broadcast_to([P, w // (2 * m), 2 * m]),
                                       ALU.subtract).then_inc(sem["diffed"], 1)

            def tail(h):
                wait(pool, "tok_out", h, TURNS)
                wait_before(pool, "us_made", h)
                pool.tensor_tensor(v_own[:], v_tok[0:NS, h[1], C:C + 1, :].broadcast_to([NS, NB, V]),
                                   own[:].unsqueeze(2).broadcast_to([NS, NB, V]), ALU.mult).then_inc(sem["own_made"], 1)

            with pool.Fori(0, HEADS // 2) as i:
                prepare((i, 0))
                differences((i, 0))
                prepare((i, 1))
                tail((i, 0))
                differences((i, 1))
                tail((i, 1))

        @block.scalar
        def _(act):
            credit(act, "abs_out e_out soft_out k_exp f_exp log_out q_silu expb_out k_decay tok_out decayed o_out "
                        "mean_out rstd_out gate_silu")

            if hgrn:
                act.wait_ge(lb_made, 1)
                act.activation(lb[:, 2, :], lb[:, 1, :], ACT.Exp).then_inc(lb_made, 1)

            def prepare(h):
                y = h[1]
                loads(act, f_in, h, 16)
                wait_before(act, "turned", h)
                act.activation(soft[:], f_raw[:], ACT.Abs).then_inc(sem["abs_out"], 1)
                wait(act, "abs_out", h, 1)
                act.activation(soft[:], soft[:], ACT.Exp, scale=-1.0).then_inc(sem["e_out"], 1)
                wait(act, "e_out", h, 1)
                act.activation(soft[:], soft[:], ACT.Ln, bias=1.0).then_inc(sem["soft_out"], 1)
                if hgrn:
                    wait(act, "log_sig", h, 1)
                    act.activation(logf[:], logf[:], ACT.Exp).then_inc(sem["f_exp"], 1)
                    wait(act, "neg_made", h, 1)
                    act.activation(k[:, y, :], k[:, y, :], ACT.Exp, scale=-1.0).then_inc(sem["k_exp"], 1)
                    wait(act, "f_clamped", h, 1)
                    act.activation(logf[:], logf[:], ACT.Ln).then_inc(sem["log_out"], 1)
                    qk_loaded(act, h)
                    act.activation(q[:, y, :], q[:, y, :], ACT.Silu).then_inc(sem["q_silu"], 1)
                wait(act, "b_made", h, 1)
                wait_before(act, "k_dec_made", h)
                act.activation(expb[:], b[:], ACT.Exp).then_inc(sem["expb_out"], 1)
                wait(act, "k_diff", h, 1)
                act.activation(soft[:], soft[:], ACT.Exp).then_inc(sem["k_decay"], 1)
                n = 0
                for tok, cs in ((k_tok, 1), (v_tok, VC)):
                    for c in range(cs):
                        for g in range(GROUPS):
                            wait(act, "turned", h, n + 1)
                            if g < GROUPS - 1:
                                act.activation(tok[:, y, 4 * g:4 * g + 4, c * P:(c + 1) * P], TB[n % 2][:],
                                               ACT.Copy).then_inc(sem["tok_out"], 1)
                            else:
                                act.activation(tok[0:NS, y, C, c * P:(c + 1) * P], TB[n % 2][0:NS, 0, :],
                                               ACT.Copy).then_inc(sem["tok_out"], 1)
                            n += 1

            def decays(h):
                for n, m in enumerate(LEVELS):
                    d = dec[:, n % 2, 0:width(n + 1)]
                    wait(act, "diffed", h, n + 1)
                    act.activation(half(d, m, False), half(d, m, False), ACT.Exp, scale=-1.0)
                    act.activation(half(d, m, True), half(d, m, True), ACT.Exp).then_inc(sem["decayed"], 1)

            def tail(h):
                loads(act, gate_in, h, 16)
                act.activation(gate[:], gate[:], ACT.Silu).then_inc(sem["gate_silu"], 1)
                act.wait_ge(stores_done, h[0] * 2 + (h[1] + 1))
                for g in range(3):
                    wait(act, "valued", h, g + 1)
                    for c in range(VC):
                        src = S[2 * c + g][:].rearrange("p c t -> p (c t)") if g < 2 else SS[:, c * NS:(c + 1) * NS]
                        t0, tn = g * 512, (512 if g < 2 else NS)
                        act.activation(o[:, c, t0:t0 + tn], src, ACT.Copy)
                        last = act.activation(sq[:, c, t0:t0 + tn], src, ACT.Square)
                    last.then_inc(sem["o_out"], 1)
                wait_before(act, "normed", h)
                for c, (t0, tn) in enumerate(CHUNKS):
                    wait(act, "mean_in", h, c + 1)
                    act.activation(rstd[:, t0:t0 + tn], mean[c][:, 0:tn], ACT.Ln, scale=1.0 / V,
                                   bias=K.eps[:, 0:1]).then_inc(sem["mean_out"], 1)
                wait(act, "mean_out", h, NC)
                act.activation(rstd[:], rstd[:], ACT.Exp, scale=-0.5).then_inc(sem["rstd_out"], 1)

            with act.Fori(0, HEADS // 2) as i:
                prepare((i, 0))
                decays((i, 0))
                prepare((i, 1))
                tail((i, 0))
                decays((i, 1))
                tail((i, 1))

        @block.vector
        def _(dve):
            credit(dve, "log_sig neg_made f_mixed f_clamped clamped b_made k_ready q_dec_made k_diff k_dec_made "
                        "x_made a_out s_made us_out normed final")
            dve.wait_ge(const_in, 48)
            dve.wait_ge(norm_in, 32 if hgrn else 16)
            dve.wait_ge(cleared, 1)
            if hgrn:
                top, e, pr = lb[:, 1, :], lb[:, 2, :], lb[:, 2, :]
                dve.tensor_tensor(top, lb[:, 0, :], lb[:, 0, :], ALU.subtract).then_inc(lb_made, 1)
                dve.wait_ge(lb_made, 2)
                dve.reciprocal(lb[:, 0, :], e).then_inc(lb_made, 1)
                dve.wait_ge(lb_made, 3)
                dve.tensor_tensor(lb[:, 1, :], e, lb[:, 0, :], ALU.mult).then_inc(lb_made, 1)
                dve.wait_ge(lb_made, 4)
                dve.tensor_tensor(lb[:, 3, :], lb[:, 1, :], lb[:, 1, :], ALU.subtract).then_inc(lb_made, 1)
                dve.wait_ge(lb_made, 5)
                dve.tensor_scalar(lb[:, 4, :], lb[:, 3, :], -1.0, 1.0, ALU.mult, ALU.add).then_inc(lb_made, 1)
                dve.wait_ge(lb_made, 6)

            def prepare(h):
                y = h[1]
                wait(dve, "soft_out", h, 1)
                dve.scalar_tensor_tensor(out=logf[:], in0=f_raw[:], scalar=0.0, in1=soft[:], op0=ALU.min,
                                         op1=ALU.subtract).then_inc(sem["log_sig"], 1)
                if hgrn:
                    dve.scalar_tensor_tensor(out=k[:, y, :], in0=f_raw[:], scalar=0.0, in1=soft[:], op0=ALU.max,
                                             op1=ALU.add).then_inc(sem["neg_made"], 1)
                    dve.tensor_copy(lbh[:, y, :], lb[:, 3:5, row(0, h, 1)].rearrange("p c a -> p (c a)")
                                    ).then_inc(lb_made, 1)
                    dve.wait_ge(lb_made, h[0] * 2 + (h[1] + 7))
                    wait(dve, "f_exp", h, 1)
                    dve.tensor_scalar(logf[:], logf[:], lbh[:, y, 1:2], lbh[:, y, 0:1], ALU.mult, ALU.add
                                      ).then_inc(sem["f_mixed"], 1)
                    wait(dve, "f_mixed", h, 1)
                    dve.tensor_scalar(logf[:], logf[:], TINY, None, ALU.max).then_inc(sem["f_clamped"], 1)
                    wait(dve, "k_exp", h, 1)
                    dve.tensor_scalar(k[:, y, :], k[:, y, :], lbh[:, y, 1:2], None, ALU.mult).then_inc(sem["k_ready"], 1)
                    wait(dve, "log_out", h, 1)
                    dve.tensor_scalar(logf[:], logf[:], 0.0, None, ALU.min).then_inc(sem["clamped"], 1)
                else:
                    wait(dve, "log_sig", h, 1)
                    dve.tensor_scalar(logf[:], logf[:], 1.0 / GATE_TAU, 0.0, ALU.mult, ALU.min
                                      ).then_inc(sem["clamped"], 1)
                wait(dve, "clamped", h, 1)
                dve.tensor_tensor_scan(b[:], starts[:], logf[:], 0.0, ALU.mult, ALU.add).then_inc(sem["b_made"], 1)
                wait(dve, "b_made", h, 1)
                for t0, t1, m in ((0, SEQ, P), (SEQ, T, TS)):
                    bl = b[:, t0:t1].rearrange("p (n m) -> p n m", m=m)
                    last = dve.tensor_tensor(soft[:, t0:t1].rearrange("p (n m) -> p n m", m=m),
                                             bl[:, :, m - 1:m].broadcast_to([P, (t1 - t0) // m, m]), bl, ALU.subtract)
                last.then_inc(sem["k_diff"], 1)
                wait(dve, "expb_out", h, 1)
                wait(dve, "q_ready", h, 1)
                dve.tensor_tensor(q_dec[:, y, :], q[:, y, :], expb[:], ALU.mult).then_inc(sem["q_dec_made"], 1)
                dve.tensor_copy(last_dec[:, y, 0:C], expb[:, P - 1:SEQ:P])
                dve.tensor_copy(last_dec[:, y, C:C + NB], expb[:, SEQ + TS - 1:T:TS])
                wait(dve, "k_decay", h, 1)
                if hgrn:
                    wait(dve, "k_ready", h, 1)
                else:
                    qk_loaded(dve, h)
                dve.tensor_tensor(soft[:], k[:, y, :], soft[:], ALU.mult).then_inc(sem["k_dec_made"], 1)

            def scores(h):
                y = h[1]

                def scale(n):
                    m, w, z = LEVELS[n], width(n + 1), n % 2
                    wait(dve, "decayed", h, n + 1)
                    if n >= 2:
                        wait(dve, "scored", h, n)
                    dve.tensor_tensor(half(x[:, z, 0:w], m, False), half(dec[:, z, 0:w], m, False),
                                      half(k[:, y, 0:w], m, False), ALU.mult)
                    dve.tensor_tensor(half(x[:, z, 0:w], m, True), half(dec[:, z, 0:w], m, True),
                                      half(q[:, y, 0:w], m, True), ALU.mult).then_inc(sem["x_made"], 1)

                def keep(li):
                    wait(dve, "scored", h, li + 1)
                    if li:
                        wait(dve, "a_out", h, li)
                    dve.sem_inc(passed, 1)
                    for g in range(2):
                        last = dve.copy_predicated(a[:, 4 * g:4 * g + 4, :],
                                                   levels[:, li:li + 1, :].broadcast_to([P, 4, P]), S[2 * (li % 2) + g][:])
                    if li < LS:
                        last = dve.copy_predicated(a[0:NS, C, 0:NS], levels[0:NS, li, 0:NS],
                                                   (SS, U)[li % 2][0:NS, 0:NS])
                    last.then_inc(sem["a_out"], 1)

                wait_before(dve, "valued", h)
                for n in range(7):
                    scale(n)
                    keep(n)
                keep(7)

            def tail(h):
                y = h[1]
                for c in range(C):
                    wait(dve, "u_made", h, c + 1)
                    u = U[:, 0:V]
                    if c == 0:
                        dve.wait_ge(stores_done, h[0] * 2 + (h[1] + 1))
                        dve.tensor_copy(state[:, 0, :], u).then_inc(sem["s_made"], 1)
                    else:
                        wait(dve, "s_made", h, c)
                        dve.scalar_tensor_tensor(out=state[:, c, :], in0=state[:, c - 1, :], scalar=last_dec[:, y, c:c + 1],
                                                 in1=u, op0=ALU.mult, op1=ALU.add).then_inc(sem["s_made"], 1)
                wait(dve, "valued", h, 3)
                for j in range(JS):
                    wait(dve, "us_made", h, j + 1)
                    for n in range(512 // V):
                        bi = j * (512 // V) + n
                        last = dve.scalar_tensor_tensor(out=s0[:, bi, :], in0=s0[:, bi, :],
                                                        scalar=last_dec[:, y, C + bi:C + bi + 1],
                                                        in1=U[:, n * V:(n + 1) * V], op0=ALU.mult, op1=ALU.add)
                    last.then_inc(sem["us_out"], 1)
                wait(dve, "rstd_out", h, 1)
                wait(dve, "o_out", h, 3)
                for c in range(VC):
                    dve.scalar_tensor_tensor(out=o[:, c, :], in0=o[:, c, :], scalar=w_norm[:, c:c + 1], in1=rstd[:],
                                             op0=ALU.mult, op1=ALU.mult).then_inc(sem["normed"], 1)
                wait(dve, "gate_silu", h, 1)
                for c in range(VC):
                    wait(dve, "normed", h, c + 1)
                    dve.tensor_tensor(o[:, c, :], o[:, c, :], gate[:, c, :], ALU.mult).then_inc(sem["final"], 1)

            with dve.Fori(0, HEADS // 2) as i:
                prepare((i, 0))
                scores((i, 0))
                prepare((i, 1))
                tail((i, 0))
                scores((i, 1))
                tail((i, 1))

        @block.tensor
        def _(pe):
            credit(pe, "turned scored u_made valued us_made mean_in")

            def prepare(h):
                y, n = h[1], 0
                wait_before(pe, "mean_out", (h[0], 0))
                for src, cs in ((None, 1), (v, VC)):
                    for c in range(cs):
                        x_f = soft[:] if src is None else v[:, c, :]
                        for g in range(GROUPS):
                            if n == 0:
                                wait(pe, "k_dec_made", h, 1)
                            if n == GROUPS:
                                loads(pe, v_in, h, 16)
                            if n < 2:
                                wait_before(pe, "tok_out", h)
                            else:
                                wait(pe, "tok_out", h, n - 1)
                            pe.sem_inc(passed, 1)
                            for i in range(4 if g < GROUPS - 1 else 1):
                                t0 = (4 * g + i) * P
                                tn = min(P, T - t0)
                                last = pe.transpose(TB[n % 2][0:tn, i, :], x_f[:, t0:t0 + tn], K.ident[:])
                            last.then_inc(sem["turned"], 1)
                            n += 1

            def scores(h):
                y = h[1]
                for li in range(L):
                    if li == 0:
                        if hgrn:
                            wait(pe, "k_ready", h, 1)
                        else:
                            qk_loaded(pe, h)
                        wait(pe, "q_ready", h, 1)
                        first, second = k[:, y, :], q[:, y, :]
                        wait_before(pe, "o_out", h)
                        wait_before(pe, "mean_out", h)
                    else:
                        wait(pe, "x_made", h, li)
                        first = second = x[:, (li - 1) % 2, :]
                        if li >= 2:
                            wait(pe, "a_out", h, li - 1)
                    for c in range(C):
                        t = slice(c * P, (c + 1) * P)
                        last = pe.matmul(S[2 * (li % 2) + c // 4][:, c % 4, :], first[:, t], second[:, t],
                                         start=True, stop=True)
                    if li < LS:
                        last = pe.matmul((SS, U)[li % 2][0:NS, 0:NS], first[:, SEQ:T], second[:, SEQ:T],
                                         start=True, stop=True)
                    last.then_inc(sem["scored"], 1)

            def tail(h):
                y = h[1]
                wait(pe, "tok_out", h, TURNS)
                wait(pe, "a_out", h, L)
                wait(pe, "q_dec_made", h, 1)
                wait_before(pe, "us_out", h)
                wait_before(pe, "mean_out", h)
                loads(pe, s0_in, h, 16)
                for c in range(C):
                    for vc in range(VC):
                        last = pe.matmul(S[2 * vc + c // 4][:, c % 4, :], v_tok[:, y, c, vc * P:(vc + 1) * P], a[:, c, :],
                                         start=True, stop=(c == 0))
                    if c:
                        wait(pe, "s_made", h, c)
                    pe.matmul(U[:, 0:V], k_tok[:, y, c, :], v_tok[:, y, c, :], start=True, stop=True
                              ).then_inc(sem["u_made"], 1)
                    for vc in range(VC if c else 0):
                        last = pe.matmul(S[2 * vc + c // 4][:, c % 4, :], state[:, c - 1, vc * P:(vc + 1) * P],
                                         q_dec[:, y, c * P:(c + 1) * P], start=False, stop=True)
                    if c % 4 == 3:
                        last.then_inc(sem["valued"], 1)
                for vc in range(VC):
                    out = SS[:, vc * NS:(vc + 1) * NS]
                    pe.matmul(out, v_tok[0:NS, y, C, vc * P:(vc + 1) * P], a[0:NS, C, 0:NS], start=True, stop=False)
                    for bi in range(NB):
                        t = slice(bi * TS, (bi + 1) * TS)
                        last = pe.matmul(out[:, t], s0[:, bi, vc * P:(vc + 1) * P],
                                         q_dec[:, y, SEQ + bi * TS:SEQ + (bi + 1) * TS], start=False,
                                         stop=(bi == NB - 1))
                last.then_inc(sem["valued"], 1)
                wait(pe, "own_made", h, 1)
                for j in range(JS):
                    if j == 0:
                        wait(pe, "s_made", h, C)
                    else:
                        wait(pe, "us_out", h, j)
                    n = 512 // V
                    pe.matmul(U[:], k_tok[0:NS, y, C, :], v_own[:, j * n:(j + 1) * n, :].rearrange("p b v -> p (b v)"),
                              start=True, stop=True).then_inc(sem["us_made"], 1)
                wait(pe, "o_out", h, 3)
                for c, (t0, tn) in enumerate(CHUNKS):
                    if c == 1:
                        wait(pe, "us_out", h, JS)
                    if c == 0 and y == 0:
                        wait(pe, "tok_out", (h[0], 1), TURNS)
                    for vc in range(VC):
                        last = pe.matmul(mean[c][:, 0:tn], K.ones[:], sq[:, vc, t0:t0 + tn], start=(vc == 0),
                                         stop=(vc == VC - 1))
                    last.then_inc(sem["mean_in"], 1)

            with pe.Fori(0, HEADS // 2) as i:
                prepare((i, 0))
                scores((i, 0))
                prepare((i, 1))
                tail((i, 0))
                scores((i, 1))
                tail((i, 1))


def latent_attention(nc, K):
    with ExitStack() as stack:
        M = Kit()

        def keep(name, shape, dt=F32):
            return stack.enter_context(nc.sbuf_tensor(name, shape, dt))

        M.qn, M.qpe = keep("mla_qn", [P, HEADS, T]), keep("mla_qpe", [P, 2, T])
        M.ckv, M.kpe = keep("mla_ckv", [P, 2, T]), keep("mla_kpe", [P, T])
        latent_stage(nc, K, M)
        M.wuv, M.rows = keep("mla_wuv", [P, 2, HEADS, P]), keep("mla_rows", [P, 9, LAT])
        M.qs = keep("mla_qs", [P, 3, NB, HEADS, TS])
        with nc.sbuf_tensor("mla_kn", [P, HEADS, SEQ], F32) as M.kn,                 nc.sbuf_tensor("mla_v", [P, 8, HEADS * P], F32) as M.v:
            keys_stage(nc, K, M)
            prompt_attention_stage(nc, K, M)
        sample_attention_stage(nc, K, M)



def program(nc, K):
    with ExitStack() as stack:
        def keep(name, shape, dt=F32):
            return stack.enter_context(nc.sbuf_tensor(name, shape, dt))

        K.xT = keep("xT", [P, KD, T])
        K.ident, K.ones = keep("ident", [P, P]), keep("ones", [P, P])
        K.norms, K.eps = keep("norms", [P, 5, KD]), keep("eps", [P, 1])
        load_stage(nc, K)
        project_stage(nc, K, "even", K.w_in_even[0], EVEN_COLS, norm=0, z=K.z)
        latent_attention(nc, K)
        scan_stage(nc, K, "hgrn", True, (Z_Q, None, Z_I, Z_G, Z_F), K.hgrn_norm[0], K.state_hgrn[0],
                   K.hgrn_prompt, K.hgrn_sample, K.mix)
        project_stage(nc, K, "evenout", K.w_out_even[0], D, mix=K.mix)
        mlp_stage(nc, K, "mlp0", 1, K.w_up[0], K.w_down[0])
        project_stage(nc, K, "odd", K.w_in_odd[0], ODD_COLS, norm=2, z=K.z)
        alpha_stage(nc, K)
        scan_stage(nc, K, "gla", False, (G_Q, G_K, G_V, G_R, G_GATE), K.gla_norm[0], K.state_gla[0],
                   K.gla_prompt, K.gla_sample, K.mix)
        project_stage(nc, K, "oddout", K.w_out_odd[0], D, mix=K.mix)
        mlp_stage(nc, K, "mlp1", 3, K.w_up[1], K.w_down[1])
        store_stage(nc, K)



def constants():
    f = np.float32
    pos = np.concatenate([np.arange(SEQ)] + [PAGES * P + np.arange(TS)] * NB)
    inv = (ROPE_THETA ** (-np.arange(ROPE // 2) / (ROPE // 2))).astype(f)
    ang = (pos.astype(f)[None, :] * inv[:, None]).astype(np.float64)
    cos = np.tile(np.cos(ang), (4, 1)).astype(f)
    sin = np.tile(np.concatenate([-np.sin(ang), np.sin(ang)]), (2, 1)).astype(f)
    rot = np.zeros((P, P), f)
    rot[np.arange(P) ^ (ROPE // 2), np.arange(P)] = 1
    i = np.arange(P)
    s, t = i[:, None], i[None, :]
    causal = np.where(t <= s, 0, NEG).astype(f)
    tok, row = np.arange(NS), np.arange(HEADS * TS)
    seen = ((tok[None, None, :] // TS == np.arange(NB)[None, :, None])
            & (tok[None, None, :] % TS <= (row % TS)[:, None, None]))
    pairs = [s == t] + [(s // (2 * m) == t // (2 * m)) & (s % (2 * m) < m) & (t % (2 * m) >= m) for m in LEVELS]
    starts = np.ones((P, T), f)
    starts[:, 0:SEQ:P] = 0
    starts[:, SEQ::TS] = 0
    return dict(c_ident=np.eye(P, dtype=f), c_cos=cos, c_sin=sin, c_rot=rot, c_causal=causal,
                c_newmask=np.where(seen, 0, NEG).astype(f), c_levels=np.stack(pairs, 1).astype(np.int32),
                c_starts=starts, c_own=(tok[:, None] // TS == np.arange(NB)[None, :]).astype(f))


OUTPUTS = dict(y_prompt=(1, SEQ, D), y_sample=(NB, TS, D), mla_rows_prompt=(1, 1, SEQ, LAT),
               mla_rows_sample=(1, NB, TS, LAT), hgrn_state_prompt=(1, 1, HEADS, P, P),
               hgrn_state_sample=(1, NB, HEADS, P, P), gla_state_prompt=(1, 1, HEADS, P, 2 * P),
               gla_state_sample=(1, NB, HEADS, P, 2 * P))


def bind(nc, a, o):
    K = Kit()
    K.x_prompt, K.x_sample = a["x_prompt"][0], a["x_sample"].rearrange("b t d -> (b t) d")
    K.cache, K.page_table = a["cache_mla"][0], a["page_table"].rearrange("(a b) p -> a (b p)", a=1)
    K.state_hgrn, K.state_gla = a["state_hgrn"], a["state_gla"]
    K.norm_mix, K.norm_mlp, K.norm_final = a["norm_mix"], a["norm_mlp"], a["norm_final"]
    K.w_in_even, K.w_out_even, K.w_in_odd, K.w_out_odd = a["w_in_even"], a["w_out_even"], a["w_in_odd"], a["w_out_odd"]
    K.w_up, K.w_down, K.w_uq, K.w_uk, K.w_uv = a["w_up"], a["w_down"], a["w_uq"], a["w_uk"], a["w_uv"]
    K.q_norm, K.kv_norm, K.hgrn_norm, K.gla_norm = a["q_norm"], a["kv_norm"], a["hgrn_norm"], a["gla_norm"]
    K.lower_bounds, K.w_alpha2, K.b_alpha = a["lower_bounds"], a["w_alpha2"], a["b_alpha"]
    K.c_ident, K.c_cos, K.c_sin, K.c_rot, K.c_causal = a["c_ident"], a["c_cos"], a["c_sin"], a["c_rot"], a["c_causal"]
    K.c_newmask, K.c_levels, K.c_starts, K.c_own = a["c_newmask"], a["c_levels"], a["c_starts"], a["c_own"]
    K.z = nc.dram_tensor("projections", [Z_ROWS, T], F32, kind="Internal").ap()
    K.mix = nc.dram_tensor("mixed", [D, T], F32, kind="Internal").ap()
    K.y_prompt, K.y_sample = o["y_prompt"][0], o["y_sample"].rearrange("b t d -> (b t) d")
    K.rows_prompt = o["mla_rows_prompt"][0, 0]
    K.rows_sample = o["mla_rows_sample"][0].rearrange("b t c -> (b t) c")
    K.hgrn_prompt, K.hgrn_sample = o["hgrn_state_prompt"][0, 0], o["hgrn_state_sample"][0]
    K.gla_prompt, K.gla_sample = o["gla_state_prompt"][0, 0], o["gla_state_sample"][0]
    return K


def kernel(**inputs):
    import concourse.bacc as bacc
    from concourse.bass_utils import run_bass_kernel_spmd

    nc = bacc.Bacc("TRN2", target_bir_lowering=False, num_devices=1)
    arrays = {f"in_{n}": np.ascontiguousarray(x) for n, x in {**inputs, **constants()}.items()}
    a = {n[3:]: nc.dram_tensor(n, x.shape, mybir.dt.from_np(x.dtype), kind="ExternalInput").ap()
         for n, x in arrays.items()}
    o = {n: nc.dram_tensor(f"out_{n}", shape, F32, kind="ExternalOutput").ap() for n, shape in OUTPUTS.items()}
    program(nc, bind(nc, a, o))
    result = run_bass_kernel_spmd(nc, [arrays], core_ids=[0]).results[0]
    return tuple(result[f"out_{n}"] for n in OUTPUTS)
```

```python
from collections import namedtuple
from contextlib import ExitStack

import numpy as np

import concourse.bass as bass
from concourse import mybir

F32 = mybir.dt.float32
F32R = mybir.dt.float32r
I32 = mybir.dt.int32
ACT = mybir.ActivationFunctionType
ALU = mybir.AluOpType
AX = mybir.AxisListType

P = 128
D = 1024
KD = D // P
SEQ = 1024
NB, TS = 8, 8
NS = NB * TS
T = SEQ + NS
HEADS = 4
CHUNKS = [(0, 384), (384, 352), (736, 352)]
NC = len(CHUNKS)
FF = 4096
EVEN_COLS = 2752
ODD_COLS = 3088
Q_LORA, KV_LORA, ROPE = 384, 256, 64
LAT = KV_LORA + ROPE
PAGES = 64
PG = 4
SCALE = (128 + ROPE) ** -0.5
ROPE_THETA = 10000.0
NEG = -1e30
EPS = 1e-6
TINY = 1e-30
GATE_RANK, GATE_TAU = 16, 16.0
LEVELS = [1, 2, 4, 8, 16, 32, 64]

Z_Q, Z_F, Z_I, Z_G, Z_CQ, Z_CKV, Z_KR = 0, 512, 1024, 1536, 2048, 2432, 2688
G_Q, G_K, G_V, G_R, G_A, G_GATE = 0, 512, 1024, 2048, 3072, 3088
Z_ROWS = 3600


class Kit:
    pass


class Stage:

    def __init__(self, nc, name):
        self.nc, self.name, self.stack, self.sems = nc, name, ExitStack(), []

    def __enter__(self):
        return self

    def __exit__(self, *a):
        self.stack.__exit__(*a)
        self.nc.clear_and_free_semaphores(self.sems)
        self.nc.all_engine_barrier()

    def sb(self, name, shape, dt=F32):
        return self.stack.enter_context(self.nc.sbuf_tensor(f"{self.name}_{name}", shape, dt))

    def ps(self, name, shape, dt=F32):
        return self.stack.enter_context(self.nc.psum_tensor(f"{self.name}_{name}", shape, dt))

    def sem(self, name):
        self.sems.append(self.nc.alloc_semaphore(f"{self.name}_{name}"))
        return self.sems[-1]

    def block(self):
        return self.stack.enter_context(self.nc.Block())


def r32(ap):
    return ap.bitcast(F32)


def mm3(pe, out, w_hi, w_lo, x_hi, x_lo, first, last):
    pe.matmul(out, w_hi, x_hi, start=first, stop=False)
    pe.matmul(out, w_hi, x_lo, start=False, stop=False)
    return pe.matmul(out, w_lo, x_hi, start=False, stop=last)


def wait_apart(eng, sem, value, spare):
    eng.wait_ge(sem, value)
    eng.sem_inc(spare, 1)



def load_stage(nc, K):
    with Stage(nc, "load") as s:
        xin = s.sb("xin", [P, 2, D])
        tp = [s.ps(f"tp{i}", [P, 4, P]) for i in range(4)]
        const_in, ident_in, xin_in = s.sem("const_in"), s.sem("ident_in"), [s.sem("xin_in0"), s.sem("xin_in1")]
        xin_used, turned = s.sem("xin_used"), s.sem("turned")
        copied_lo, copied_hi = s.sem("copied_lo"), s.sem("copied_hi")
        block = s.block()
        xp, xs = K.x_prompt, K.x_sample

        @block.sync
        def _(sp):
            sp.dma_start(K.ident[:], K.c_ident).then_inc(ident_in, 16)
            for i in range(2):
                sp.dma_start(xin[:, i, :], xp[i * P:(i + 1) * P, :]).then_inc(xin_in[i], 16)
            with sp.Fori(1, 4) as j:
                for i in range(2):
                    sp.wait_ge(xin_used, 2 * j + (i - 1))
                    sp.dma_start(xin[:, i, :], xp[bass.ds(j * 2 * P + i * P, P), :]).then_inc(xin_in[i], 16)
            sp.wait_ge(xin_used, 7)
            sp.dma_start(xin[0:NS, 0, :], xs).then_inc(xin_in[0], 16)

        @block.gpsimd
        def _(pool):
            pool.memset(K.ones[:], 1.0)
            pool.memset(K.eps[:], EPS)
            with nc.allow_non_contiguous_dma(reason="a column of each norm weight, once"):
                for n, w in enumerate([K.norm_mix[0], K.norm_mlp[0], K.norm_mix[1], K.norm_mlp[1]]):
                    pool.dma_start(K.norms[:, n, :], w.rearrange("(k p) -> p k", p=P)).then_inc(const_in, 16)
            pool.wait_ge(const_in, 4 * 16)

        @block.tensor
        def _(pe):
            def turn(tile, i, rows):
                for half in range(2):
                    pe.wait_ge(copied_lo if half == 0 else copied_hi, tile + 1)
                    for k in range(4):
                        c = (4 * half + k) * P
                        last = pe.transpose(tp[2 * i + half][:, k, 0:rows], xin[0:rows, i, c:c + P],
                                            K.ident[0:rows, 0:rows])
                    last.then_inc(turned, 1)
            pe.wait_ge(ident_in, 16)
            with pe.Fori(0, 4) as j:
                for i in range(2):
                    pe.wait_ge(xin_in[i], j * 16 + 16)
                    turn(j * 2 + i, i, P)
            pe.wait_ge(xin_in[0], 5 * 16)
            turn(8, 0, NS)

        def copy_out(eng, copy, half, copied):
            eng.sem_inc(copied, 2)
            dst = K.xT[:, 4 * half:4 * half + 4, :]
            with eng.Fori(0, 4) as j:
                for i in range(2):
                    eng.wait_ge(turned, j * 4 + (2 * i + half + 1))
                    copy(dst[:, :, bass.ds(j * 2 * P + i * P, P)], tp[2 * i + half][:]).then_inc(copied, 1)
                    if half:
                        eng.sem_inc(xin_used, 1)
            eng.wait_ge(turned, 17 + half)
            copy(dst[:, :, SEQ:T], tp[half][:, :, 0:NS]).then_inc(copied, 1)

        @block.scalar
        def _(act):
            copy_out(act, lambda o, x: act.activation(o, x, ACT.Copy), 0, copied_lo)

        @block.vector
        def _(dve):
            copy_out(dve, lambda o, x: dve.tensor_copy(o, x), 1, copied_hi)


def store_stage(nc, K):
    with Stage(nc, "store") as s:
        y, sq = s.sb("y", [P, 4, D]), s.sb("sq", [P, D])
        mean, root, rstd = s.sb("mean", [P, 9]), s.sb("root", [P, 9]), s.sb("rstd", [P, 9])
        weight = s.sb("weight", [P, D])
        tp = [s.ps(f"tp{i}", [P, D]) for i in range(4)]
        weight_in = s.sem("weight_in")
        turned, squared, rooted, inverted, normed = (s.sem(n) for n in ("turned", "squared", "rooted", "inverted", "normed"))
        y_out = [s.sem(f"y_out{i}") for i in range(4)]
        block = s.block()
        yp, ys = K.y_prompt, K.y_sample
        TILES = 9

        def rows(tile):
            return P if tile < 8 else NS

        @block.tensor
        def _(pe):
            for tile in range(TILES):
                if tile >= 4:
                    pe.wait_ge(normed, tile - 3)
                for k in range(KD):
                    last = pe.transpose(tp[tile % 4][0:rows(tile), k * P:(k + 1) * P],
                                        K.xT[:, k, tile * P:tile * P + rows(tile)], K.ident[:])
                last.then_inc(turned, 1)

        @block.scalar
        def _(act):
            for tile in range(TILES):
                n = rows(tile)
                act.wait_ge(turned, tile + 1)
                if tile:
                    act.wait_ge(squared, tile)
                act.activation(sq[0:n], tp[tile % 4][0:n], ACT.Square, accum_out=mean[0:n, tile:tile + 1]).then_inc(squared, 1)
                act.wait_ge(squared, tile + 1)
                act.activation(root[0:n, tile:tile + 1], mean[0:n, tile:tile + 1], ACT.Sqrt, scale=1.0 / D,
                               bias=K.eps[0:n, 0:1]).then_inc(rooted, 1)

        @block.vector
        def _(dve):
            dve.wait_ge(weight_in, 16)
            for tile in range(TILES):
                n = rows(tile)
                dve.wait_ge(rooted, tile + 1)
                dve.reciprocal(rstd[0:n, tile:tile + 1], root[0:n, tile:tile + 1]).then_inc(inverted, 1)
                dve.wait_ge(inverted, tile + 1)
                if tile >= 4:
                    dve.wait_ge(y_out[tile % 4], 16 * (tile // 4))
                dve.scalar_tensor_tensor(out=y[0:n, tile % 4, :], in0=tp[tile % 4][0:n], scalar=rstd[0:n, tile:tile + 1],
                                         in1=weight[0:n, :], op0=ALU.mult, op1=ALU.mult).then_inc(normed, 1)

        @block.sync
        def _(sp):
            sp.dma_start(weight[:], K.norm_final.rearrange("(a d) -> a d", a=1).broadcast_to([P, D])).then_inc(weight_in, 16)
            for tile in range(TILES):
                sp.wait_ge(normed, tile + 1)
                dst = yp[tile * P:(tile + 1) * P, :] if tile < 8 else ys
                sp.dma_start(dst, y[0:rows(tile), tile % 4, :]).then_inc(y_out[tile % 4], 16)
            for i in range(4):
                sp.wait_ge(y_out[i], 16 * ((TILES + 3 - i) // 4))


class Norm:
    SUMS = [(0, 512), (512, 512), (1024, NS)]

    def __init__(self, s, K):
        self.K = K
        self.sq, self.acc, self.rstd = s.sb("sq", [P, 2, T]), s.sb("acc", [P, T]), s.sb("rstd", [P, T])
        self.sq_pool = s.sb("sq_pool", [P, 2, T])
        self.psum = [s.ps("sum0", [P, 512]), s.ps("sum1", [P, 512])]
        self.squared, self.sq_used = s.sem("squared"), s.sem("sq_used")
        self.pool_squared, self.pool_added = s.sem("pool_squared"), s.sem("pool_added")
        self.mean_in, self.logged, self.rstd_ready = s.sem("mean_in"), s.sem("logged"), s.sem("rstd_ready")

    def act_squares(self, act):
        act.sem_inc(self.sq_used, 2)
        for k in range(KD - 2):
            act.wait_ge(self.sq_used, k + 1)
            act.activation(self.sq[:, k % 2, :], self.K.xT[:, k, :], ACT.Square).then_inc(self.squared, 1)

    def pool_squares(self, pool):
        for i in range(2):
            x = self.K.xT[:, KD - 2 + i, :]
            pool.tensor_tensor(self.sq_pool[:, i, :], x, x, ALU.mult).then_inc(self.pool_squared, 1)
        pool.wait_ge(self.pool_squared, 2)
        pool.tensor_tensor(self.sq_pool[:, 0, :], self.sq_pool[:, 0, :], self.sq_pool[:, 1, :], ALU.add
                           ).then_inc(self.pool_added, 1)

    def dve_sum(self, dve):
        for k in range(KD - 2):
            dve.wait_ge(self.squared, k + 1)
            if k == 0:
                dve.tensor_copy(self.acc[:], self.sq[:, 0, :]).then_inc(self.sq_used, 1)
            else:
                dve.wait_ge(self.sq_used, 2 + k)
                dve.tensor_tensor(self.acc[:], self.acc[:], self.sq[:, k % 2, :], ALU.add).then_inc(self.sq_used, 1)

    def pe(self, pe):
        pe.wait_ge(self.sq_used, KD)
        pe.wait_ge(self.pool_added, 1)
        for c, (t0, tn) in enumerate(self.SUMS):
            if c == 2:
                pe.wait_ge(self.logged, 1)
            out = self.psum[c % 2][:, 0:tn]
            pe.matmul(out, self.K.ones[:], self.acc[:, t0:t0 + tn], start=True, stop=False)
            pe.matmul(out, self.K.ones[:], self.sq_pool[:, 0, t0:t0 + tn], start=False, stop=True
                      ).then_inc(self.mean_in, 1)

    def act_rstd(self, act):
        for c, (t0, tn) in enumerate(self.SUMS):
            act.wait_ge(self.mean_in, c + 1)
            act.activation(self.rstd[:, t0:t0 + tn], self.psum[c % 2][:, 0:tn], ACT.Ln,
                           scale=1.0 / D, bias=self.K.eps[:, 0:1]).then_inc(self.logged, 1)
        act.wait_ge(self.logged, len(self.SUMS))
        act.activation(self.rstd[:], self.rstd[:], ACT.Exp, scale=-0.5).then_inc(self.rstd_ready, 1)


def split_x(K, norm, x_hi, x_lo):
    def high(act, k, done):
        act.activation(x_hi[:, k, :], K.xT[:, k, :], ACT.Copy, scale=K.norms[:, norm, k:k + 1]).then_inc(done, 1)

    def low(dve, k, done):
        dve.scalar_tensor_tensor(out=x_lo[:, k, :], in0=K.xT[:, k, :], scalar=K.norms[:, norm, k:k + 1],
                                 in1=r32(x_hi[:, k, :]), op0=ALU.mult, op1=ALU.subtract).then_inc(done, 1)

    return high, low


class FirstWeights:

    def __init__(self, s, raw, w_hi, w_lo, raw_in, hi_done, lo_done):
        self.views, self.raw_in, self.hi_done, self.lo_done = (raw, w_hi, w_lo), raw_in, hi_done, lo_done
        self.half_in, self.half_hi, self.half_lo = s.sem("half_in"), s.sem("half_hi"), s.sem("half_lo")

    def half(self, i):
        return [v[:, i * 512:(i + 1) * 512] for v in self.views]

    def load(self, sp, src):
        for i, done in enumerate((self.half_in, self.raw_in)):
            sp.dma_start(self.half(i)[0].rearrange("p (k n) -> p k n", n=P), src[:, 4 * i:4 * i + 4, :]).then_inc(done, 16)

    def high(self, act):
        for i, (loaded, done) in enumerate(((self.half_in, self.half_hi), (self.raw_in, self.hi_done))):
            raw, hi, _ = self.half(i)
            act.wait_ge(loaded, 16)
            act.activation(hi, raw, ACT.Copy).then_inc(done, 1)

    def low(self, dve):
        for i, (ready, done) in enumerate(((self.half_hi, self.half_lo), (self.hi_done, self.lo_done))):
            raw, hi, lo = self.half(i)
            dve.wait_ge(ready, 1)
            dve.tensor_tensor(lo, raw, r32(hi), ALU.subtract).then_inc(done, 1)


def first_two_groups(pe, bank, w, x_hi, x_lo, first, xlo_done, summed, norm):
    LAG = 2
    for step in range(KD + LAG):
        for i, k in ((0, step), (1, step - LAG)):
            if not 0 <= k < KD:
                continue
            if k == 0:
                pe.wait_ge(*((first.half_lo, 1) if i == 0 else (first.lo_done, 2)))
            if i == 0 and k == 4:
                pe.wait_ge(first.lo_done, 1)
            if i == 0:
                pe.wait_ge(xlo_done, k + 1)
            for c, (t0, tn) in enumerate(CHUNKS):
                last = mm3(pe, bank[i][c][:, 0:tn], w(i)[0][:, k, :], w(i)[1][:, k, :],
                           x_hi[:, k, t0:t0 + tn], x_lo[:, k, t0:t0 + tn], k == 0, k == KD - 1)
                if k == KD - 1:
                    last.then_inc(summed, 1)
        if norm is not None and step == KD - 2:
            norm.pe(pe)



def project_stage(nc, K, name, w, cols, norm=None, z=None, mix=None):
    pairs = cols // P // 2
    tail = [(col, min(P, cols - col)) for col in range(2 * pairs * P, cols, P)]
    with Stage(nc, name) as s:
        x_hi, x_lo = s.sb("x_hi", [P, KD, T], F32R), s.sb("x_lo", [P, KD, T], F32R)
        raw = s.sb("raw", [P, 2, KD, P])
        w_hi, w_lo = s.sb("w_hi", [P, 2, KD, P], F32R), s.sb("w_lo", [P, 2, KD, P], F32R)
        bank = [[s.ps(f"bank{i}{c}", [P, 512]) for c in range(NC)] for i in range(2)]
        raw_in = [s.sem("raw_in0"), s.sem("raw_in1")]
        hi_done, lo_done = s.sem("hi_done"), s.sem("lo_done")
        summed, evacuated = s.sem("summed"), s.sem("evacuated")
        xhi_done, xlo_done = s.sem("xhi_done"), s.sem("xlo_done")
        z_out = [s.sem("z_out0"), s.sem("z_out1")]
        MIXES = 4
        mix_in = [s.sem(f"mix_in{i}") for i in range(MIXES)]
        n = None
        if mix is None:
            zout, n = s.sb("zout", [P, 2, T]), Norm(s, K)
            rstd = n.rstd
            high, low = split_x(K, norm, x_hi, x_lo)
        else:
            mixed = s.sb("mixed", [P, MIXES, T])
        first = FirstWeights(s, *(v[:, 0].rearrange("p k n -> p (k n)") for v in (raw, w_hi, w_lo)),
                             raw_in[0], hi_done, lo_done)
        block = s.block()
        wv = w.rearrange("(k p) n -> p k n", p=P)

        @block.sync
        def _(sp):
            def load(g, i, width=P):
                sp.dma_start(raw[:, i, :, 0:width], wv[:, :, bass.ds(g * P, width)]).then_inc(raw_in[i], 16)

            def store(g, i, width=P):
                sp.wait_ge(evacuated, 3 * g + 9)
                sp.dma_start(z[bass.ds(g * P, width), :], zout[0:width, i, :]).then_inc(z_out[i], 16)

            first.load(sp, wv[:, :, 0:P])
            load(1, 1)
            if mix is not None:
                for k in range(KD):
                    if k >= MIXES:
                        sp.wait_ge(xlo_done, k - MIXES + 1)
                    sp.dma_start(mixed[:, k % MIXES, :], mix[k * P:(k + 1) * P, :]).then_inc(mix_in[k % MIXES], 16)
            with sp.Fori(1, pairs) as j:
                for i in range(2):
                    sp.wait_ge(lo_done, j * 2 + (i - 1))
                    load(j * 2 + i, i)
                    if z is not None:
                        store(j * 2 + (i - 2), i)
            for m, (col, width) in enumerate(tail):
                g = 2 * pairs + m
                sp.wait_ge(lo_done, g - 1)
                load(g, g % 2, width)
            if z is not None:
                for g in range(2 * pairs - 2, 2 * pairs + len(tail)):
                    store(g, g % 2, tail[g - 2 * pairs][1] if g >= 2 * pairs else P)
                total = 2 * pairs + len(tail)
                sp.wait_ge(z_out[0], 16 * ((total + 1) // 2))
                sp.wait_ge(z_out[1], 16 * (total // 2))

        @block.scalar
        def _(act):
            def split(i, width=P):
                act.activation(w_hi[:, i, :, 0:width], raw[:, i, :, 0:width], ACT.Copy).then_inc(hi_done, 1)

            for k in range(KD):
                if k == 2:
                    first.high(act)
                if k == 4:
                    act.wait_ge(raw_in[1], 16)
                    split(1)
                if mix is None:
                    high(act, k, xhi_done)
                else:
                    act.wait_ge(mix_in[k % MIXES], 16 * (k // MIXES + 1))
                    act.activation(x_hi[:, k, :], mixed[:, k % MIXES, :], ACT.Copy).then_inc(xhi_done, 1)
            def split_later(j, i):
                act.wait_ge(raw_in[i], j * 16 + 16)
                act.wait_ge(summed, j * 6 + (3 * i - 3))
                split(i)

            if n is not None:
                n.act_squares(act)
                n.act_rstd(act)
            with act.Fori(1, pairs) as j:
                for i in range(2):
                    split_later(j, i)
            for m, (col, width) in enumerate(tail):
                g = 2 * pairs + m
                act.wait_ge(raw_in[g % 2], 16 * (g // 2 + 1))
                act.wait_ge(summed, 3 * g - 3)
                split(g % 2, width)

        @block.vector
        def _(dve):
            for k in range(KD):
                if k == 2:
                    first.low(dve)
                dve.wait_ge(xhi_done, k + 1)
                if mix is None:
                    low(dve, k, xlo_done)
                else:
                    dve.tensor_tensor(x_lo[:, k, :], mixed[:, k % MIXES, :], r32(x_hi[:, k, :]),
                                      ALU.subtract).then_inc(xlo_done, 1)
            if n is not None:
                n.dve_sum(dve)
                dve.wait_ge(n.rstd_ready, 1)

            def evacuate(g, i, width=P):
                for c, (t0, tn) in enumerate(CHUNKS):
                    dve.wait_ge(summed, 3 * g + (c + 1))
                    if mix is None:
                        dve.tensor_tensor(zout[0:width, i, t0:t0 + tn], bank[i][c][0:width, 0:tn],
                                          rstd[0:width, t0:t0 + tn], ALU.mult).then_inc(evacuated, 1)
                    else:
                        x = K.xT[:, bass.ds(g, 1), t0:t0 + tn].rearrange("p k t -> p (k t)")
                        dve.tensor_tensor(x, x, bank[i][c][:, 0:tn], ALU.add).then_inc(evacuated, 1)

            for i in range(2):
                evacuate(i, i)
            with dve.Fori(1, pairs) as j:
                for i in range(2):
                    if z is not None:
                        dve.wait_ge(z_out[i], j * 16)
                    evacuate(j * 2 + i, i)
            for m, (col, width) in enumerate(tail):
                g = 2 * pairs + m
                if z is not None:
                    dve.wait_ge(z_out[g % 2], 16 * (g // 2))
                evacuate(g, g % 2, width)

        @block.gpsimd
        def _(pool):
            def split(g, i, width=P):
                pool.wait_ge(hi_done, g + 1)
                pool.tensor_tensor(w_lo[:, i, :, 0:width], raw[:, i, :, 0:width],
                                   r32(w_hi[:, i, :, 0:width]), ALU.subtract).then_inc(lo_done, 1)

            pool.wait_ge(lo_done, 1)
            split(1, 1)
            if n is not None:
                n.pool_squares(pool)
            with pool.Fori(1, pairs) as j:
                for i in range(2):
                    split(j * 2 + i, i)
            for m, (col, width) in enumerate(tail):
                split(2 * pairs + m, (2 * pairs + m) % 2, width)

        @block.tensor
        def _(pe):
            pe.sem_inc(evacuated, 6)
            first_two_groups(pe, bank, lambda i: (w_hi[:, i], w_lo[:, i]), x_hi, x_lo, first, xlo_done, summed, n)

            def group(g, i):
                pe.wait_ge(lo_done, g + 1)
                for c, (t0, tn) in enumerate(CHUNKS):
                    pe.wait_ge(evacuated, 3 * g + (c + 1))
                    for k in range(KD):
                        last = mm3(pe, bank[i][c][:, 0:tn], w_hi[:, i, k, :], w_lo[:, i, k, :],
                                   x_hi[:, k, t0:t0 + tn], x_lo[:, k, t0:t0 + tn], k == 0, k == KD - 1)
                    last.then_inc(summed, 1)

            with pe.Fori(1, pairs) as j:
                for i in range(2):
                    group(j * 2 + i, i)
            for m in range(len(tail)):
                group(2 * pairs + m, (2 * pairs + m) % 2)



def mlp_stage(nc, K, name, norm, w_up, w_down):
    UP, DOWN = 4, KD
    blocks = FF // (UP * P)
    with Stage(nc, name) as s:
        x_hi, x_lo = s.sb("x_hi", [P, KD, T], F32R), s.sb("x_lo", [P, KD, T], F32R)
        a_hi, a_lo = s.sb("a_hi", [P, UP, T], F32R), s.sb("a_lo", [P, UP, T], F32R)
        raw = s.sb("raw", [P, 2, KD * P])
        w_hi, w_lo = s.sb("w_hi", [P, 2, KD * P], F32R), s.sb("w_lo", [P, 2, KD * P], F32R)
        bank = [[s.ps(f"bank{i}{c}", [P, 512]) for c in range(NC)] for i in range(2)]
        n = Norm(s, K)
        rstd = n.rstd
        high, low_x = split_x(K, norm, x_hi, x_lo)
        relu, act2 = s.sb("relu", [P, 2, 384]), s.sb("act2", [P, 2, 384])
        raw_in = [s.sem("raw_in0"), s.sem("raw_in1")]
        hi_done, lo_done = s.sem("hi_done"), s.sem("lo_done")
        up_summed, up_out = s.sem("up_summed"), s.sem("up_out")
        down_summed, down_out = s.sem("down_summed"), s.sem("down_out")
        squared, ahi_done, alo_done = s.sem("squared_a"), s.sem("ahi_done"), s.sem("alo_done")
        xhi_done, xlo_done = s.sem("xhi_done"), s.sem("xlo_done")
        first_tile = FirstWeights(s, raw[:, 0, :], w_hi[:, 0, :], w_lo[:, 0, :], raw_in[0], hi_done, lo_done)
        block = s.block()
        up_v = w_up.rearrange("(k p) f -> p k f", p=P)
        down_v = w_down.rearrange("(f p) d -> p f d", p=P)
        TILES = UP + DOWN // 2
        UPC, DNC = UP * NC, DOWN * NC

        def used_before(j, t):
            u = t - 2
            if u < 0:
                return down_summed, (j - 1) * DNC + NC * 2 * (TILES + u - UP + 1)
            if u < UP:
                return up_summed, j * UPC + NC * (u + 1)
            return down_summed, j * DNC + NC * 2 * (u - UP + 1)

        @block.sync
        def _(sp):
            def load(j, t):
                i = t % 2
                if t < UP:
                    src = up_v[:, :, bass.ds(j * (UP * P) + t * P, P)]
                    dst = raw[:, i, :].rearrange("p (k n) -> p k n", k=KD)
                else:
                    src = down_v[:, bass.ds(j * UP, UP), (t - UP) * 256:(t - UP + 1) * 256]
                    dst = raw[:, i, :].rearrange("p (f n) -> p f n", f=UP)
                sp.dma_start(dst, src).then_inc(raw_in[i], 16)

            def body(j, first=False):
                for t in range(TILES):
                    if not (first and t < 2):
                        sp.wait_ge(lo_done, j * TILES + (t - 1))
                    if first and t == 0:
                        first_tile.load(sp, up_v[:, :, 0:P])
                    else:
                        load(j, t)

            body(0, True)
            with sp.Fori(1, blocks) as j:
                body(j)

        @block.scalar
        def _(act):
            def split(j, t, first=False):
                act.wait_ge(raw_in[t % 2], j * (16 * TILES // 2) + 16 * (t // 2 + 1))
                if not (first and t < 2):
                    act.wait_ge(*used_before(j, t))
                act.activation(w_hi[:, t % 2, :], raw[:, t % 2, :], ACT.Copy).then_inc(hi_done, 1)

            def square(j, u):
                for c, (t0, tn) in enumerate(CHUNKS):
                    m = u * NC + c
                    act.wait_ge(up_out, j * UPC + (m + 1))
                    act.wait_ge(alo_done, j * UPC + (m + 1))
                    act.activation(act2[:, m % 2, 0:tn], relu[:, m % 2, 0:tn], ACT.Square).then_inc(squared, 1)
                    act.wait_ge(squared, j * UPC + (m + 1))
                    act.activation(a_hi[:, u, t0:t0 + tn], act2[:, m % 2, 0:tn], ACT.Copy).then_inc(ahi_done, 1)

            def body(j, first=False):
                for t in range(TILES):
                    if 2 <= t < 2 + UP and not first:
                        square(j, t - 2)
                    if not (first and t < 2):
                        split(j, t, first)
                    if 2 <= t < 2 + UP and first:
                        square(j, t - 2)

            for k in range(KD):
                if k == 2:
                    first_tile.high(act)
                if k == 4:
                    split(0, 1, True)
                high(act, k, xhi_done)
            n.act_squares(act)
            n.act_rstd(act)
            body(0, True)
            with act.Fori(1, blocks) as j:
                body(j)

        @block.gpsimd
        def _(pool):
            def split(j, t):
                pool.wait_ge(hi_done, j * TILES + (t + 1))
                pool.tensor_tensor(w_lo[:, t % 2, :], raw[:, t % 2, :], r32(w_hi[:, t % 2, :]),
                                   ALU.subtract).then_inc(lo_done, 1)

            pool.wait_ge(lo_done, 1)
            split(0, 1)
            n.pool_squares(pool)
            for t in range(2, TILES):
                split(0, t)
            with pool.Fori(1, blocks) as j:
                for t in range(TILES):
                    split(j, t)

        @block.vector
        def _(dve):
            for k in range(KD):
                if k == 2:
                    first_tile.low(dve)
                dve.wait_ge(xhi_done, k + 1)
                low_x(dve, k, xlo_done)
            n.dve_sum(dve)
            dve.wait_ge(n.rstd_ready, 1)
            dve.sem_inc(alo_done, 2)

            def low(j, m):
                u, (t0, tn) = m // NC, CHUNKS[m % NC]
                dve.wait_ge(ahi_done, j * UPC + (m + 1))
                dve.tensor_tensor(a_lo[:, u, t0:t0 + tn], act2[:, m % 2, 0:tn], r32(a_hi[:, u, t0:t0 + tn]),
                                  ALU.subtract).then_inc(alo_done, 1)

            with dve.Fori(0, blocks) as j:
                for m in range(UPC):
                    u, (t0, tn) = m // NC, CHUNKS[m % NC]
                    dve.wait_ge(up_summed, j * UPC + (m + 1))
                    dve.scalar_tensor_tensor(out=relu[:, m % 2, 0:tn], in0=bank[u % 2][m % NC][:, 0:tn], scalar=0.0,
                                             in1=rstd[:, t0:t0 + tn], op0=ALU.max, op1=ALU.mult).then_inc(up_out, 1)
                    if m:
                        low(j, m - 1)
                low(j, UPC - 1)
                for d in range(DOWN):
                    for c, (t0, tn) in enumerate(CHUNKS):
                        dve.wait_ge(down_summed, j * DNC + (d * NC + c + 1))
                        dve.tensor_tensor(K.xT[:, d, t0:t0 + tn], K.xT[:, d, t0:t0 + tn], bank[d % 2][c][:, 0:tn],
                                          ALU.add).then_inc(down_out, 1)

        @block.tensor
        def _(pe):
            pe.sem_inc(down_out, 6)

            def up(j, u):
                i = u % 2
                w = [w[:, i, :].rearrange("p (k n) -> p k n", k=KD) for w in (w_hi, w_lo)]
                pe.wait_ge(lo_done, j * TILES + (u + 1))
                for c, (t0, tn) in enumerate(CHUNKS):
                    if u < 2:
                        pe.wait_ge(down_out, j * DNC + (NC * u + c + 1))
                    else:
                        pe.wait_ge(up_out, j * UPC + (NC * (u - 2) + c + 1))
                    for k in range(KD):
                        last = mm3(pe, bank[i][c][:, 0:tn], w[0][:, k, :], w[1][:, k, :],
                                   x_hi[:, k, t0:t0 + tn], x_lo[:, k, t0:t0 + tn], k == 0, k == KD - 1)
                    last.then_inc(up_summed, 1)

            def down(j, d):
                i, t = d % 2, UP + d // 2
                w = [w[:, t % 2, :].rearrange("p (f n) -> p f n", f=UP)[:, :, (d % 2) * P:(d % 2 + 1) * P]
                     for w in (w_hi, w_lo)]
                pe.wait_ge(lo_done, j * TILES + (t + 1))
                for c in range(NC):
                    if d < 2:
                        pe.wait_ge(up_out, j * UPC + (NC * (UP - 2 + d) + c + 1))
                    else:
                        pe.wait_ge(down_out, j * DNC + (NC * (d - 2) + c + 7))
                    if d == 0:
                        if c == 0:
                            pe.wait_ge(alo_done, j * UPC + NC * (UP - 1) + 2)
                        fs = range(UP - 1)
                    else:
                        fs = range(UP)
                    for f in fs:
                        t0, tn = CHUNKS[c]
                        last = mm3(pe, bank[i][c][:, 0:tn], w[0][:, f, :], w[1][:, f, :],
                                   a_hi[:, f, t0:t0 + tn], a_lo[:, f, t0:t0 + tn], f == 0, f == UP - 1)
                    if d:
                        last.then_inc(down_summed, 1)
                if d == 0:
                    for c, (t0, tn) in enumerate(CHUNKS):
                        f = UP - 1
                        pe.wait_ge(alo_done, j * UPC + (NC * f + c + 3))
                        mm3(pe, bank[i][c][:, 0:tn], w[0][:, f, :], w[1][:, f, :],
                            a_hi[:, f, t0:t0 + tn], a_lo[:, f, t0:t0 + tn], False, True).then_inc(down_summed, 1)

            first_two_groups(pe, bank, lambda i: [w[:, i, :].rearrange("p (k n) -> p k n", k=KD) for w in (w_hi, w_lo)],
                             x_hi, x_lo, first_tile, xlo_done, up_summed, n)
            for u in range(2, UP):
                up(0, u)
            for d in range(DOWN):
                down(0, d)
            with pe.Fori(1, blocks) as j:
                for u in range(UP):
                    up(j, u)
                for d in range(DOWN):
                    down(j, d)



def latent_stage(nc, K, M):
    with Stage(nc, "latent") as s:
        cq = s.sb("cq", [P, 3, T])
        cq_hi, cq_lo = s.sb("cq_hi", [P, 3, T], F32R), s.sb("cq_lo", [P, 3, T], F32R)
        w_raw = s.sb("w_raw", [P, 3, HEADS, 192])
        w_hi, w_lo = s.sb("w_hi", [P, 3, 6, P], F32R), s.sb("w_lo", [P, 3, 6, P], F32R)
        cos, sin, rot = s.sb("cos", [P, T]), s.sb("sin", [P, T]), s.sb("rot", [P, P])
        norm_q, norm_kv = s.sb("norm_q", [P, 3]), s.sb("norm_kv", [P, 2])
        square = s.sb("square", [P, 5, T])
        rstd = s.sb("rstd", [P, 2, T])
        turned = s.sb("turned", [P, 2, 512])
        bank = [s.ps(f"bank{i}", [P, 512]) for i in range(8)]
        cq_in, ckv_in, kr_in, w_in, tab_in, norm_in = (s.sem(n) for n in ("cq_in", "ckv_in", "kr_in", "w_in", "tab_in", "norm_in"))
        squared, summed, logged, rstd_ready = (s.sem(n) for n in ("squared", "summed", "logged", "rstd_ready"))
        cq_normed, cqhi_done, cqlo_done = s.sem("cq_normed"), s.sem("cqhi_done"), s.sem("cqlo_done")
        whi_done, wlo_done = s.sem("whi_done"), s.sem("wlo_done")
        projected, q_out = s.sem("projected"), s.sem("q_out")
        rotated, rot_out, by_sin, by_cos = s.sem("rotated"), s.sem("rot_out"), s.sem("by_sin"), s.sem("by_cos")
        block = s.block()

        @block.sync
        def _(sp):
            sp.dma_start(cq[:], K.z[Z_CQ:Z_CKV, :].rearrange("(k p) t -> p k t", p=P)).then_inc(cq_in, 16)
            sp.dma_start(M.ckv[:], K.z[Z_CKV:Z_KR, :].rearrange("(k p) t -> p k t", p=P)).then_inc(ckv_in, 16)
            sp.dma_start(w_raw[:], K.w_uq[0].rearrange("(k p) (h n) -> p k h n", p=P, h=HEADS)).then_inc(w_in, 16)
            for i in range(2):
                sp.dma_start(M.kpe[64 * i:64 * i + 64, :], K.z[Z_KR:Z_KR + ROPE, :]).then_inc(kr_in, 16)
            for dst, src in ((cos, K.c_cos), (sin, K.c_sin), (rot, K.c_rot)):
                sp.dma_start(dst[:], src).then_inc(tab_in, 16)

        @block.gpsimd
        def _(pool):
            with nc.allow_non_contiguous_dma(reason="a column of each norm weight, once"):
                pool.dma_start(norm_q[:], K.q_norm[0].rearrange("(k p) -> p k", p=P)).then_inc(norm_in, 16)
                pool.dma_start(norm_kv[:], K.kv_norm[0].rearrange("(k p) -> p k", p=P)).then_inc(norm_in, 16)
            pool.wait_ge(norm_in, 32)
            pool.wait_ge(whi_done, 2)
            pool.wait_ge(w_in, 16)
            raw = w_raw[:]
            pool.tensor_tensor(w_lo[:, :, 0:4, :], raw[:, :, :, 0:P], r32(w_hi[:, :, 0:4, :]),
                               ALU.subtract).then_inc(wlo_done, 1)
            pool.tensor_tensor(w_lo[:, :, 4:6, :].rearrange("p k g (h n) -> p k (g h) n", h=2), raw[:, :, :, P:192],
                               r32(w_hi[:, :, 4:6, :]).rearrange("p k g (h n) -> p k (g h) n", h=2),
                               ALU.subtract).then_inc(wlo_done, 1)

        @block.scalar
        def _(act):
            act.wait_ge(cq_in, 16)
            for k in range(3):
                act.activation(square[:, k, :], cq[:, k, :], ACT.Square).then_inc(squared, 1)
            act.wait_ge(ckv_in, 16)
            for k in range(2):
                act.activation(square[:, 3 + k, :], M.ckv[:, k, :], ACT.Square).then_inc(squared, 1)
            act.wait_ge(w_in, 16)
            act.activation(w_hi[:, :, 0:4, :], w_raw[:, :, :, 0:P], ACT.Copy).then_inc(whi_done, 1)
            act.activation(w_hi[:, :, 4:6, :].rearrange("p k g (h n) -> p k (g h) n", h=2), w_raw[:, :, :, P:192],
                           ACT.Copy).then_inc(whi_done, 1)
            for m, width in ((0, Q_LORA), (1, KV_LORA)):
                for c, (t0, tn) in enumerate(CHUNKS):
                    act.wait_ge(summed, NC * m + c + 1)
                    act.activation(rstd[:, m, t0:t0 + tn], bank[NC * m + c][:, 0:tn], ACT.Ln,
                                   scale=1.0 / width, bias=K.eps[:, 0:1]).then_inc(logged, 1)
                act.wait_ge(logged, NC * (m + 1))
                act.activation(rstd[:, m, :], rstd[:, m, :], ACT.Exp, scale=-0.5).then_inc(rstd_ready, 1)
            for k in range(3):
                act.wait_ge(cq_normed, k + 1)
                act.activation(cq_hi[:, k, :], cq[:, k, :], ACT.Copy).then_inc(cqhi_done, 1)
            for g in range(6):
                for c, (t0, tn) in enumerate(CHUNKS):
                    act.wait_ge(projected, NC * g + c + 1)
                    dst = M.qn[:, g, t0:t0 + tn] if g < 4 else M.qpe[:, g - 4, t0:t0 + tn]
                    act.activation(dst, bank[NC * (g % 2) + c][:, 0:tn], ACT.Copy).then_inc(q_out, 1)

        @block.tensor
        def _(pe):
            for m, ks in ((0, range(3)), (1, range(3, 5))):
                pe.wait_ge(squared, ks[-1] + 1)
                for c, (t0, tn) in enumerate(CHUNKS):
                    for k in ks:
                        last = pe.matmul(bank[NC * m + c][:, 0:tn], K.ones[:], square[:, k, t0:t0 + tn],
                                         start=(k == ks[0]), stop=(k == ks[-1]))
                    last.then_inc(summed, 1)
            pe.wait_ge(logged, 2 * NC)
            pe.wait_ge(wlo_done, 2)
            pe.wait_ge(cqlo_done, 3)
            for g in range(6):
                for c, (t0, tn) in enumerate(CHUNKS):
                    if g >= 2:
                        pe.wait_ge(q_out, NC * (g - 2) + c + 1)
                    for k in range(3):
                        last = mm3(pe, bank[NC * (g % 2) + c][:, 0:tn], w_hi[:, k, g, :], w_lo[:, k, g, :],
                                   cq_hi[:, k, t0:t0 + tn], cq_lo[:, k, t0:t0 + tn], k == 0, k == 2)
                    last.then_inc(projected, 1)
            pe.wait_ge(q_out, 6 * NC)
            pe.wait_ge(tab_in, 48)
            pe.wait_ge(kr_in, 32)
            for m, x in enumerate((M.qpe[:, 0, :], M.qpe[:, 1, :], M.kpe[:])):
                for c, (t0, tn) in enumerate(CHUNKS):
                    i = NC * m + c
                    if i >= 2:
                        pe.wait_ge(by_sin, i - 1)
                    pe.matmul(bank[6 + i % 2][:, 0:tn], rot[:], x[:, t0:t0 + tn], start=True, stop=True
                              ).then_inc(rotated, 1)

        @block.vector
        def _(dve):
            dve.wait_ge(norm_in, 32)
            dve.wait_ge(rstd_ready, 1)
            for k in range(3):
                dve.scalar_tensor_tensor(out=cq[:, k, :], in0=cq[:, k, :], scalar=norm_q[:, k:k + 1], in1=rstd[:, 0, :],
                                         op0=ALU.mult, op1=ALU.mult).then_inc(cq_normed, 1)
            for k in range(3):
                dve.wait_ge(cqhi_done, k + 1)
                dve.tensor_tensor(cq_lo[:, k, :], cq[:, k, :], r32(cq_hi[:, k, :]), ALU.subtract).then_inc(cqlo_done, 1)
            dve.wait_ge(rstd_ready, 2)
            for k in range(2):
                dve.scalar_tensor_tensor(out=M.ckv[:, k, :], in0=M.ckv[:, k, :], scalar=norm_kv[:, k:k + 1],
                                         in1=rstd[:, 1, :], op0=ALU.mult, op1=ALU.mult)
            for m, x in enumerate((M.qpe[:, 0, :], M.qpe[:, 1, :], M.kpe[:])):
                for c, (t0, tn) in enumerate(CHUNKS):
                    i = NC * m + c
                    dve.wait_ge(rotated, i + 1)
                    dve.tensor_tensor(turned[:, i % 2, 0:tn], bank[6 + i % 2][:, 0:tn], sin[:, t0:t0 + tn],
                                      ALU.mult).then_inc(by_sin, 1)
                    dve.tensor_tensor(x[:, t0:t0 + tn], x[:, t0:t0 + tn], cos[:, t0:t0 + tn], ALU.mult).then_inc(by_cos, 1)
                    dve.wait_ge(by_sin, i + 1)
                    dve.wait_ge(by_cos, i + 1)
                    dve.tensor_tensor(x[:, t0:t0 + tn], x[:, t0:t0 + tn], turned[:, i % 2, 0:tn],
                                      ALU.add).then_inc(rot_out, 1)


def keys_stage(nc, K, M):
    with Stage(nc, "keys") as s:
        wuk = s.sb("wuk", [P, HEADS, 2, P])
        wukT = s.sb("wukT", [P, HEADS, 2, P])
        bank = [s.ps(f"bank{i}", [P, 512]) for i in range(4)]
        wuk_in, wuv_in = s.sem("wuk_in"), s.sem("wuv_in")
        made, out_act, out_dve = s.sem("made"), s.sem("out_act"), s.sem("out_dve")
        block = s.block()
        KN, V, WT, ROWS, QL = 0, 8, 16, 20, 29
        END = 33

        @block.sync
        def _(sp):
            sp.dma_start(wuk[:], K.w_uk[0].rearrange("h (k p) n -> p (h k) n", p=P)).then_inc(wuk_in, 16)
            for k in range(2):
                sp.dma_start(M.wuv[:, k, :, :], K.w_uv[0][:, k * P:(k + 1) * P, :].rearrange("h p v -> p h v")
                             ).then_inc(wuv_in, 16)

        @block.tensor
        def _(pe):
            def free(n):
                if n >= 4:
                    pe.wait_ge(out_act if n % 2 == 0 else out_dve, (n - 4) // 2 + 1)
                return bank[n % 4]

            pe.wait_ge(wuk_in, 16)
            pe.wait_ge(wuv_in, 32)
            for n in range(8):
                h, half = n // 2, n % 2
                b = free(KN + n)
                for k in range(2):
                    last = pe.matmul(b[:], wuk[:, h, k, :], M.ckv[:, k, half * 512:half * 512 + 512],
                                     start=(k == 0), stop=(k == 1))
                last.then_inc(made, 1)
            for n in range(8):
                b = free(V + n)
                for k in range(2):
                    last = pe.matmul(b[:], M.ckv[:, k, n * P:(n + 1) * P],
                                     M.wuv[:, k, :, :].rearrange("p h v -> p (h v)"), start=(k == 0), stop=(k == 1))
                last.then_inc(made, 1)
            for h in range(HEADS):
                b = free(WT + h)
                for k in range(2):
                    last = pe.transpose(b[:, k * P:(k + 1) * P], wuk[:, h, k, :], K.ident[:])
                last.then_inc(made, 1)
            for n in range(9):
                b, rows = free(ROWS + n), (P if n < 8 else NS)
                for k in range(2):
                    pe.transpose(b[0:rows, k * P:(k + 1) * P], M.ckv[:, k, n * P:n * P + rows], K.ident[:])
                pe.transpose(b[0:rows, KV_LORA:LAT], M.kpe[0:ROPE, n * P:n * P + rows], K.ident[0:ROPE, 0:ROPE]
                             ).then_inc(made, 1)
            for h in range(HEADS):
                b = free(QL + h)
                if h == 0:
                    pe.wait_ge(out_act, (WT + 4) // 2)
                    pe.wait_ge(out_dve, (WT + 4) // 2)
                for k in range(2):
                    last = pe.matmul(b[:, k * NS:(k + 1) * NS], wukT[:, h, k, :], M.qn[:, h, SEQ:T],
                                     start=True, stop=True)
                last.then_inc(made, 1)

        def copies(eng, copy, parity, out):
            for n in range(parity, END, 2):
                b = bank[n % 4]
                eng.wait_ge(made, n + 1)
                if n < V:
                    h, half = n // 2, n % 2
                    last = copy(M.kn[:, h, half * 512:half * 512 + 512], b[:])
                elif n < WT:
                    last = copy(M.v[:, n - V, :], b[:])
                elif n < ROWS:
                    last = copy(wukT[:, n - WT, :, :].rearrange("p k c -> p (k c)"), b[:, 0:2 * P])
                elif n < QL:
                    rows = P if n - ROWS < 8 else NS
                    last = copy(M.rows[0:rows, n - ROWS, :], b[0:rows, 0:LAT])
                else:
                    last = copy(M.qs[:, 0:2, :, n - QL, :], b[:, 0:2 * NS].rearrange("p (k b t) -> p k b t", k=2, b=NB))
                last.then_inc(out, 1)

        @block.scalar
        def _(act):
            for h in range(HEADS):
                o = 64 * (h % 2)
                for to in (0, ROPE):
                    act.activation(M.qs[to:to + ROPE, 2, :, h, :],
                                   M.qpe[o:o + ROPE, h // 2, SEQ:T].rearrange("p (b t) -> p b t", b=NB), ACT.Copy)
            copies(act, lambda o, x: act.activation(o, x, ACT.Copy), 0, out_act)

        @block.vector
        def _(dve):
            copies(dve, lambda o, x: dve.tensor_copy(o, x), 1, out_dve)


def prompt_attention_stage(nc, K, M):
    with Stage(nc, "pattn") as s:
        q = s.sb("q", [P, 2, SEQ])
        qpe = s.sb("qpe", [P, SEQ])
        v = s.sb("v", [P, 2, 8, P])
        p, pT = s.sb("p", [P, 2, SEQ]), s.sb("pT", [P, 2, 8, P])
        o = s.sb("o", [P, 2, SEQ])
        diag = s.sb("diag", [P, P])
        top, ntop, den, rden = (s.sb(n, [P, 2]) for n in ("top", "ntop", "den", "rden"))
        S = [s.ps(f"S{i}", [P, SEQ]) for i in range(2)]
        PT = s.ps("PT", [P, 8, P])
        O = [s.ps(f"O{i}", [P, 512]) for i in range(2)]
        diag_in, q_ready = s.sem("diag_in"), s.sem("q_ready")
        scored, masked, topped, ntopped = s.sem("scored"), s.sem("masked"), s.sem("topped"), s.sem("ntopped")
        expd, inverted, p_ready, turned = s.sem("expd"), s.sem("inverted"), s.sem("p_ready"), s.sem("turned")
        out_lo, out_hi, valued, o_out = s.sem("out_lo"), s.sem("out_hi"), s.sem("valued"), s.sem("o_out")
        stored = [s.sem("stored0"), s.sem("stored1")]
        o_free, rows_out = s.sem("o_free"), s.sem("rows_out")
        block = s.block()
        TILES = 16

        @block.sync
        def _(sp):
            sp.dma_start(diag[:], K.c_causal).then_inc(diag_in, 16)
            sp.dma_start(K.rows_prompt.rearrange("(i p) c -> p i c", p=P), M.rows[:, 0:8, :]).then_inc(rows_out, 16)
            sp.dma_start(K.rows_sample, M.rows[0:NS, 8, :]).then_inc(rows_out, 16)
            sp.sem_inc(o_free, 2)
            with sp.Fori(0, 2) as i:
                for hd in range(2):
                    sp.wait_ge(o_out, i * TILES + (8 * hd + 10))
                    sp.dma_start(K.mix[bass.ds(i * 256 + (512 + P * hd), P), 0:SEQ], o[:, hd, :]).then_inc(stored[hd], 16)
                for hd in range(2):
                    sp.wait_ge(stored[hd], i * 16 + 16)
                    sp.sem_inc(o_free, 1)
            sp.wait_ge(rows_out, 32)

        @block.vector
        def _(dve):
            def soften(i, n):
                hd, qt, x = n // 8, n % 8, n % 2
                dve.wait_ge(scored, i * TILES + (n + 1))
                d = S[x][:, qt * P:(qt + 1) * P]
                dve.tensor_tensor(d, d, diag[:], ALU.add).then_inc(masked, 1)
                dve.wait_ge(masked, i * TILES + (n + 1))
                dve.tensor_reduce(top[:, x:x + 1], S[x][:, 0:(qt + 1) * P], AX.X, ALU.max).then_inc(topped, 1)
                dve.wait_ge(topped, i * TILES + (n + 1))
                dve.tensor_scalar(ntop[:, x:x + 1], top[:, x:x + 1], -SCALE, None, ALU.mult).then_inc(ntopped, 1)

            def divide(i, n):
                hd, qt, x = n // 8, n % 8, n % 2
                dve.wait_ge(expd, i * TILES + (n + 3))
                dve.reciprocal(rden[:, x:x + 1], den[:, x:x + 1]).then_inc(inverted, 1)
                dve.wait_ge(inverted, i * TILES + (n + 1))
                dve.tensor_scalar(p[:, x, 0:(qt + 1) * P], p[:, x, 0:(qt + 1) * P], rden[:, x:x + 1], None,
                                  ALU.mult).then_inc(p_ready, 1)

            def copy_hi(i, n):
                hd, qt, x = n // 8, n % 8, n % 2
                if qt >= 4:
                    dve.wait_ge(turned, i * TILES + (n + 3))
                    dve.wait_ge(valued, i * TILES + (n + 1))
                    dve.tensor_copy(pT[:, x, 4:qt + 1, :], PT[:, 4:qt + 1, :]).then_inc(out_hi, 1)

            dve.wait_ge(diag_in, 16)
            dve.sem_inc(out_hi, 1)
            with dve.Fori(0, 2) as i:
                dve.wait_ge(valued, i * TILES + 2)
                for hd in range(2):
                    h = i * 2 + hd
                    dve.tensor_copy(q[:, hd, :], M.qn[:, bass.ds(h, 1), 0:SEQ].rearrange("p a t -> p (a t)"))
                    dve.tensor_copy(v[:, hd, :, :], M.v[:, :, bass.ds(h * P, P)])
                dve.tensor_copy(qpe[:], M.qpe[:, bass.ds(i, 1), 0:SEQ].rearrange("p a t -> p (a t)")).then_inc(q_ready, 1)
                soften(i, 0)
                for n in range(TILES):
                    divide(i, n)
                    if n + 1 < TILES:
                        soften(i, n + 1)
                    copy_hi(i, n)

        @block.scalar
        def _(act):
            act.sem_inc(expd, 2)
            act.sem_inc(out_lo, 1)
            act.sem_inc(o_out, 2)

            def softmax(i, n):
                hd, qt, x = n // 8, n % 8, n % 2
                act.wait_ge(ntopped, i * TILES + (n + 1))
                act.wait_ge(turned, i * TILES + (n + 1))
                act.activation(p[:, x, 0:(qt + 1) * P], S[x][:, 0:(qt + 1) * P], ACT.Exp, bias=ntop[:, x:x + 1],
                               scale=SCALE, accum_out=den[:, x:x + 1]).then_inc(expd, 1)

            def copy_lo(i, n):
                hd, qt, x = n // 8, n % 8, n % 2
                m = min(qt + 1, 4)
                act.wait_ge(turned, i * TILES + (n + 3))
                act.wait_ge(valued, i * TILES + (n + 1))
                act.activation(pT[:, x, 0:m, :], PT[:, 0:m, :], ACT.Copy).then_inc(out_lo, 1)

            def copy_o(i, n):
                hd, qt, x = n // 8, n % 8, n % 2
                act.wait_ge(valued, i * TILES + (n + 3))
                if qt == 0:
                    act.wait_ge(o_free, i * 2 + (hd + 1))
                act.activation(o[:, hd, qt * P:(qt + 1) * P], O[x][:, 0:P], ACT.Copy).then_inc(o_out, 1)

            with act.Fori(0, 2) as i:
                softmax(i, 0)
                for n in range(TILES):
                    if n + 1 < TILES:
                        softmax(i, n + 1)
                    copy_lo(i, n)
                    if n:
                        copy_o(i, n - 1)
                copy_o(i, TILES - 1)

        @block.tensor
        def _(pe):
            pe.sem_inc(turned, 2)
            pe.sem_inc(valued, 2)

            def score(i, n):
                hd, qt, x = n // 8, n % 8, n % 2
                pe.wait_ge(expd, i * TILES + (n + 1))
                keys, o64 = (qt + 1) * P, 64 * hd
                for k0 in range(0, keys, 512):
                    kn = min(512, keys - k0)
                    pe.matmul(S[x][:, k0:k0 + kn], q[:, hd, qt * P:(qt + 1) * P],
                              M.kn[:, bass.ds(i * 2 + hd, 1), k0:k0 + kn].rearrange("p a t -> p (a t)"),
                              start=True, stop=False)
                    last = pe.matmul(S[x][:, k0:k0 + kn], qpe[o64:o64 + 64, qt * P:(qt + 1) * P],
                                     M.kpe[o64:o64 + 64, k0:k0 + kn], start=False, stop=True)
                last.then_inc(scored, 1)

            def turn(i, n):
                hd, qt, x = n // 8, n % 8, n % 2
                pe.wait_ge(p_ready, i * TILES + (n + 1))
                pe.wait_ge(out_lo, i * TILES + (n + 1))
                if qt >= 4:
                    pe.wait_ge(out_hi, i * 8 + (4 * hd + qt - 3))
                for k in range(qt + 1):
                    last = pe.transpose(PT[:, k, :], p[:, x, k * P:(k + 1) * P], K.ident[:])
                last.then_inc(turned, 1)

            def value(i, n):
                hd, qt, x = n // 8, n % 8, n % 2
                pe.wait_ge(out_lo, i * TILES + (n + 2))
                if qt >= 4:
                    pe.wait_ge(out_hi, i * 8 + (4 * hd + qt - 2))
                pe.wait_ge(o_out, i * TILES + (n + 1))
                for k in range(qt + 1):
                    last = pe.matmul(O[x][:, 0:P], v[:, hd, k, :], pT[:, x, k, :], start=(k == 0), stop=(k == qt))
                last.then_inc(valued, 1)

            with pe.Fori(0, 2) as i:
                pe.wait_ge(q_ready, i + 1)
                score(i, 0)
                for n in range(TILES):
                    if n + 1 < TILES:
                        score(i, n + 1)
                    turn(i, n)
                    if n:
                        value(i, n - 1)
                value(i, TILES - 1)


def sample_attention_stage(nc, K, M):
    Place = namedtuple("Place", "opens starts last")
    GROUPS = PAGES // PG
    RING = 4
    Q = HEADS * TS
    Q2 = 2 * Q
    with Stage(nc, "sattn") as s:
        lat = s.sb("lat", [P, RING, PG, LAT])
        lat_hi, lat_lo = (s.sb(n, [P, RING, PG, KV_LORA], F32R) for n in ("lat_hi", "lat_lo"))
        k_hi, k_lo = (s.sb(n, [P, 2, 2, 512], F32R) for n in ("k_hi", "k_lo"))
        k_rot = s.sb("k_rot", [P, 2, 512], F32R)
        pages = s.sb("pages", [1, NB * PAGES], I32)
        newmask = s.sb("newmask", [Q2, NB, NS])
        q = s.sb("q", [P, 3, NB, Q2])
        q_hi_all, q_lo_all = (s.sb(n, [P, 3, NB, Q2], F32R) for n in ("q_hi_all", "q_lo_all"))
        q_hi, q_lo = (s.sb(n, [P, 3, Q2], F32R) for n in ("q_hi", "q_lo"))
        p, pT = s.sb("p", [Q2, 2, 512]), s.sb("pT", [P, 2, PG, Q2], F32R)
        sn, pn, pnT = s.sb("sn", [Q2, NB, NS]), s.sb("pn", [Q2, NB, NS]), s.sb("pnT", [NS, NB, Q2])
        m_new, nm_new, den_new = (s.sb(n, [Q2, NB]) for n in ("m_new", "nm_new", "den_new"))
        acc_new, acc, acc_div = s.sb("acc_new", [Q2, NB, KV_LORA]), s.sb("acc", [Q2, KV_LORA]), s.sb("acc_div", [Q2, KV_LORA])
        m, gm, alpha, gsum = s.sb("m", [Q2, 2]), s.sb("gm", [Q2, 2]), s.sb("alpha", [Q2, RING]), s.sb("gsum", [Q2, RING])
        den, nm, rden = (s.sb(n, [Q2, 1]) for n in ("den", "nm", "rden"))
        halves = s.sb("halves", [Q2, Q])
        outT = s.sb("outT", [P, 2, HEADS, NS])
        o = s.sb("o", [P, HEADS, NS])
        KT = s.ps("KT", [P, 3, 512])
        S = [s.ps(f"S{i}", [P, 512]) for i in range(2)]
        PT, O, X = s.ps("PT", [P, 512]), s.ps("O", [P, 512]), s.ps("X", [P, 512])
        OT = X[:, 0:2 * Q]
        passed = s.sem("passed")
        tab_in, mask_in, lat_in = s.sem("tab_in"), s.sem("mask_in"), [s.sem(f"lat_in{i}") for i in range(RING)]
        halves_made, q_made, zeroed = s.sem("halves_made"), s.sem("q_made"), s.sem("zeroed")
        sn_made, sn_masked, sn_topped, nm_made = (s.sem(n) for n in ("sn_made", "sn_masked", "sn_topped", "nm_made"))
        pn_made, pn_turned, pn_out, on_made, on_out = (s.sem(n) for n in (
            "pn_made", "pn_turned", "pn_out", "on_made", "on_out"))
        kt_made, khi_done, klo_done = s.sem("kt_made"), s.sem("khi_done"), s.sem("klo_done")
        lathi_done, latlo_done = s.sem("lathi_done"), s.sem("latlo_done")
        qhi_split, qlo_split = s.sem("qhi_split"), s.sem("qlo_split")
        qhi_done, qlo_done = s.sem("qhi_done"), s.sem("qlo_done")
        scored, group_topped, topped, expd, alpha_done = (s.sem(n) for n in (
            "scored", "group_topped", "topped", "expd", "alpha_done"))
        turned, pthi_done, pt_out, valued, acc_done = (s.sem(n) for n in (
            "turned", "pthi_done", "pt_out", "valued", "acc_done"))
        inverted, divided, ot_made, ot_out = (s.sem(n) for n in ("inverted", "divided", "ot_made", "ot_out"))
        o_made, o_out, stored = s.sem("o_made"), s.sem("o_out"), s.sem("stored")
        block = s.block()

        def over_groups(eng, step):
            def quad(b, g, first, start=False, last=False):
                for i in range(RING):
                    step(b, g, i, Place(first, start, last and i == RING - 1))

            quad(0, 0, True, start=True)
            with eng.Fori(RING, GROUPS, RING) as g:
                quad(0, g, False)
            with eng.Fori(1, NB - 1) as b:
                quad(b, 0, True)
                with eng.Fori(RING, GROUPS, RING) as g:
                    quad(b, g, False)
            quad(NB - 1, 0, True)
            with eng.Fori(RING, GROUPS - RING, RING) as g:
                quad(NB - 1, g, False)
            quad(NB - 1, GROUPS - RING, False, last=True)

        def begun(at, i, lag):
            return not (at.starts and i < lag)

        @block.sync
        def _(sp):
            sp.dma_start(pages[:], K.page_table).then_inc(tab_in, 16)
            for i in range(2):
                sp.dma_start(newmask[i * Q:(i + 1) * Q], K.c_newmask).then_inc(mask_in, 16)
            sp.wait_ge(tab_in, 16)

            def load(g, i):
                for n in range(PG):
                    page = sp.value_load(pages[0:1, bass.ds(g * PG + n, 1)])
                    sp.dma_start(lat[:, i, n, :], K.cache[bass.ds(page, 1), :, :].rearrange("a p c -> (a p) c")
                                 ).then_inc(lat_in[i], 16)

            for i in range(RING):
                load(i, i)
            with sp.Fori(1, NB * GROUPS // RING) as j:
                for i in range(RING):
                    sp.wait_ge(latlo_done, j * RING + (i - RING + 1))
                    load(j * RING + i, i)
            sp.wait_ge(o_out, 1)
            sp.dma_start(K.mix[512:1024, SEQ:T].rearrange("(h p) t -> p h t", p=P), o[:]).then_inc(stored, 16)
            sp.wait_ge(stored, 16)

        def pages_in(eng, b, g, i):
            eng.wait_ge(lat_in[i % RING],
                        b * (16 * PAGES // RING) + g * (16 * PG // RING) + (i // RING + 1) * 16 * PG)

        @block.tensor
        def _(pe):
            pe.sem_inc(turned, 2)
            pe.sem_inc(valued, 2)
            pe.sem_inc(ot_made, 1)
            pe.wait_ge(q_made, 2)
            pe.wait_ge(halves_made, 1)
            for b in range(NB):
                for c, w in ((0, P), (1, P), (2, ROPE)):
                    k = M.ckv[:, c, SEQ:T] if c < 2 else M.kpe[0:ROPE, SEQ:T]
                    last = pe.matmul(S[0][0:Q2, b * NS:(b + 1) * NS], q[0:w, c, b, :], k, start=(c == 0), stop=(c == 2))
            last.then_inc(sn_made, 1)
            pe.wait_ge(pn_made, NB)
            for b in range(NB):
                last = pe.transpose(X[0:NS, b * Q2:(b + 1) * Q2], pn[:, b, :], K.ident[0:Q2, 0:Q2])
            last.then_inc(pn_turned, 1)
            pe.wait_ge(zeroed, 1)
            pe.wait_ge(pn_out, 1)
            for b in range(NB):
                bank = KT[0:Q2, b // 2, :] if b < 6 else S[1][0:Q2, :]
                last = pe.matmul(bank[:, (b % 2) * KV_LORA:(b % 2 + 1) * KV_LORA], pnT[:, b, :], M.rows[0:NS, 8, 0:KV_LORA],
                                 start=True, stop=True)
            last.then_inc(on_made, 1)

            def turn_keys(b, g, i, first=False):
                pages_in(pe, b, g, i)
                for c, w in ((2, ROPE), (0, P), (1, P)):
                    if not first and c == 2:
                        wait_apart(pe, klo_done, b * (2 * GROUPS) + 2 * g + (2 * i - 1), passed)
                    if not first and c == 0:
                        pe.wait_ge(klo_done, b * (2 * GROUPS) + 2 * g + 2 * i)
                    for n in range(PG):
                        last = pe.transpose(KT[0:w, c, n * P:(n + 1) * P], lat[:, i % RING, n, c * P:c * P + w], K.ident[:])
                    if c != 0:
                        last.then_inc(kt_made, 1)

            def turn(b, g, i):
                pe.wait_ge(expd, b * GROUPS + g + (i + 3))
                pe.wait_ge(pt_out, b * GROUPS + g + (i + 1))
                pe.sem_inc(passed, 1)
                for n in range(PG):
                    last = pe.transpose(PT[:, n * Q2:(n + 1) * Q2], p[:, i % 2, n * P:(n + 1) * P], K.ident[0:Q2, 0:Q2])
                last.then_inc(turned, 1)

            def value(b, g, i):
                pe.wait_ge(pt_out, b * GROUPS + g + (i + 2))
                pe.wait_ge(latlo_done, b * GROUPS + g + (i + 1))
                pe.wait_ge(acc_done, b * GROUPS + g + (i + 1))
                pe.sem_inc(passed, 1)
                for n in range(PG):
                    pe.matmul(O[0:Q2, 0:KV_LORA], pT[:, i % 2, n, :], lat_hi[:, i % RING, n, :], start=(n == 0), stop=False)
                    last = pe.matmul(O[0:Q2, 0:KV_LORA], pT[:, i % 2, n, :], lat_lo[:, i % RING, n, :], start=False,
                                     stop=(n == PG - 1))
                last.then_inc(valued, 1)

            def merge(b):
                pe.wait_ge(divided, b)
                pe.wait_ge(ot_out, b)
                pe.sem_inc(passed, 1)
                for c in range(2):
                    last = pe.matmul(OT[:, c * Q:(c + 1) * Q], acc_div[:, c * P:(c + 1) * P], halves[:],
                                     start=True, stop=True)
                last.then_inc(ot_made, 1)

            def step(b, g, i, at):
                if not at.last:
                    turn_keys(b, g, i + 1)
                pe.wait_ge(klo_done, b * (2 * GROUPS) + 2 * g + (2 * i + 2))
                pe.wait_ge(expd, b * GROUPS + g + (i + 1))
                if at.opens and i == 0:
                    pe.wait_ge(qhi_done, b + 1)
                    pe.wait_ge(qlo_done, b + 1)
                pe.sem_inc(passed, 1)
                out, y = S[i % 2][0:Q2, :], i % 2
                for c in range(2):
                    mm3(pe, out, q_hi[:, c, :], q_lo[:, c, :], k_hi[:, y, c, :], k_lo[:, y, c, :], c == 0, False)
                pe.matmul(out, q_hi[:, 2, :], k_rot[:, y, :], start=False, stop=False)
                pe.matmul(out, q_lo[0:ROPE, 2, :], k_rot[0:ROPE, y, :], start=False, stop=True).then_inc(scored, 1)
                if begun(at, i, 1):
                    turn(b, g, i - 1)
                if at.opens and not at.starts and i == 2:
                    merge(b)
                if begun(at, i, 2):
                    value(b, g, i - 2)

            pe.wait_ge(on_out, 2)
            turn_keys(0, 0, 0, first=True)
            over_groups(pe, step)
            turn(NB - 1, GROUPS - RING, RING - 1)
            value(NB - 1, GROUPS - RING, RING - 2)
            value(NB - 1, GROUPS - RING, RING - 1)
            merge(NB)
            pe.wait_ge(ot_out, NB + 1)
            for h in range(HEADS):
                for c in range(2):
                    last = pe.matmul(X[:, h * NS:(h + 1) * NS], M.wuv[:, c, h, :], outT[:, c, h, :],
                                     start=(c == 0), stop=(c == 1))
            last.then_inc(o_made, 1)

        @block.scalar
        def _(act):
            act.sem_inc(expd, 2)
            act.sem_inc(ot_out, 1)
            act.activation(q[:, :, :, 0:Q], M.qs[:].rearrange("p c b h t -> p c b (h t)"), ACT.Copy).then_inc(q_made, 1)
            act.wait_ge(q_made, 2)
            act.activation(q_hi_all[:], q[:], ACT.Copy).then_inc(qhi_split, 1)
            for b in range(NB):
                act.wait_ge(nm_made, 1)
                act.activation(pn[:, b, :], sn[:, b, :], ACT.Exp, bias=nm_new[:, b:b + 1], scale=SCALE,
                               accum_out=den_new[:, b:b + 1]).then_inc(pn_made, 1)
            act.wait_ge(pn_turned, 1)
            act.activation(pnT[:, :, 0:Q], X[0:NS, :].rearrange("p (b q) -> p b q", b=NB)[:, :, 0:Q], ACT.Copy
                           ).then_inc(pn_out, 1)

            def split_rotated_keys(b, g, i):
                act.wait_ge(kt_made, b * (2 * GROUPS) + 2 * g + (2 * i + 1))
                act.activation(k_rot[0:ROPE, i % 2, :], KT[0:ROPE, 2, :], ACT.Copy).then_inc(khi_done, 1)

            def split_latent_keys(b, g, i):
                act.wait_ge(kt_made, b * (2 * GROUPS) + 2 * g + (2 * i + 2))
                act.activation(k_hi[:, i % 2, :, :], KT[:, 0:2, :], ACT.Copy).then_inc(khi_done, 1)

            def exponentials(b, g, i):
                y, z = i % 2, i % RING
                act.wait_ge(topped, b * GROUPS + g + (i + 1))
                act.wait_ge(turned, b * GROUPS + g + (i + 1))
                act.activation(p[:, y, :], S[y][0:Q2, :], ACT.Exp, bias=nm[:, 0:1], scale=SCALE,
                               accum_out=gsum[:, z:z + 1]).then_inc(expd, 1)

            def rescaling(b, g, i):
                y, z = i % 2, i % RING
                act.activation(alpha[:, z:z + 1], m[:, 1 - y:2 - y], ACT.Exp, bias=nm[:, 0:1], scale=SCALE
                               ).then_inc(alpha_done, 1)

            def step(b, g, i, at):
                if begun(at, i, 1):
                    act.wait_ge(scored, b * GROUPS + g + i)
                if at.opens and i == 0:
                    act.activation(q_hi[:], q_hi_all[:, :, bass.ds(b, 1), :].rearrange("p c a q -> p c (a q)"), ACT.Copy
                                   ).then_inc(qhi_done, 1)
                if not at.last:
                    split_rotated_keys(b, g, i + 1)
                if begun(at, i, 1):
                    exponentials(b, g, i - 1)
                if not at.last:
                    split_latent_keys(b, g, i + 1)
                if begun(at, i, 1):
                    rescaling(b, g, i - 1)
                split_latents(b, g, i, begun(at, i, 1))
                if at.opens and not at.starts and i == 2:
                    copy_merged(b)

            def split_latents(b, g, i, wait):
                pages_in(act, b, g, i)
                if wait:
                    act.wait_ge(valued, b * GROUPS + g + i)
                act.activation(lat_hi[:, i % RING, :, :], lat[:, i % RING, :, 0:KV_LORA], ACT.Copy).then_inc(lathi_done, 1)

            def copy_merged(b):
                act.wait_ge(ot_made, b + 1)
                act.activation(outT[:, :, :, bass.ds(b * TS - TS, TS)],
                               OT.rearrange("p (c h t) -> p c h t", c=2, h=HEADS), ACT.Copy).then_inc(ot_out, 1)

            split_rotated_keys(0, 0, 0)
            split_latent_keys(0, 0, 0)
            over_groups(act, step)
            exponentials(NB - 1, GROUPS - RING, RING - 1)
            rescaling(NB - 1, GROUPS - RING, RING - 1)
            copy_merged(NB)
            act.wait_ge(o_made, 1)
            act.activation(o[:], X[:, 0:HEADS * NS].rearrange("p (h t) -> p h t", h=HEADS), ACT.Copy).then_inc(o_out, 1)

        @block.gpsimd
        def _(pool):
            pool.memset(pnT[:, :, Q:Q2], 0.0).then_inc(zeroed, 1)
            pool.wait_ge(qhi_split, 1)
            pool.wait_ge(q_made, 2)
            pool.tensor_tensor(q_lo_all[:], q[:], r32(q_hi_all[:]), ALU.subtract).then_inc(qlo_split, 1)

            def step(b, g, i, at):
                pool.wait_ge(lathi_done, b * GROUPS + g + (i + 1))
                pool.tensor_tensor(lat_lo[:, i % RING, :, :], lat[:, i % RING, :, 0:KV_LORA], r32(lat_hi[:, i % RING, :, :]),
                                   ALU.subtract).then_inc(latlo_done, 1)

            over_groups(pool, step)

        @block.vector
        def _(dve):
            dve.sem_inc(pt_out, 1)
            dve.sem_inc(acc_done, 1)
            dve.tensor_copy(q[:, :, :, Q:Q2], M.qs[:].rearrange("p c b h t -> p c b (h t)")).then_inc(q_made, 1)
            dve.tensor_tensor(halves[:], K.ident[0:Q2, 0:Q], K.ident[0:Q2, Q:Q2], ALU.add).then_inc(halves_made, 1)
            dve.wait_ge(mask_in, 32)
            dve.wait_ge(sn_made, 1)
            dve.tensor_tensor(sn[:], S[0][0:Q2, :].rearrange("p (b t) -> p b t", b=NB), newmask[:], ALU.add
                              ).then_inc(sn_masked, 1)
            dve.wait_ge(sn_masked, 1)
            dve.tensor_reduce(m_new[:], sn[:], AX.X, ALU.max).then_inc(sn_topped, 1)
            dve.wait_ge(sn_topped, 1)
            dve.tensor_scalar(nm_new[:], m_new[:], -SCALE, None, ALU.mult).then_inc(nm_made, 1)
            dve.wait_ge(on_made, 1)
            dve.tensor_copy(acc_new[:, 0:6, :].rearrange("p b v -> p (b v)"), KT[0:Q2, :, :].rearrange("p c v -> p (c v)")
                            ).then_inc(on_out, 1)
            dve.tensor_copy(acc_new[:, 6:8, :].rearrange("p b v -> p (b v)"), S[1][0:Q2, :]).then_inc(on_out, 1)

            def split_latent_keys(b, g, i):
                y = i % 2
                dve.wait_ge(khi_done, b * (2 * GROUPS) + 2 * g + (2 * i + 2))
                dve.tensor_tensor(k_lo[:, y, :, :], KT[:, 0:2, :], r32(k_hi[:, y, :, :]), ALU.subtract).then_inc(klo_done, 1)

            def split_rotated_keys(b, g, i):
                y = i % 2
                dve.wait_ge(khi_done, b * (2 * GROUPS) + 2 * g + (2 * i + 1))
                dve.tensor_tensor(k_rot[ROPE:P, y, :], KT[0:ROPE, 2, :], r32(k_rot[0:ROPE, y, :]), ALU.subtract
                                  ).then_inc(klo_done, 1)

            def split_p(b, g, i):
                dve.wait_ge(turned, b * GROUPS + g + (i + 3))
                dve.wait_ge(valued, b * GROUPS + g + (i + 1))
                src = PT[:, 0:PG * Q2].rearrange("p (n q) -> p n q", n=PG)
                y = i % 2
                dve.tensor_copy(pT[:, y, :, 0:Q], src[:, :, 0:Q]).then_inc(pthi_done, 1)
                dve.wait_ge(pthi_done, b * GROUPS + g + (i + 1))
                dve.tensor_tensor(pT[:, y, :, Q:Q2], src[:, :, Q:Q2], r32(pT[:, y, :, 0:Q]), ALU.subtract).then_inc(pt_out, 1)

            def top(b, g, i, first, wait):
                x = i % 2
                if first:
                    dve.tensor_copy(m[:, 1:2], m_new[:, bass.ds(b, 1)])
                dve.wait_ge(scored, b * GROUPS + g + (i + 1))
                dve.tensor_reduce(gm[:, x:x + 1], S[x][0:Q2, :], AX.X, ALU.max).then_inc(group_topped, 1)
                if wait:
                    dve.wait_ge(alpha_done, b * GROUPS + g + i)
                dve.wait_ge(group_topped, b * GROUPS + g + (i + 1))
                dve.tensor_tensor(m[:, x:x + 1], m[:, 1 - x:2 - x], gm[:, x:x + 1], ALU.max)
                dve.tensor_scalar(nm[:], gm[:, x:x + 1], m[:, 1 - x:2 - x], -SCALE, ALU.max, ALU.mult).then_inc(topped, 1)

            def gather(b, g, i, from_new):
                y = i % RING
                dve.wait_ge(valued, b * GROUPS + g + (i + 3))
                den_in = den_new[:, bass.ds(b, 1)] if from_new else den[:]
                acc_in = acc_new[:, bass.ds(b, 1), :].rearrange("p a v -> p (a v)") if from_new else acc[:]
                dve.scalar_tensor_tensor(out=den[:], in0=den_in, scalar=alpha[:, y:y + 1], in1=gsum[:, y:y + 1],
                                         op0=ALU.mult, op1=ALU.add)
                dve.scalar_tensor_tensor(out=acc[:], in0=acc_in, scalar=alpha[:, y:y + 1], in1=O[0:Q2, 0:KV_LORA],
                                         op0=ALU.mult, op1=ALU.add).then_inc(acc_done, 1)

            def divide(b):
                dve.wait_ge(acc_done, b * GROUPS + 1)
                dve.reciprocal(rden[:], den[:]).then_inc(inverted, 1)
                dve.wait_ge(inverted, b)
                dve.wait_ge(ot_made, b)
                dve.tensor_scalar(acc_div[:], acc[:], rden[:, 0:1], None, ALU.mult).then_inc(divided, 1)

            def step(b, g, i, at):
                if at.opens and i == 0:
                    if begun(at, i, 1):
                        dve.wait_ge(scored, b * GROUPS)
                    dve.tensor_copy(q_lo[:], q_lo_all[:, :, bass.ds(b, 1), :].rearrange("p c a q -> p c (a q)")
                                    ).then_inc(qlo_done, 1)
                if not at.last:
                    split_rotated_keys(b, g, i + 1)
                    split_latent_keys(b, g, i + 1)
                top(b, g, i, at.opens and i == 0, begun(at, i, 1))
                if begun(at, i, 1):
                    split_p(b, g, i - 1)
                if begun(at, i, 2):
                    gather(b, g, i - 2, at.opens and i == 2)
                if at.opens and not at.starts and i == 1:
                    divide(b)

            dve.wait_ge(qlo_split, 1)
            split_rotated_keys(0, 0, 0)
            split_latent_keys(0, 0, 0)
            over_groups(dve, step)
            split_p(NB - 1, GROUPS - RING, RING - 1)
            gather(NB - 1, GROUPS - RING, RING - 2, False)
            dve.wait_ge(alpha_done, NB * GROUPS)
            gather(NB - 1, GROUPS - RING, RING - 1, False)
            divide(NB)



def alpha_stage(nc, K):
    with Stage(nc, "alpha") as s:
        a1, w2, bias = s.sb("a1", [GATE_RANK, T]), s.sb("w2", [GATE_RANK, HEADS * P]), s.sb("bias", [P, HEADS])
        out = s.sb("out", [P, HEADS, T])
        bank = [[s.ps(f"bank{i}{c}", [P, 512]) for c in range(NC)] for i in range(2)]
        loaded, projected, biased, stored = (s.sem(n) for n in ("loaded", "projected", "biased", "stored"))
        block = s.block()

        @block.sync
        def _(sp):
            sp.dma_start(a1[:], K.z[G_A:G_A + GATE_RANK, :]).then_inc(loaded, 16)
            sp.dma_start(w2[:], K.w_alpha2[0]).then_inc(loaded, 16)
            with nc.allow_non_contiguous_dma(reason="a column of b_alpha for each head, once"):
                sp.dma_start(bias[:], K.b_alpha[0].rearrange("(h p) -> p h", p=P)).then_inc(loaded, 16)
            for h in range(HEADS):
                sp.wait_ge(biased, NC * (h + 1))
                sp.dma_start(K.z[G_GATE + h * P:G_GATE + (h + 1) * P, :], out[:, h, :]).then_inc(stored, 16)
            sp.wait_ge(stored, 16 * HEADS)

        @block.tensor
        def _(pe):
            pe.wait_ge(loaded, 48)
            for h in range(HEADS):
                for c, (t0, tn) in enumerate(CHUNKS):
                    if h >= 2:
                        pe.wait_ge(biased, NC * (h - 2) + c + 1)
                    pe.matmul(bank[h % 2][c][:, 0:tn], w2[:, h * P:(h + 1) * P], a1[:, t0:t0 + tn],
                              start=True, stop=True).then_inc(projected, 1)

        @block.scalar
        def _(act):
            act.wait_ge(loaded, 48)
            for h in range(HEADS):
                for c, (t0, tn) in enumerate(CHUNKS):
                    act.wait_ge(projected, NC * h + c + 1)
                    act.activation(out[:, h, t0:t0 + tn], bank[h % 2][c][:, 0:tn], ACT.Identity,
                                   bias=bias[:, h:h + 1]).then_inc(biased, 1)


def scan_stage(nc, K, name, hgrn, rows, norm_w, state_in, state_prompt, state_sample, mix):
    VC = 1 if hgrn else 2
    V = VC * P
    C = SEQ // P
    L = len(LEVELS) + 1
    LS = 4
    UC = 512 // V
    JS = NB * V // 512
    r_q, r_k, r_v, r_g, r_f = rows
    with Stage(nc, name) as s:
        f_raw = s.sb("f_raw", [P, T])
        q, k = s.sb("q", [P, 2, T]), s.sb("k", [P, 2, T])
        v, gate = s.sb("v", [P, VC, T]), s.sb("gate", [P, VC, T])
        soft, logf, b = s.sb("soft", [P, T]), s.sb("logf", [P, T]), s.sb("b", [P, T])
        expb = s.sb("expb", [P, T])
        q_dec = s.sb("q_dec", [P, 2, T])
        last_dec = s.sb("last_dec", [P, 2, C + NB])
        k_tok, v_tok = s.sb("k_tok", [P, 2, C + 1, P]), s.sb("v_tok", [P, 2, C + 1, V])
        dec, x = s.sb("dec", [P, 2, T]), s.sb("x", [P, 2, T])
        a = s.sb("a", [P, C + 1, P])
        state, s0 = s.sb("state", [P, C, V]), s.sb("s0", [P, NB, V])
        v_own = s.sb("v_own", [NS, NB, V])
        o, sq, rstd = s.sb("o", [P, VC, T]), s.sb("sq", [P, VC, T]), s.sb("rstd", [P, T])
        levels, starts, own = s.sb("levels", [P, L, P], I32), s.sb("starts", [P, T]), s.sb("own", [NS, NB])
        w_norm = s.sb("w_norm", [P, VC])
        lb = s.sb("lb", [P, 5, HEADS]) if hgrn else None
        lbh = s.sb("lbh", [P, 2, 2]) if hgrn else None
        S = [s.ps(f"S{i}", [P, 4, P]) for i in range(4)]
        TB = [s.ps(f"TB{i}", [P, 4, P]) for i in range(2)]
        SS, U = s.ps("SS", [P, 512]), s.ps("U", [P, 512])
        mean = [TB[0][:].rearrange("p c t -> p (c t)"), TB[1][:].rearrange("p c t -> p (c t)"), SS]
        const_in, norm_in, f_in, v_in, gate_in, s0_in = (s.sem(n) for n in (
            "const_in", "norm_in", "f_in", "v_in", "gate_in", "s0_in"))
        qk_in = [s.sem("qk_in0"), s.sem("qk_in1")]
        passed = s.sem("passed")
        stores_done = s.sem("stores_done")
        stored, lb_made, cleared = s.sem("stored"), s.sem("lb_made"), s.sem("cleared")
        QK = 16 if hgrn else 32
        GROUPS = 3
        TURNS = GROUPS * (1 + VC)
        TURN_K = 3
        per = dict(abs_out=1, sig_out=1, soft_out=1, log_sig=1, k_sig=1, f_mixed=1, f_clamped=1,
                   log_out=1, clamped=1, b_made=1, q_sig=1, q_silu=1, q_ready=1, k_ready=1, expb_out=1, q_dec_made=1,
                   k_diff=1, k_decay=1, k_dec_made=1, turned=TURNS, tok_out=TURNS,
                   diffed=7, decayed=7, x_made=7, scored=L, a_out=L,
                   u_made=C // UC, s_made=C, valued=3, o_out=3, own_made=1, us_made=JS, us_out=JS,
                   mean_in=NC, mean_out=NC, rstd_out=1, gate_silu=1, normed=VC, final=VC)
        sem = {n: s.sem(n) for n in per}
        block = s.block()

        def wait(eng, n, h, count):
            eng.wait_ge(sem[n], h[0] * (2 * per[n]) + (h[1] * per[n] + per[n] + count))

        def wait_before(eng, n, h, count=None):
            count = per[n] if count is None else count
            eng.wait_ge(sem[n], h[0] * (2 * per[n]) + (h[1] * per[n] + count))

        def credit(eng, names):
            for n in names.split():
                eng.sem_inc(sem[n], per[n])

        def loads(eng, sm, h, of_head):
            eng.wait_ge(sm, h[0] * (2 * of_head) + (h[1] + 1) * of_head)

        def qk_loaded(eng, h):
            eng.wait_ge(qk_in[h[1]], h[0] * QK + QK)

        def row(base, h, width=P):
            return bass.ds(h[0] * (2 * width) + (base + h[1] * width), width)

        def half(ap, m, second):
            n = ap.shape[-1]
            return ap.rearrange("p (n m) -> p n m", m=2 * m)[:, :, m:2 * m] if second else \
                ap.rearrange("p (n m) -> p n m", m=2 * m)[:, :, 0:m]

        def width(li):
            return T if li < LS else SEQ

        @block.sync
        def _(sp):
            sp.dma_start(levels[:], K.c_levels).then_inc(const_in, 16)
            sp.dma_start(starts[:], K.c_starts).then_inc(const_in, 16)
            sp.dma_start(own[:], K.c_own).then_inc(const_in, 16)
            sp.sem_inc(stores_done, 1)

            def load_head(h, first=False):
                if not first:
                    wait_before(sp, "k_sig" if hgrn else "log_sig", h)
                sp.dma_start(f_raw[:], K.z[row(r_f, h), :]).then_inc(f_in, 16)
                if not first:
                    wait_before(sp, "turned", h)
                    sp.wait_ge(sem["a_out"], h[0] * (2 * L) + h[1] * L)
                    sp.wait_ge(sem["k_dec_made"], h[0] * 2 + h[1])
                sp.dma_start(q[:, h[1], :], K.z[row(r_q, h), :]).then_inc(qk_in[h[1]], 16)
                if not hgrn:
                    sp.dma_start(k[:, h[1], :], K.z[row(r_k, h), :]).then_inc(qk_in[h[1]], 16)
                sp.dma_start(v[:], K.z[row(r_v, h, V), :].rearrange("(c p) t -> p c t", p=P)).then_inc(v_in, 16)

            def load_tail(h, first=False):
                if not first:
                    wait_before(sp, "final", h)
                    sp.wait_ge(stored, h[0] * 96 + h[1] * 48)
                    sp.sem_inc(stores_done, 1)
                sp.dma_start(gate[:], K.z[row(r_g, h, V), :].rearrange("(c p) t -> p c t", p=P)).then_inc(gate_in, 16)
                sp.dma_start(s0[:], state_in[:, row(0, h, 1), :, :].rearrange("b a k v -> k (b a) v")).then_inc(s0_in, 16)

            def store(h):
                wait(sp, "s_made", h, C)
                sp.dma_start(state_prompt[row(0, h, 1), :, :].rearrange("a k v -> (a k) v"),
                             state[:, C - 1, :]).then_inc(stored, 16)
                wait(sp, "us_out", h, JS)
                sp.dma_start(state_sample[:, row(0, h, 1), :, :].rearrange("b a k v -> k (b a) v"), s0[:]
                             ).then_inc(stored, 16)
                wait(sp, "final", h, VC)
                sp.dma_start(mix[row(0, h, V), :].rearrange("(c p) t -> p c t", p=P), o[:]).then_inc(stored, 16)

            load_head((0, 0), True)
            load_tail((0, 0), True)
            load_head((0, 1))
            store((0, 0))
            load_tail((0, 1))
            with sp.Fori(1, HEADS // 2) as i:
                load_head((i, 0))
                store((i - 1, 1))
                load_tail((i, 0))
                load_head((i, 1))
                store((i, 0))
                load_tail((i, 1))
            store((HEADS // 2 - 1, 1))
            sp.wait_ge(stored, 48 * HEADS)

        @block.gpsimd
        def _(pool):
            credit(pool, "q_silu q_ready diffed own_made")
            with nc.allow_non_contiguous_dma(reason="norm weights and lower bounds, once"):
                pool.dma_start(w_norm[:], norm_w.rearrange("(c p) -> p c", p=P)).then_inc(norm_in, 16)
                if hgrn:
                    pool.dma_start(lb[:, 0, :], K.lower_bounds[0].rearrange("(h p) -> p h", p=P)).then_inc(norm_in, 16)
            pool.memset(a[:], 0.0).then_inc(cleared, 1)
            pool.wait_ge(const_in, 48)

            def prepare(h):
                y = h[1]
                if hgrn:
                    wait(pool, "q_sig", h, 1)
                    pool.tensor_tensor(q[:, y, :], q[:, y, :], soft[:], ALU.mult).then_inc(sem["q_silu"], 1)
                    wait(pool, "q_silu", h, 1)
                else:
                    qk_loaded(pool, h)
                pool.sem_inc(passed, 1)
                pool.tensor_scalar(q[:, y, :], q[:, y, :], P ** -0.5, None, ALU.mult).then_inc(sem["q_ready"], 1)

            def differences(h):
                wait(pool, "b_made", h, 1)
                for n, m in enumerate(LEVELS):
                    w = width(n + 1)
                    blocks = b[:, 0:w].rearrange("p (n m) -> p n m", m=2 * m)
                    wait(pool, "x_made", h, max(n - 1, 0))
                    pool.tensor_tensor(dec[:, n % 2, 0:w].rearrange("p (n m) -> p n m", m=2 * m), blocks,
                                       blocks[:, :, m - 1:m].broadcast_to([P, w // (2 * m), 2 * m]),
                                       ALU.subtract).then_inc(sem["diffed"], 1)

            def tail(h):
                wait(pool, "tok_out", h, TURNS)
                wait_before(pool, "us_made", h)
                pool.tensor_tensor(v_own[:], v_tok[0:NS, h[1], C:C + 1, :].broadcast_to([NS, NB, V]),
                                   own[:].unsqueeze(2).broadcast_to([NS, NB, V]), ALU.mult).then_inc(sem["own_made"], 1)

            with pool.Fori(0, HEADS // 2) as i:
                prepare((i, 0))
                differences((i, 0))
                prepare((i, 1))
                tail((i, 0))
                differences((i, 1))
                tail((i, 1))

        @block.scalar
        def _(act):
            credit(act, "abs_out sig_out soft_out k_sig log_out q_sig expb_out k_decay tok_out decayed o_out "
                        "mean_out rstd_out gate_silu")

            if hgrn:
                act.wait_ge(lb_made, 1)
                act.activation(lb[:, 2, :], lb[:, 1, :], ACT.Exp).then_inc(lb_made, 1)

            def gates(h):
                y = h[1]
                loads(act, f_in, h, 16)
                if hgrn:
                    wait_before(act, "b_made", h)
                    act.activation(logf[:], f_raw[:], ACT.Sigmoid).then_inc(sem["sig_out"], 1)
                    act.activation(k[:, y, :], f_raw[:], ACT.Sigmoid, scale=-1.0).then_inc(sem["k_sig"], 1)
                    qk_loaded(act, h)
                    wait_before(act, "turned", h)
                    act.activation(soft[:], q[:, y, :], ACT.Sigmoid).then_inc(sem["q_sig"], 1)
                    wait(act, "f_clamped", h, 1)
                    act.activation(logf[:], logf[:], ACT.Ln).then_inc(sem["log_out"], 1)
                else:
                    wait_before(act, "turned", h)
                    act.activation(soft[:], f_raw[:], ACT.Abs).then_inc(sem["abs_out"], 1)
                    wait(act, "abs_out", h, 1)
                    act.activation(soft[:], soft[:], ACT.Sigmoid).then_inc(sem["sig_out"], 1)
                    wait(act, "sig_out", h, 1)
                    act.activation(soft[:], soft[:], ACT.Ln).then_inc(sem["soft_out"], 1)

            def decayed_forms(h):
                wait(act, "b_made", h, 1)
                wait_before(act, "k_dec_made", h)
                act.activation(expb[:], b[:], ACT.Exp).then_inc(sem["expb_out"], 1)
                wait(act, "k_diff", h, 1)
                act.activation(soft[:], soft[:], ACT.Exp).then_inc(sem["k_decay"], 1)

            def copy_values(h):
                for c in range(VC):
                    copy_tokens(h, v_tok, c, c)

            def copy_tokens(h, tok, c, n):
                for g in range(GROUPS):
                    wait(act, "turned", h, GROUPS * n + g + 1)
                    src = TB[(GROUPS * n + g) % 2]
                    if g < GROUPS - 1:
                        act.activation(tok[:, h[1], 4 * g:4 * g + 4, c * P:(c + 1) * P], src[:], ACT.Copy
                                       ).then_inc(sem["tok_out"], 1)
                    else:
                        act.activation(tok[0:NS, h[1], C, c * P:(c + 1) * P], src[0:NS, 0, :], ACT.Copy
                                       ).then_inc(sem["tok_out"], 1)

            def decays(h):
                for n, m in enumerate(LEVELS):
                    d = dec[:, n % 2, 0:width(n + 1)]
                    wait(act, "diffed", h, n + 1)
                    act.activation(half(d, m, False), half(d, m, False), ACT.Exp, scale=-1.0)
                    act.activation(half(d, m, True), half(d, m, True), ACT.Exp).then_inc(sem["decayed"], 1)
                    if n == TURN_K + 1:
                        copy_tokens(h, k_tok, 0, VC)

            def gate_silu(h):
                loads(act, gate_in, h, 16)
                act.activation(gate[:], gate[:], ACT.Silu).then_inc(sem["gate_silu"], 1)

            def outputs(h):
                act.wait_ge(stores_done, h[0] * 2 + (h[1] + 1))
                for g in range(3):
                    wait(act, "valued", h, g + 1)
                    for c in range(VC):
                        src = S[2 * c + g][:].rearrange("p c t -> p (c t)") if g < 2 else SS[:, c * NS:(c + 1) * NS]
                        t0, tn = g * 512, (512 if g < 2 else NS)
                        act.activation(o[:, c, t0:t0 + tn], src, ACT.Copy)
                        last = act.activation(sq[:, c, t0:t0 + tn], src, ACT.Square)
                    last.then_inc(sem["o_out"], 1)
                wait_before(act, "normed", h)
                for c, (t0, tn) in enumerate(CHUNKS):
                    wait(act, "mean_in", h, c + 1)
                    act.activation(rstd[:, t0:t0 + tn], mean[c][:, 0:tn], ACT.Ln, scale=1.0 / V,
                                   bias=K.eps[:, 0:1]).then_inc(sem["mean_out"], 1)
                wait(act, "mean_out", h, NC)
                act.activation(rstd[:], rstd[:], ACT.Exp, scale=-0.5).then_inc(sem["rstd_out"], 1)

            with act.Fori(0, HEADS // 2) as i:
                gates((i, 0))
                decayed_forms((i, 0))
                copy_values((i, 0))
                decays((i, 0))
                gate_silu((i, 0))
                gates((i, 1))
                outputs((i, 0))
                decayed_forms((i, 1))
                copy_values((i, 1))
                decays((i, 1))
                gate_silu((i, 1))
                outputs((i, 1))

        @block.vector
        def _(dve):
            credit(dve, "log_sig f_mixed f_clamped clamped b_made k_ready q_dec_made k_diff k_dec_made "
                        "x_made a_out s_made us_out normed final")
            dve.wait_ge(const_in, 48)
            dve.wait_ge(norm_in, 32 if hgrn else 16)
            dve.wait_ge(cleared, 1)
            if hgrn:
                top, e = lb[:, 1, :], lb[:, 2, :]
                dve.tensor_tensor(top, lb[:, 0, :], lb[:, 0, :], ALU.subtract).then_inc(lb_made, 1)
                dve.wait_ge(lb_made, 2)
                dve.reciprocal(lb[:, 0, :], e).then_inc(lb_made, 1)
                dve.wait_ge(lb_made, 3)
                dve.tensor_tensor(lb[:, 1, :], e, lb[:, 0, :], ALU.mult).then_inc(lb_made, 1)
                dve.wait_ge(lb_made, 4)
                dve.tensor_tensor(lb[:, 3, :], lb[:, 1, :], lb[:, 1, :], ALU.subtract).then_inc(lb_made, 1)
                dve.wait_ge(lb_made, 5)
                dve.tensor_scalar(lb[:, 4, :], lb[:, 3, :], -1.0, 1.0, ALU.mult, ALU.add).then_inc(lb_made, 1)
                dve.wait_ge(lb_made, 6)

            def gates(h):
                y = h[1]
                if hgrn:
                    dve.tensor_copy(lbh[:, y, :], lb[:, 3:5, row(0, h, 1)].rearrange("p c a -> p (c a)")
                                    ).then_inc(lb_made, 1)
                    dve.wait_ge(lb_made, h[0] * 2 + (h[1] + 7))
                    wait(dve, "sig_out", h, 1)
                    dve.tensor_scalar(logf[:], logf[:], lbh[:, y, 1:2], lbh[:, y, 0:1], ALU.mult, ALU.add
                                      ).then_inc(sem["f_mixed"], 1)
                    wait(dve, "f_mixed", h, 1)
                    dve.tensor_scalar(logf[:], logf[:], TINY, None, ALU.max).then_inc(sem["f_clamped"], 1)
                    wait(dve, "k_sig", h, 1)
                    dve.tensor_scalar(k[:, y, :], k[:, y, :], lbh[:, y, 1:2], None, ALU.mult).then_inc(sem["k_ready"], 1)
                else:
                    wait(dve, "soft_out", h, 1)
                    dve.scalar_tensor_tensor(out=logf[:], in0=f_raw[:], scalar=0.0, in1=soft[:], op0=ALU.min,
                                             op1=ALU.add).then_inc(sem["log_sig"], 1)
                    wait(dve, "log_sig", h, 1)
                    dve.tensor_scalar(logf[:], logf[:], 1.0 / GATE_TAU, 0.0, ALU.mult, ALU.min
                                      ).then_inc(sem["clamped"], 1)

            def running_sum(h):
                if hgrn:
                    wait(dve, "log_out", h, 1)
                    dve.tensor_scalar(logf[:], logf[:], 0.0, None, ALU.min).then_inc(sem["clamped"], 1)
                wait(dve, "clamped", h, 1)
                dve.tensor_tensor_scan(b[:], starts[:], logf[:], 0.0, ALU.mult, ALU.add).then_inc(sem["b_made"], 1)
                wait(dve, "b_made", h, 1)
                wait_before(dve, "turned", h)
                if hgrn:
                    wait(dve, "q_silu", h, 1)
                for t0, t1, m in ((0, SEQ, P), (SEQ, T, TS)):
                    bl = b[:, t0:t1].rearrange("p (n m) -> p n m", m=m)
                    last = dve.tensor_tensor(soft[:, t0:t1].rearrange("p (n m) -> p n m", m=m),
                                             bl[:, :, m - 1:m].broadcast_to([P, (t1 - t0) // m, m]), bl, ALU.subtract)
                last.then_inc(sem["k_diff"], 1)

            def decayed_forms(h):
                y = h[1]
                wait(dve, "expb_out", h, 1)
                wait(dve, "q_ready", h, 1)
                dve.tensor_tensor(q_dec[:, y, :], q[:, y, :], expb[:], ALU.mult).then_inc(sem["q_dec_made"], 1)
                dve.tensor_copy(last_dec[:, y, 0:C], expb[:, P - 1:SEQ:P])
                dve.tensor_copy(last_dec[:, y, C:C + NB], expb[:, SEQ + TS - 1:T:TS])
                wait(dve, "k_decay", h, 1)
                if hgrn:
                    wait(dve, "k_ready", h, 1)
                else:
                    qk_loaded(dve, h)
                dve.tensor_tensor(soft[:], k[:, y, :], soft[:], ALU.mult).then_inc(sem["k_dec_made"], 1)

            def scores(h):
                y = h[1]

                def scale(n):
                    m, w, z = LEVELS[n], width(n + 1), n % 2
                    wait(dve, "decayed", h, n + 1)
                    if n >= 2:
                        wait(dve, "scored", h, n)
                    dve.tensor_tensor(half(x[:, z, 0:w], m, False), half(dec[:, z, 0:w], m, False),
                                      half(k[:, y, 0:w], m, False), ALU.mult)
                    dve.tensor_tensor(half(x[:, z, 0:w], m, True), half(dec[:, z, 0:w], m, True),
                                      half(q[:, y, 0:w], m, True), ALU.mult).then_inc(sem["x_made"], 1)

                def keep(li):
                    wait(dve, "scored", h, li + 1)
                    if li:
                        wait(dve, "a_out", h, li)
                    dve.sem_inc(passed, 1)
                    for g in range(2):
                        last = dve.copy_predicated(a[:, 4 * g:4 * g + 4, :],
                                                   levels[:, li:li + 1, :].broadcast_to([P, 4, P]), S[2 * (li % 2) + g][:])
                    if li < LS:
                        last = dve.copy_predicated(a[0:NS, C, 0:NS], levels[0:NS, li, 0:NS],
                                                   (SS, U)[li % 2][0:NS, 0:NS])
                    last.then_inc(sem["a_out"], 1)

                wait_before(dve, "valued", h)
                for n in range(7):
                    scale(n)
                    keep(n)
                keep(7)

            def states(h):
                y = h[1]
                for c in range(C):
                    if c % UC == 0:
                        wait(dve, "u_made", h, c // UC + 1)
                    u = U[:, (c % UC) * V:(c % UC + 1) * V]
                    if c == 0:
                        dve.wait_ge(stores_done, h[0] * 2 + (h[1] + 1))
                        dve.tensor_copy(state[:, 0, :], u).then_inc(sem["s_made"], 1)
                    else:
                        wait(dve, "s_made", h, c)
                        dve.scalar_tensor_tensor(out=state[:, c, :], in0=state[:, c - 1, :], scalar=last_dec[:, y, c:c + 1],
                                                 in1=u, op0=ALU.mult, op1=ALU.add).then_inc(sem["s_made"], 1)

            def sample_states(h):
                y = h[1]
                wait(dve, "valued", h, 3)
                for j in range(JS):
                    wait(dve, "us_made", h, j + 1)
                    for n in range(512 // V):
                        bi = j * (512 // V) + n
                        last = dve.scalar_tensor_tensor(out=s0[:, bi, :], in0=s0[:, bi, :],
                                                        scalar=last_dec[:, y, C + bi:C + bi + 1],
                                                        in1=U[:, n * V:(n + 1) * V], op0=ALU.mult, op1=ALU.add)
                    last.then_inc(sem["us_out"], 1)

            def outputs(h):
                wait(dve, "rstd_out", h, 1)
                wait(dve, "o_out", h, 3)
                for c in range(VC):
                    dve.scalar_tensor_tensor(out=o[:, c, :], in0=o[:, c, :], scalar=w_norm[:, c:c + 1], in1=rstd[:],
                                             op0=ALU.mult, op1=ALU.mult).then_inc(sem["normed"], 1)
                wait(dve, "gate_silu", h, 1)
                for c in range(VC):
                    wait(dve, "normed", h, c + 1)
                    dve.tensor_tensor(o[:, c, :], o[:, c, :], gate[:, c, :], ALU.mult).then_inc(sem["final"], 1)

            with dve.Fori(0, HEADS // 2) as i:
                gates((i, 0))
                running_sum((i, 0))
                decayed_forms((i, 0))
                scores((i, 0))
                gates((i, 1))
                states((i, 0))
                running_sum((i, 1))
                sample_states((i, 0))
                outputs((i, 0))
                decayed_forms((i, 1))
                scores((i, 1))
                states((i, 1))
                sample_states((i, 1))
                outputs((i, 1))

        @block.tensor
        def _(pe):
            credit(pe, "turned scored u_made valued us_made mean_in")

            def turn(h, src, n):
                for g in range(GROUPS):
                    x = GROUPS * n + g
                    if x < 2:
                        wait_before(pe, "tok_out", h)
                    else:
                        wait(pe, "tok_out", h, x - 1)
                    pe.sem_inc(passed, 1)
                    for i in range(4 if g < GROUPS - 1 else 1):
                        t0 = (4 * g + i) * P
                        tn = min(P, T - t0)
                        last = pe.transpose(TB[x % 2][0:tn, i, :], src[:, t0:t0 + tn], K.ident[:])
                    last.then_inc(sem["turned"], 1)

            def turn_values(h):
                wait_before(pe, "mean_out", h)
                loads(pe, v_in, h, 16)
                for c in range(VC):
                    turn(h, v[:, c, :], c)

            def scores(h):
                y = h[1]
                for li in range(L):
                    if li == 0:
                        if hgrn:
                            wait(pe, "k_ready", h, 1)
                        else:
                            qk_loaded(pe, h)
                        wait(pe, "q_ready", h, 1)
                        first, second = k[:, y, :], q[:, y, :]
                        wait_before(pe, "o_out", h)
                        wait_before(pe, "mean_out", h)
                    else:
                        wait(pe, "x_made", h, li)
                        first = second = x[:, (li - 1) % 2, :]
                        if li >= 2:
                            wait(pe, "a_out", h, li - 1)
                    for c in range(C):
                        t = slice(c * P, (c + 1) * P)
                        last = pe.matmul(S[2 * (li % 2) + c // 4][:, c % 4, :], first[:, t], second[:, t],
                                         start=True, stop=True)
                    if li < LS:
                        last = pe.matmul((SS, U)[li % 2][0:NS, 0:NS], first[:, SEQ:T], second[:, SEQ:T],
                                         start=True, stop=True)
                    last.then_inc(sem["scored"], 1)
                    if li == TURN_K:
                        wait(pe, "k_dec_made", h, 1)
                        turn(h, soft[:], VC)

            def tail(h):
                y = h[1]
                wait(pe, "tok_out", h, TURNS)
                wait(pe, "a_out", h, L)
                wait(pe, "q_dec_made", h, 1)
                wait_before(pe, "us_out", h)
                wait_before(pe, "mean_out", h)
                loads(pe, s0_in, h, 16)
                def output(c):
                    if c:
                        wait(pe, "s_made", h, c)
                    for vc in range(VC):
                        out = S[2 * vc + c // 4][:, c % 4, :]
                        last = pe.matmul(out, v_tok[:, y, c, vc * P:(vc + 1) * P], a[:, c, :], start=True, stop=(c == 0))
                        if c:
                            last = pe.matmul(out, state[:, c - 1, vc * P:(vc + 1) * P], q_dec[:, y, c * P:(c + 1) * P],
                                             start=False, stop=True)
                    if c % 4 == 3:
                        last.then_inc(sem["valued"], 1)

                for n in range(C // UC + 1):
                    if n < C // UC:
                        if n:
                            wait(pe, "s_made", h, n * UC)
                        for c in range(n * UC, (n + 1) * UC):
                            last = pe.matmul(U[:, (c % UC) * V:(c % UC + 1) * V], k_tok[:, y, c, :], v_tok[:, y, c, :],
                                             start=True, stop=True)
                        last.then_inc(sem["u_made"], 1)
                    if n:
                        for c in range(max((n - 1) * UC, 1), n * UC):
                            output(c)
                    else:
                        output(0)
                for vc in range(VC):
                    out = SS[:, vc * NS:(vc + 1) * NS]
                    pe.matmul(out, v_tok[0:NS, y, C, vc * P:(vc + 1) * P], a[0:NS, C, 0:NS], start=True, stop=False)
                    for bi in range(NB):
                        t = slice(bi * TS, (bi + 1) * TS)
                        last = pe.matmul(out[:, t], s0[:, bi, vc * P:(vc + 1) * P],
                                         q_dec[:, y, SEQ + bi * TS:SEQ + (bi + 1) * TS], start=False,
                                         stop=(bi == NB - 1))
                last.then_inc(sem["valued"], 1)
                def mean_of(c):
                    t0, tn = CHUNKS[c]
                    for vc in range(VC):
                        last = pe.matmul(mean[c][:, 0:tn], K.ones[:], sq[:, vc, t0:t0 + tn], start=(vc == 0),
                                         stop=(vc == VC - 1))
                    last.then_inc(sem["mean_in"], 1)

                wait(pe, "own_made", h, 1)
                for j in range(JS):
                    if j == 0:
                        wait(pe, "s_made", h, C)
                    else:
                        wait(pe, "us_out", h, j)
                    n = 512 // V
                    pe.matmul(U[:], k_tok[0:NS, y, C, :], v_own[:, j * n:(j + 1) * n, :].rearrange("p b v -> p (b v)"),
                              start=True, stop=True).then_inc(sem["us_made"], 1)
                    if j == 0:
                        wait(pe, "o_out", h, 3)
                    if j < NC:
                        mean_of(j)
                for c in range(JS, NC):
                    mean_of(c)

            with pe.Fori(0, HEADS // 2) as i:
                turn_values((i, 0))
                scores((i, 0))
                tail((i, 0))
                turn_values((i, 1))
                scores((i, 1))
                tail((i, 1))


def latent_attention(nc, K):
    with ExitStack() as stack:
        M = Kit()

        def keep(name, shape, dt=F32):
            return stack.enter_context(nc.sbuf_tensor(name, shape, dt))

        M.ckv, M.kpe = keep("mla_ckv", [P, 2, T]), keep("mla_kpe", [P, T])
        M.wuv, M.rows = keep("mla_wuv", [P, 2, HEADS, P]), keep("mla_rows", [P, 9, LAT])
        M.qs = keep("mla_qs", [P, 3, NB, HEADS, TS])
        with ExitStack() as prompt:
            M.qn = prompt.enter_context(nc.sbuf_tensor("mla_qn", [P, HEADS, T], F32))
            M.qpe = prompt.enter_context(nc.sbuf_tensor("mla_qpe", [P, 2, T], F32))
            latent_stage(nc, K, M)
            M.kn = prompt.enter_context(nc.sbuf_tensor("mla_kn", [P, HEADS, SEQ], F32))
            M.v = prompt.enter_context(nc.sbuf_tensor("mla_v", [P, 8, HEADS * P], F32))
            keys_stage(nc, K, M)
            prompt_attention_stage(nc, K, M)
        sample_attention_stage(nc, K, M)



def program(nc, K):
    with ExitStack() as stack:
        def keep(name, shape, dt=F32):
            return stack.enter_context(nc.sbuf_tensor(name, shape, dt))

        K.xT = keep("xT", [P, KD, T])
        K.ident, K.ones = keep("ident", [P, P]), keep("ones", [P, P])
        K.norms, K.eps = keep("norms", [P, 4, KD]), keep("eps", [P, 1])
        load_stage(nc, K)
        project_stage(nc, K, "even", K.w_in_even[0], EVEN_COLS, norm=0, z=K.z)
        latent_attention(nc, K)
        scan_stage(nc, K, "hgrn", True, (Z_Q, None, Z_I, Z_G, Z_F), K.hgrn_norm[0], K.state_hgrn[0],
                   K.hgrn_prompt, K.hgrn_sample, K.mix)
        project_stage(nc, K, "evenout", K.w_out_even[0], D, mix=K.mix)
        mlp_stage(nc, K, "mlp0", 1, K.w_up[0], K.w_down[0])
        project_stage(nc, K, "odd", K.w_in_odd[0], ODD_COLS, norm=2, z=K.z)
        alpha_stage(nc, K)
        scan_stage(nc, K, "gla", False, (G_Q, G_K, G_V, G_R, G_GATE), K.gla_norm[0], K.state_gla[0],
                   K.gla_prompt, K.gla_sample, K.mix)
        project_stage(nc, K, "oddout", K.w_out_odd[0], D, mix=K.mix)
        mlp_stage(nc, K, "mlp1", 3, K.w_up[1], K.w_down[1])
        store_stage(nc, K)



def constants():
    f = np.float32
    pos = np.concatenate([np.arange(SEQ)] + [PAGES * P + np.arange(TS)] * NB)
    inv = (ROPE_THETA ** (-np.arange(ROPE // 2) / (ROPE // 2))).astype(f)
    ang = (pos.astype(f)[None, :] * inv[:, None]).astype(np.float64)
    cos = np.tile(np.cos(ang), (4, 1)).astype(f)
    sin = np.tile(np.concatenate([-np.sin(ang), np.sin(ang)]), (2, 1)).astype(f)
    rot = np.zeros((P, P), f)
    rot[np.arange(P) ^ (ROPE // 2), np.arange(P)] = 1
    i = np.arange(P)
    s, t = i[:, None], i[None, :]
    causal = np.where(t <= s, 0, NEG).astype(f)
    tok, row = np.arange(NS), np.arange(HEADS * TS)
    seen = ((tok[None, None, :] // TS == np.arange(NB)[None, :, None])
            & (tok[None, None, :] % TS <= (row % TS)[:, None, None]))
    pairs = [s == t] + [(s // (2 * m) == t // (2 * m)) & (s % (2 * m) < m) & (t % (2 * m) >= m) for m in LEVELS]
    starts = np.ones((P, T), f)
    starts[:, 0:SEQ:P] = 0
    starts[:, SEQ::TS] = 0
    return dict(c_ident=np.eye(P, dtype=f), c_cos=cos, c_sin=sin, c_rot=rot, c_causal=causal,
                c_newmask=np.where(seen, 0, NEG).astype(f), c_levels=np.stack(pairs, 1).astype(np.int32),
                c_starts=starts, c_own=(tok[:, None] // TS == np.arange(NB)[None, :]).astype(f))


OUTPUTS = dict(y_prompt=(1, SEQ, D), y_sample=(NB, TS, D), mla_rows_prompt=(1, 1, SEQ, LAT),
               mla_rows_sample=(1, NB, TS, LAT), hgrn_state_prompt=(1, 1, HEADS, P, P),
               hgrn_state_sample=(1, NB, HEADS, P, P), gla_state_prompt=(1, 1, HEADS, P, 2 * P),
               gla_state_sample=(1, NB, HEADS, P, 2 * P))


def bind(nc, a, o):
    K = Kit()
    K.x_prompt, K.x_sample = a["x_prompt"][0], a["x_sample"].rearrange("b t d -> (b t) d")
    K.cache, K.page_table = a["cache_mla"][0], a["page_table"].rearrange("(a b) p -> a (b p)", a=1)
    K.state_hgrn, K.state_gla = a["state_hgrn"], a["state_gla"]
    K.norm_mix, K.norm_mlp, K.norm_final = a["norm_mix"], a["norm_mlp"], a["norm_final"]
    K.w_in_even, K.w_out_even, K.w_in_odd, K.w_out_odd = a["w_in_even"], a["w_out_even"], a["w_in_odd"], a["w_out_odd"]
    K.w_up, K.w_down, K.w_uq, K.w_uk, K.w_uv = a["w_up"], a["w_down"], a["w_uq"], a["w_uk"], a["w_uv"]
    K.q_norm, K.kv_norm, K.hgrn_norm, K.gla_norm = a["q_norm"], a["kv_norm"], a["hgrn_norm"], a["gla_norm"]
    K.lower_bounds, K.w_alpha2, K.b_alpha = a["lower_bounds"], a["w_alpha2"], a["b_alpha"]
    K.c_ident, K.c_cos, K.c_sin, K.c_rot, K.c_causal = a["c_ident"], a["c_cos"], a["c_sin"], a["c_rot"], a["c_causal"]
    K.c_newmask, K.c_levels, K.c_starts, K.c_own = a["c_newmask"], a["c_levels"], a["c_starts"], a["c_own"]
    K.z = nc.dram_tensor("projections", [Z_ROWS, T], F32, kind="Internal").ap()
    K.mix = nc.dram_tensor("mixed", [D, T], F32, kind="Internal").ap()
    K.y_prompt, K.y_sample = o["y_prompt"][0], o["y_sample"].rearrange("b t d -> (b t) d")
    K.rows_prompt = o["mla_rows_prompt"][0, 0]
    K.rows_sample = o["mla_rows_sample"][0].rearrange("b t c -> (b t) c")
    K.hgrn_prompt, K.hgrn_sample = o["hgrn_state_prompt"][0, 0], o["hgrn_state_sample"][0]
    K.gla_prompt, K.gla_sample = o["gla_state_prompt"][0, 0], o["gla_state_sample"][0]
    return K


def kernel(**inputs):
    import concourse.bacc as bacc
    from concourse.bass_utils import run_bass_kernel_spmd

    nc = bacc.Bacc("TRN2", target_bir_lowering=False, num_devices=1)
    arrays = {f"in_{n}": np.ascontiguousarray(x) for n, x in {**inputs, **constants()}.items()}
    a = {n[3:]: nc.dram_tensor(n, x.shape, mybir.dt.from_np(x.dtype), kind="ExternalInput").ap()
         for n, x in arrays.items()}
    o = {n: nc.dram_tensor(f"out_{n}", shape, F32, kind="ExternalOutput").ap() for n, shape in OUTPUTS.items()}
    program(nc, bind(nc, a, o))
    result = run_bass_kernel_spmd(nc, [arrays], core_ids=[0]).results[0]
    return tuple(result[f"out_{n}"] for n in OUTPUTS)
```
